# Optimizing a Trainium2 kernel written in Bass

```python
import jax, jax.numpy as jnp
from jax import lax
import numpy as np

D_MODEL = 1024
BATCH = 1
SEQ = 256
DEPTH = 2

GLA_HEADS = 4
GLA_DK = 32
GLA_DV = 64
GLA_LOWRANK = 16
GLA_GATE_TAU = 16.0
MOBA_HEADS = 8
MOBA_HD = 64
MOBA_BLOCK = 256
MOBA_TOPK = 3
MOBA_QCHUNK = 128
ROT_DIM = MOBA_HD // 4
ROPE_THETA = 500000.0
HGRN_HEADS = 4
HGRN_DK = 64
HGRN_DV = 64
LIN_CHUNK = 16
GLA_KW = GLA_HEADS * GLA_DK
GLA_VW = GLA_HEADS * GLA_DV
MOBA_W = MOBA_HEADS * MOBA_HD
HGRN_KW = HGRN_HEADS * HGRN_DK
HGRN_VW = HGRN_HEADS * HGRN_DV
MIX_WIDTH = GLA_VW + MOBA_W + HGRN_VW
IN_SPLITS = (GLA_KW, GLA_KW, GLA_VW, GLA_VW, GLA_LOWRANK,
             MOBA_W, MOBA_W, MOBA_W,
             HGRN_KW, HGRN_KW, HGRN_VW, HGRN_VW)
IN_COLS = sum(IN_SPLITS)
MOE_GROUPS = 4
MOE_EXPERTS_PER_GROUP = 4
MOE_N_EXPERTS = MOE_GROUPS * MOE_EXPERTS_PER_GROUP
MOE_TOPK = 2
MOE_FF = 512
NORM_EPS = 1e-6

kernel_name = 'hymba_style_gla_moba_hgrn2_hmoe'

def rms_norm(x, g):
    xf = x.astype(jnp.float32)
    y = xf * lax.rsqrt(jnp.mean(xf * xf, axis=-1, keepdims=True) + NORM_EPS)
    return (y * g.astype(jnp.float32)).astype(x.dtype)

def partial_rotary(x, pos):
    half = ROT_DIM // 2
    inv_freq = ROPE_THETA ** (-(jnp.arange(0, ROT_DIM, 2, dtype=jnp.float32) / ROT_DIM))
    ang = pos.astype(jnp.float32)[:, None] * inv_freq[None, :]
    cos = jnp.cos(ang)[None, :, None, :]
    sin = jnp.sin(ang)[None, :, None, :]
    x1 = x[..., :half].astype(jnp.float32)
    x2 = x[..., half:ROT_DIM].astype(jnp.float32)
    rot = jnp.concatenate([x1 * cos - x2 * sin, x2 * cos + x1 * sin], axis=-1)
    return jnp.concatenate([rot.astype(x.dtype), x[..., ROT_DIM:]], axis=-1)

def gated_linear_chunked(q, k, v, log_a):
    B, S, H, dk = q.shape
    dv = v.shape[-1]
    C = LIN_CHUNK
    N = S // C
    f32 = jnp.float32

    def chunk(t):
        return t.astype(f32).reshape(B, N, C, H, t.shape[-1]).transpose(0, 3, 1, 2, 4)

    q, k, v, log_a = chunk(q), chunk(k), chunk(v), chunk(log_a)
    b = jnp.cumsum(log_a, axis=3)
    b_last = b[:, :, :, -1:, :]
    causal = jnp.tril(jnp.ones((C, C), dtype=bool))[:, :, None]
    diff = b[:, :, :, :, None, :] - b[:, :, :, None, :, :]
    decay = jnp.exp(jnp.where(causal, diff, -jnp.inf))
    scores = jnp.einsum('bhnik,bhnjk,bhnijk->bhnij', q, k, decay)
    o = jnp.einsum('bhnij,bhnjv->bhniv', scores, v)
    chunk_kv = jnp.einsum('bhnck,bhncv->bhnkv', k * jnp.exp(b_last - b), v)
    chunk_decay = jnp.exp(b_last[:, :, :, 0, :])

    def step(state, inp):
        a, kv = inp
        return a[..., None] * state + kv, state

    _, states = lax.scan(step, jnp.zeros((B, H, dk, dv), f32),
                         (jnp.moveaxis(chunk_decay, 2, 0), jnp.moveaxis(chunk_kv, 2, 0)))
    states = jnp.moveaxis(states, 0, 2)
    o = o + jnp.einsum('bhnck,bhnkv->bhncv', q * jnp.exp(b), states)
    return o.transpose(0, 2, 3, 1, 4).reshape(B, S, H, dv)

def moba_attention(q, k, v):
    B, S, H, D = q.shape
    BLK, Q = MOBA_BLOCK, MOBA_QCHUNK
    f32 = jnp.float32
    nb = -(-S // BLK)
    pad = nb * BLK - S
    q = q.transpose(0, 2, 1, 3)
    k = jnp.pad(k.transpose(0, 2, 1, 3), ((0, 0), (0, 0), (0, pad), (0, 0)))
    v = jnp.pad(v.transpose(0, 2, 1, 3), ((0, 0), (0, 0), (0, pad), (0, 0)))
    k_blocks = k.reshape(B, H, nb, BLK, D)
    v_blocks = v.reshape(B, H, nb, BLK, D)
    k_mean = jnp.mean(k_blocks.astype(f32), axis=3)
    pos = jnp.arange(S)
    q_blk = pos // BLK
    gate = jnp.einsum('bhsd,bhnd->bhsn', q.astype(f32), k_mean)
    fully_past = jnp.arange(nb)[None, :] < q_blk[:, None]
    gate = jnp.where(fully_past, gate, -jnp.inf)
    topk = min(MOBA_TOPK, nb)
    top_val, top_idx = lax.top_k(gate, topk)
    sel_ok = top_val > -jnp.inf
    nqc = S // Q

    def to_chunks(t):
        rest = t.shape[3:]
        t = t.reshape((B, H, nqc, Q) + rest).swapaxes(1, 2)
        return t.reshape((B * nqc, H, Q) + rest)

    b_ids = jnp.repeat(jnp.arange(B, dtype=jnp.int32), nqc)
    c_ids = jnp.tile(jnp.arange(nqc, dtype=jnp.int32), B)
    scale = D ** -0.5
    h_ar = jnp.arange(H)[:, None, None]

    def one_chunk(args):
        qc, idx, ok, bi, ci = args
        kb = k_blocks[bi]
        vb = v_blocks[bi]
        ks = kb[h_ar, idx]
        vs = vb[h_ar, idx]
        s_sel = jnp.einsum('hqd,hqjkd->hqjk', qc, ks).astype(f32) * scale
        s_sel = jnp.where(ok[..., None], s_sel, -jnp.inf).reshape(H, Q, topk * BLK)
        n_own = (ci * Q) // BLK
        k_own = lax.dynamic_index_in_dim(kb, n_own, axis=1, keepdims=False)
        v_own = lax.dynamic_index_in_dim(vb, n_own, axis=1, keepdims=False)
        s_own = jnp.einsum('hqd,hkd->hqk', qc, k_own).astype(f32) * scale
        qpos = ci * Q + jnp.arange(Q)
        kpos = n_own * BLK + jnp.arange(BLK)
        s_own = jnp.where((kpos[None, :] <= qpos[:, None])[None], s_own, -jnp.inf)
        p = jax.nn.softmax(jnp.concatenate([s_sel, s_own], axis=-1), axis=-1)
        p_sel = p[..., :topk * BLK].reshape(H, Q, topk, BLK).astype(vs.dtype)
        p_own = p[..., topk * BLK:].astype(v_own.dtype)
        return (jnp.einsum('hqjk,hqjkd->hqd', p_sel, vs)
                + jnp.einsum('hqk,hkd->hqd', p_own, v_own))

    out = lax.map(one_chunk, (to_chunks(q), to_chunks(top_idx), to_chunks(sel_ok), b_ids, c_ids))
    out = out.reshape(B, nqc, H, Q, D).transpose(0, 1, 3, 2, 4)
    return out.reshape(B, S, H * D)

def hierarchical_moe(h, w_rg, w_re, w_g, w_u, w_d):
    B, S, D = h.shape
    t = h.reshape(-1, D)
    f32 = jnp.float32
    lg = (t @ w_rg).astype(f32)
    p_group = jax.nn.softmax(lg, axis=-1)
    g_sel = jnp.argmax(lg, axis=-1)
    gate_group = jnp.take_along_axis(p_group, g_sel[:, None], axis=1)[:, 0]
    le = (t @ w_re).astype(f32).reshape(-1, MOE_GROUPS, MOE_EXPERTS_PER_GROUP)
    le = jnp.take_along_axis(le, g_sel[:, None, None], axis=1)[:, 0]
    top_v, top_i = lax.top_k(le, MOE_TOPK)
    w_sel = jax.nn.softmax(top_v, axis=-1) * gate_group[:, None]
    e_ids = g_sel[:, None] * MOE_EXPERTS_PER_GROUP + top_i
    comb = jnp.sum(jax.nn.one_hot(e_ids, MOE_N_EXPERTS, dtype=f32) * w_sel[..., None], axis=1)
    comb = comb.astype(t.dtype)
    y = jnp.zeros_like(t)
    for e in range(MOE_N_EXPERTS):
        he = jax.nn.silu(t @ w_g[e]) * (t @ w_u[e])
        y = y + comb[:, e:e + 1] * (he @ w_d[e])
    return y.reshape(B, S, D)

def setup_inputs(seed: int = 0) -> dict:
    key = jax.random.key(seed)
    ks = jax.random.split(key, 17)
    f32 = jnp.float32
    nrm = lambda k, shape, s: jax.random.normal(k, shape, f32) * s
    gain = lambda k, shape: 1.0 + 0.02 * jax.random.normal(k, shape, f32)
    return {
        'x': nrm(ks[0], (BATCH, SEQ, D_MODEL), 1.0),
        'attn_norm_g': gain(ks[1], (DEPTH, D_MODEL)),
        'w_in': nrm(ks[2], (DEPTH, D_MODEL, IN_COLS), D_MODEL ** -0.5),
        'gla_gk_w2': nrm(ks[3], (DEPTH, GLA_LOWRANK, GLA_KW), GLA_LOWRANK ** -0.5),
        'gla_gk_b': nrm(ks[4], (DEPTH, GLA_KW), 0.1),
        'gla_norm_g': gain(ks[5], (DEPTH, GLA_DV)),
        'moba_qnorm_g': gain(ks[6], (DEPTH, MOBA_HD)),
        'moba_knorm_g': gain(ks[7], (DEPTH, MOBA_HD)),
        'hgrn_lb_param': nrm(ks[8], (DEPTH, HGRN_KW), 1.0),
        'hgrn_norm_g': gain(ks[9], (DEPTH, HGRN_DV)),
        'w_out': nrm(ks[10], (DEPTH, MIX_WIDTH, D_MODEL), MIX_WIDTH ** -0.5),
        'ffn_norm_g': gain(ks[11], (DEPTH, D_MODEL)),
        'w_router_group': nrm(ks[12], (DEPTH, D_MODEL, MOE_GROUPS), D_MODEL ** -0.5),
        'w_router_expert': nrm(ks[13], (DEPTH, D_MODEL, MOE_N_EXPERTS), D_MODEL ** -0.5),
        'w_exp_gate': nrm(ks[14], (DEPTH, MOE_N_EXPERTS, D_MODEL, MOE_FF), D_MODEL ** -0.5),
        'w_exp_up': nrm(ks[15], (DEPTH, MOE_N_EXPERTS, D_MODEL, MOE_FF), D_MODEL ** -0.5),
        'w_exp_down': nrm(ks[16], (DEPTH, MOE_N_EXPERTS, MOE_FF, D_MODEL), MOE_FF ** -0.5),
    }

def reference(x, attn_norm_g, w_in, gla_gk_w2, gla_gk_b, gla_norm_g, moba_qnorm_g,
              moba_knorm_g, hgrn_lb_param, hgrn_norm_g, w_out, ffn_norm_g,
              w_router_group, w_router_expert, w_exp_gate, w_exp_up, w_exp_down):
    B, S, _ = x.shape
    f32 = jnp.float32
    pos = jnp.arange(S)
    offs = np.cumsum(IN_SPLITS)[:-1].tolist()
    lb_p = jax.nn.softmax(hgrn_lb_param.astype(f32), axis=0)
    lower_bounds = jnp.cumsum(lb_p, axis=0) - lb_p[0]

    def heads(t, n):
        return t.reshape(B, S, n, -1)

    for l in range(DEPTH):
        h = rms_norm(x, attn_norm_g[l])
        proj = h @ w_in[l]
        (a_q, a_k, a_v, a_g, a_lr, b_q, b_k, b_v,
         c_q, c_f, c_i, c_g) = jnp.split(proj, offs, axis=-1)

        log_alpha = jax.nn.log_sigmoid((a_lr @ gla_gk_w2[l] + gla_gk_b[l]).astype(f32)) / GLA_GATE_TAU
        o_a = gated_linear_chunked(heads(a_q, GLA_HEADS) * (GLA_DK ** -0.5), heads(a_k, GLA_HEADS),
                                   heads(a_v, GLA_HEADS), heads(log_alpha, GLA_HEADS))
        o_a = rms_norm(o_a.astype(x.dtype), gla_norm_g[l]) * jax.nn.silu(heads(a_g, GLA_HEADS))

        mq = partial_rotary(rms_norm(heads(b_q, MOBA_HEADS), moba_qnorm_g[l]), pos)
        mk = partial_rotary(rms_norm(heads(b_k, MOBA_HEADS), moba_knorm_g[l]), pos)
        o_b = moba_attention(mq, mk, heads(b_v, MOBA_HEADS))

        lb = lower_bounds[l].reshape(HGRN_HEADS, HGRN_DK)
        f_raw = heads(c_f, HGRN_HEADS).astype(f32)
        log_f = jnp.log(lb + (1.0 - lb) * jax.nn.sigmoid(f_raw))
        k_c = (1.0 - lb) * jax.nn.sigmoid(-f_raw)
        o_c = gated_linear_chunked(jax.nn.silu(heads(c_q, HGRN_HEADS)), k_c,
                                   heads(c_i, HGRN_HEADS), log_f)
        o_c = rms_norm(o_c.astype(x.dtype), hgrn_norm_g[l]) * jax.nn.silu(heads(c_g, HGRN_HEADS))

        mix = jnp.concatenate([o_a.reshape(B, S, GLA_VW), o_b, o_c.reshape(B, S, HGRN_VW)], axis=-1)
        x = x + mix @ w_out[l]

        h2 = rms_norm(x, ffn_norm_g[l])
        x = x + hierarchical_moe(h2, w_router_group[l], w_router_expert[l],
                                 w_exp_gate[l], w_exp_up[l], w_exp_down[l])
    return x


_drawn_inputs = setup_inputs


def setup_inputs(seed=0):
    import zlib

    import numpy as np

    out = dict(_drawn_inputs(seed))
    spreads = {}
    factors = {'moba_qnorm_g': 4.238, 'moba_knorm_g': 6.873}
    for name, (base, spread) in spreads.items():
        noise = np.random.default_rng([zlib.crc32(name.encode()), seed]).standard_normal(out[name].shape)
        drawn = base * np.exp(spread * noise) if base else spread * noise
        out[name] = __import__('jax').numpy.asarray(drawn.astype(out[name].dtype))
    for name, factor in factors.items():
        out[name] = (out[name] * factor).astype(out[name].dtype)
    return out
```

```python
from contextlib import ExitStack

import numpy as np

import concourse.bass as bass
from concourse import mybir

F32 = mybir.dt.float32
U32 = mybir.dt.uint32
I32 = mybir.dt.int32
ALU = mybir.AluOpType
ACT = mybir.ActivationFunctionType
AX = mybir.AxisListType

P = 128
D_MODEL = 1024
SEQ = 256
DEPTH = 2
NT = SEQ // P
KC = D_MODEL // P
LIN_HEADS = 8
GLA_HEADS = 4
GLA_DK = 32
LOWRANK = 16
HEAD = 64
LIN_CHUNK = 16
MOBA_HEADS = 8
EXPERTS = 16
GROUPS = 4
FF = 512
FC = FF // P
EPS = 1e-6
GLA_TAU = 16.0
SLOTS = 64
ROUNDS = SEQ // SLOTS
PAIRS = EXPERTS // 2
LEVELS = 8
NEG = -1.0e30
F_MIN = 2.0 ** -60
LN_F_MIN = float(np.log(F_MIN))

A_Q, A_K, A_V, A_G, A_LR, B_Q, B_K, B_V, C_Q, C_F, C_I, C_G = (
    0, 128, 256, 512, 768, 784, 1296, 1808, 2320, 2576, 2832, 3088)
IN_CHUNKS = [(C_Q, 512), (A_G, 272), (A_Q, 512), (C_I, 256), (C_G, 256), (B_Q, 512), (B_K, 512), (B_V, 512)]
LAST_UNIT = [1, 3, 5, 7, 8, 10, 12, 14]
OUT_COLS = 256
OUT_CHUNKS = D_MODEL // OUT_COLS
RING = 6
RING_ELEMS = 4096
ATT_CHUNKS = len(IN_CHUNKS) + OUT_CHUNKS
assert ATT_CHUNKS % RING == 0

PG_ATT, PG_FFN, P_GLA, P_QN, P_KN, P_HGRN, P_LB, P_GKB, P_W2, P_WR = 0, 8, 16, 17, 18, 19, 20, 22, 23, 151
NPAR = P_WR + KC * (GROUPS + EXPERTS)
NR = GROUPS + EXPERTS
R_EXP = 400

CONSTS = {}


def host_constants():
    i = np.arange(P)
    cols = []

    def add(name, a):
        a = np.asarray(a, np.float32).reshape(P, -1)
        CONSTS[name] = (sum(c.shape[1] for c in cols), a.shape[1])
        cols.append(a)

    add("ident", np.eye(P))
    add("head_ones", (i[:, None] // HEAD) == (i[None, :] // HEAD))
    add("all_ones", np.ones((P, P)))
    add("before", i[:, None] < i[None, :])
    d = i % HEAD
    swap = np.zeros((P, P))
    for m in range(P):
        if d[m] < 8:
            swap[m + 8, m] = -1.0
        elif d[m] < 16:
            swap[m - 8, m] = 1.0
    add("swap", swap)
    inv = np.float32(500000.0) ** (-(np.arange(0, 16, 2, dtype=np.float32) / np.float32(16)))
    ang = np.arange(SEQ, dtype=np.float32)[:, None] * inv[None, :].astype(np.float32)
    cos, sin = np.ones((P, SEQ)), np.zeros((P, SEQ))
    for m in range(P):
        if d[m] < 16:
            cos[m] = np.cos(ang[:, d[m] % 8])
            sin[m] = np.sin(ang[:, d[m] % 8])
    add("cos", cos)
    add("sin", sin)
    add("causal", np.where(i[None, :] <= i[:, None], 0.0, NEG))
    masks = np.zeros((P, LEVELS, P))
    masks[i, 0, i] = 1.0
    for n in range(1, LEVELS):
        s = 1 << (n - 1)
        same = (i[:, None] // (2 * s)) == (i[None, :] // (2 * s))
        masks[:, n] = same & ((i[:, None] // s) % 2 == 0) & ((i[None, :] // s) % 2 == 1)
    add("masks", masks)
    add("chunk_keep", np.tile((np.arange(SEQ) % LIN_CHUNK != 0)[None, :], (P, 1)))
    add("ones_row", np.ones((P, SEQ)))
    add("edges", np.tile(np.arange(1, ROUNDS) * SLOTS, (P, 1)))
    add("slot", np.tile(np.arange(SLOTS), (P, 1)))
    add("rank", np.tile(EXPERTS - np.arange(EXPERTS), (P, 1)))
    add("eps", np.full((P, 1), EPS))
    add("one", np.ones((P, 1)))
    return np.concatenate(cols, axis=1)


class Signal:

    def __init__(self, sem, per, ahead=0):
        self.sem, self.per, self.ahead = sem, per, ahead

    def by(self, ins, k=1):
        ins.then_inc(self.sem, k)
        return ins

    def at(self, base, n):
        return base * self.per + (n + self.ahead)


def build(nc, a, out):
    with ExitStack() as ctx:
        def sb(name, cols, dt=F32):
            return ctx.enter_context(nc.sbuf_tensor(name, [P, cols], dt))

        def view(t, off, *dims):
            n = int(np.prod(dims))
            v = t[:, off:off + n]
            if len(dims) == 2:
                v = v.rearrange("p (a b) -> p a b", a=dims[0])
            elif len(dims) == 3:
                v = v.rearrange("p (a b c) -> p a b c", a=dims[0], b=dims[1])
            return v

        ncst = sum(n for _, n in CONSTS.values())
        cst = sb("cst", ncst)
        par_all = sb("par_all", DEPTH * NPAR)
        par = sb("par", NPAR)
        ring = sb("ring", RING * RING_ELEMS)
        x_buf = sb("x_buf", NT * D_MODEL)
        n_buf = sb("n_buf", NT * D_MODEL)
        t_buf = sb("t_buf", KC * SEQ)
        lin_buf = sb("lin_buf", 4 * 3 * SEQ)
        gate_buf = sb("gate_buf", 4 * SEQ)
        v_buf = sb("v_buf", NT * D_MODEL)
        mqk_buf = sb("mqk_buf", 2 * 4 * SEQ)
        work = sb("work", 8 * 3 * SEQ)
        st_buf = sb("st_buf", LIN_HEADS * 3 * P)
        small = sb("small", 640)
        npairs_i = sb("npairs_i", 2, I32)
        banks = ctx.enter_context(nc.psum_tensor("banks", [P, 8, 512], F32))

        def const(name, *dims):
            off, n = CONSTS[name]
            return view(cst, off, *(dims or (n,)))

        ident, head_ones, all_ones, before, swap = (const(n) for n in ("ident", "head_ones", "all_ones", "before", "swap"))
        cos, sin, causal = const("cos"), const("sin"), const("causal")
        masks = const("masks", LEVELS, P)
        eps, one = const("eps"), const("one")

        x_tok = view(x_buf, 0, NT, D_MODEL)
        xn = view(n_buf, 0, NT, KC, P)
        mix_t = view(n_buf, 0, KC, SEQ)
        h_t = view(t_buf, 0, KC, SEQ)
        sq = view(t_buf, 0, 4 * SEQ)
        rs = view(t_buf, 4 * SEQ, 4 * SEQ)
        qf, kf, b_chunk, b_full = (view(lin_buf, i * 3 * SEQ, 3, SEQ) for i in range(4))
        gates = view(gate_buf, 0, 4, SEQ)
        v_tok = view(v_buf, 0, NT, D_MODEL)
        mq, mk = view(mqk_buf, 0, 4, SEQ), view(mqk_buf, 4 * SEQ, 4, SEQ)
        w3 = 3 * SEQ
        dist = [view(work, (4 * i + 0) * w3, w3) for i in range(2)]
        fall = [view(work, (4 * i + 1) * w3, w3) for i in range(2)]
        q_lvl = [view(work, (4 * i + 2) * w3, 3, SEQ) for i in range(2)]
        k_lvl = [view(work, (4 * i + 3) * w3, 3, SEQ) for i in range(2)]
        log_d = view(work, 0, 3, SEQ)
        st = view(st_buf, 0, LIN_HEADS, 3 * P)
        st_pair = st_buf[:, :].rearrange("p (h i c) -> p h i c", h=2, i=4)
        sig_p, sig_n, f_low = (view(st_buf, i * 2 * SEQ, 2, SEQ) for i in range(3))
        gk_z, lr_t, gk_e = (view(st_buf, (6 + i) * SEQ, SEQ) for i in range(3))
        ln_f = view(st_buf, 9 * SEQ, 2, SEQ)
        prob = [view(work, i * 2 * 3 * P, 2, 3 * P) for i in range(2)]
        prob_t = [view(work, (2 + i) * 2 * 3 * P, 2, 3 * P) for i in range(2)]
        xg = view(work, 0, KC, P)
        sel = view(work, 1024, NT, P)
        selw = view(work, 1280, NT, P)
        selw_t = view(work, 1536, SEQ)
        silu_g = view(work, 1792, FC, P)
        hid = view(work, 2304, FC, P)
        hid_t = view(work, 2816, FC, P)
        y_e = view(work, 3328, D_MODEL)
        rt = view(work, 4352, 1024)

        ssq, std, rstd = small[:, 0:2], small[:, 2:4], small[:, 4:6]
        lb_one, lb_ind = small[:, 6:8], small[:, 8:10]
        mx4, nb4 = [small[:, 10 + 4 * i:14 + 4 * i] for i in range(2)], [small[:, 18 + 4 * i:22 + 4 * i] for i in range(2)]
        sum4, rsum4 = [small[:, 26 + 4 * i:30 + 4 * i] for i in range(2)], [small[:, 34 + 4 * i:38 + 4 * i] for i in range(2)]
        NCOL = 2 * PAIRS * ROUNDS + 4
        pos_r = view(small, 64, NT, NCOL)
        comb_r = view(small, 64 + NT * NCOL, NT, NCOL)
        lbt = small[:, 42:64]

        def sem(name):
            return ctx.enter_context(nc.semaphore(name))

        signals = []

        def signal(name, per, ahead=0):
            s = Signal(sem(name), per, ahead)
            signals.append((name, s))
            return s

        s_cst, s_par, s_x, s_zero = sem("constants_in"), sem("params_in"), sem("x_in"), sem("params_cleared")
        s_lb, s_lbe = sem("lower_bounds"), sem("lower_bound_exp")
        s_out = sem("out_stored")
        s_slot = [sem(f"slot{i}_in") for i in range(RING)]
        s_par_l = signal("layer_params", 1)
        s_ssq = signal("square_sums", 4)
        s_std = signal("std", 2)
        s_xn = signal("tokens_normed", 4)
        s_tr = signal("tokens_transposed", 8)
        s_ht = signal("h_t_ready", 8)
        s_pj = signal("projected", 15)
        s_ev = signal("projection_copied", 15)
        s_sig = signal("sigmoids", 1)
        s_flow = signal("f_low_read", 1)
        s_fcl = signal("f_clamped", 1)
        s_lnf = signal("log_f", 1)
        s_gke = signal("gla_log_part", 1)
        s_dist = signal("level_distance", LEVELS)
        s_fall = signal("level_decay", LEVELS)
        s_qk = signal("level_qk", LEVELS + 1)
        s_sc = signal("level_scores", 4 * LEVELS + 4)
        s_st = signal("level_scores_taken", 4 * LEVELS)
        s_stx = signal("cross_scores_taken", 4)
        s_sq = signal("head_squares", 6)
        s_ss = signal("head_square_sums", 6)
        s_hs = signal("head_std", 6)
        s_nrm = signal("moba_normed", 4)
        s_rot = signal("moba_swapped", 4)
        s_mqk = signal("moba_qk_ready", 4)
        s_lo = signal("linear_out", 2)
        s_lmix = signal("linear_mixed", 2)
        s_ms = signal("moba_scores", 8)
        s_mm = signal("moba_max", 4)
        s_me = signal("moba_exp", 4)
        s_mp = signal("moba_probs", 4)
        s_mt = signal("moba_probs_transposed", 4)
        s_mtc = signal("moba_probs_t_copied", 4)
        s_mo = signal("moba_out", 4)
        s_moc = signal("moba_out_copied", 4)
        s_wo = signal("out_projected", OUT_CHUNKS)
        s_xa = signal("x_attended", 2 * OUT_CHUNKS)
        s_lg = signal("router_logits", 1)
        s_ra = signal("router_exp_in", 1)
        s_re = signal("router_exp", 1)
        s_sel1 = signal("experts_chosen", 1)
        s_pos = signal("slots_counted", 1)
        s_np = signal("pair_count", 1)
        s_vec = sem("vector_step")
        s_act = sem("scalar_step")
        m_sel = signal("selection", 1)
        m_g = signal("gathered", 2)
        m_xg = signal("gathered_copied", 2)
        m_swt = signal("selection_transposed", 1)
        m_swc = signal("selection_t_copied", 1)
        m_silu = signal("silu", 1)
        m_h = signal("hidden", 1)
        m_ht = signal("hidden_transposed", 1)
        m_htc = signal("hidden_t_copied", 1)
        m_yc = signal("down_copied", 2)
        m_z = signal("scattered", 4)
        m_xadd = signal("x_added", 4, ahead=4)
        m_free = signal("expert_chunks_used", RING, ahead=RING)

        def lay(ap, l):
            return ap[l]

        def bc(ap, *shape):
            return ap.to_broadcast([P, *shape])

        block = ctx.enter_context(nc.Block())

        @block.sync
        def _(sp):
            sp.dma_start(x_tok, a["x"][0].rearrange("(t p) d -> p t d", p=P)).then_inc(s_x, 16)
            sp.dma_start(cst[:, :], a["consts"]).then_inc(s_cst, 16)
            sp.wait_ge(s_zero, 1)
            for l in range(DEPTH):
                def col(c, n=1, rows=slice(0, P)):
                    return par_all[rows, l * NPAR + c:l * NPAR + c + n]
                sp.dma_start(col(PG_ATT, KC), a["attn_norm_g"][l].rearrange("(p c) -> p c", c=KC)).then_inc(s_par, 16)
                sp.dma_start(col(PG_FFN, KC), a["ffn_norm_g"][l].rearrange("(p c) -> p c", c=KC)).then_inc(s_par, 16)
                for half in range(2):
                    rows = slice(half * HEAD, (half + 1) * HEAD)
                    for c, name in ((P_GLA, "gla_norm_g"), (P_QN, "moba_qnorm_g"), (P_KN, "moba_knorm_g"), (P_HGRN, "hgrn_norm_g")):
                        sp.dma_start(col(c, 1, rows), a[name][l].rearrange("(p o) -> p o", o=1)).then_inc(s_par, 16)
                for f in range(2):
                    sp.dma_start(col(P_LB + f), a["hgrn_lb_param"][l, f * P:(f + 1) * P].rearrange("(p o) -> p o", o=1)).then_inc(s_par, 16)
                sp.dma_start(col(P_GKB), a["gla_gk_b"][l].rearrange("(p o) -> p o", o=1)).then_inc(s_par, 16)
                sp.dma_start(col(P_W2, P, slice(0, LOWRANK)), a["gla_gk_w2"][l]).then_inc(s_par, 16)
                wr = col(P_WR, KC * NR).rearrange("p (c n) -> p c n", n=NR)
                sp.dma_start(wr[:, :, 0:GROUPS], a["w_router_group"][l].rearrange("(p c) n -> p c n", c=KC)).then_inc(s_par, 16)
                sp.dma_start(wr[:, :, GROUPS:NR], a["w_router_expert"][l].rearrange("(p c) n -> p c n", c=KC)).then_inc(s_par, 16)

            def chunk_used(l, j):
                if j < len(IN_CHUNKS):
                    sp.wait_ge(s_pj.sem, s_pj.at(l, LAST_UNIT[j] + 1))
                else:
                    sp.wait_ge(s_wo.sem, s_wo.at(l, j - len(IN_CHUNKS) + 1))

            base = 0
            for l in range(DEPTH):
                for j in range(ATT_CHUNKS):
                    if j >= RING:
                        chunk_used(l, j - RING)
                    elif l > 0:
                        sp.wait_ge(m_free.sem, m_free.at(base, j + 1 - RING))
                    slot = ring[:, (j % RING) * RING_ELEMS:(j % RING + 1) * RING_ELEMS]
                    if j < len(IN_CHUNKS):
                        c0, n = IN_CHUNKS[j]
                        dst = slot[:, 0:KC * n].rearrange("p (c n) -> p c n", c=KC)
                        src = lay(a["w_in"], l).rearrange("(p c) n -> p c n", c=KC)[:, :, c0:c0 + n]
                    else:
                        c0, n = (j - len(IN_CHUNKS)) * OUT_COLS, OUT_COLS
                        dst = slot[:, 0:KC * n].rearrange("p (c n) -> p c n", c=KC)
                        src = lay(a["w_out"], l).rearrange("(c p) n -> p c n", c=KC)[:, :, c0:c0 + n]
                    sp.dma_start(dst, src).then_inc(s_slot[j % RING], 16)

                def load_pair(before, first=False):
                    for j in range(RING):
                        kind, half = j // 2, j % 2
                        if first:
                            chunk_used(l, ATT_CHUNKS - RING + j)
                        else:
                            sp.wait_ge(m_free.sem, m_free.at(base + before, j + 1))
                        e0 = ((before + 1) % PAIRS) * 2
                        name = ("w_exp_gate", "w_exp_up", "w_exp_down")[kind]
                        w = lay(a[name], l)[bass.ds(e0, 2)]
                        rows = KC if kind < 2 else FC
                        run = rows * (FF if kind < 2 else D_MODEL) // 2
                        src = w.rearrange("e (p c) n -> p e (c n)", p=P)[:, :, half * run:(half + 1) * run]
                        dst = ring[:, j * RING_ELEMS:(j + 1) * RING_ELEMS].rearrange("p (e r) -> p e r", e=2)
                        sp.dma_start(dst, src).then_inc(s_slot[j], 16)

                load_pair(-1, first=True)
                with sp.Fori(0, PAIRS - 1) as p:
                    load_pair(p)
                sp.wait_ge(s_np.sem, s_np.at(l, 1))
                n = sp.value_load(npairs_i[0:1, l:l + 1], min_val=PAIRS, max_val=PAIRS * ROUNDS)
                with sp.If(n > PAIRS):
                    with sp.Fori(PAIRS - 1, n - 1) as p:
                        load_pair(p)
                base = base + n
            sp.wait_ge(m_xadd.sem, m_xadd.at(base, 0))
            sp.dma_start(out[0].rearrange("(t p) d -> p t d", p=P), x_tok).then_inc(s_out, 16)
            sp.wait_ge(s_out, 16)

        @block.tensor
        def _(pe):
            mm = nc.tensor.matmul

            def chunk_in(l, j, base):
                pe.wait_ge(s_slot[j % RING], 16 * (2 * l + base + j // RING + 1))

            def ring_slot(j, n):
                s = j % RING
                return ring[:, s * RING_ELEMS:s * RING_ELEMS + KC * n].rearrange("p (c n) -> p c n", c=KC)

            def transpose_tokens(l, use):
                for t in range(NT):
                    pe.wait_ge(s_xn.sem, s_xn.at(l, use * NT + t + 1))
                    for half in range(2):
                        b = t * 2 + half
                        for c in range(4):
                            last = nc.tensor.transpose(banks[:, b, c * P:(c + 1) * P], xn[:, t, half * 4 + c, :], ident)
                        s_tr.by(last)

            def project_t(u, j, f0, tiles, width=P):
                w = ring_slot(j, IN_CHUNKS[j][1])
                for i in range(tiles):
                    for c in range(KC):
                        last = mm(banks[0:width, u % 4, i * SEQ:(i + 1) * SEQ], w[:, c, f0 + i * P:f0 + i * P + width],
                                  h_t[:, c, :], start=c == 0, stop=c == KC - 1)
                return last

            def project_tok(u, t_list, j, f0, n):
                w = ring_slot(j, IN_CHUNKS[j][1])
                for i, t in enumerate(t_list):
                    for c in range(KC):
                        last = mm(banks[:, u % 4, i * n:(i + 1) * n], h_t[:, c, t * P:(t + 1) * P],
                                  w[:, c, f0:f0 + n], start=c == 0, stop=c == KC - 1)
                return last

            def head_rows(h):
                if h < GLA_HEADS:
                    return 0, h * GLA_DK, (h + 1) * GLA_DK
                return 1 + (h - GLA_HEADS) // 2, (h % 2) * HEAD, (h % 2 + 1) * HEAD

            def level(l, n):
                q_, k_ = (qf, kf) if n == 0 else (q_lvl[n % 2], k_lvl[n % 2])
                pe.wait_ge(s_qk.sem, s_qk.at(l, n + 1))
                if n == 0:
                    pe.wait_ge(s_ev.sem, s_ev.at(l, 5))
                if n > 0:
                    pe.wait_ge(s_st.sem, s_st.at(l, 4 * n))
                for hh in range(2):
                    for t in range(NT):
                        for i in range(4):
                            f, r0, r1 = head_rows(hh * 4 + i)
                            col = (2 * hh + t) * P
                            last = mm(banks[:, 4 + i, col:col + P], k_[r0:r1, f, t * P:(t + 1) * P],
                                      q_[r0:r1, f, t * P:(t + 1) * P], start=True, stop=True, tile_position=(r0, 0))
                            if hh == 1 and t == NT - 1:
                                s_sc.by(last)

            def cross(l):
                n = LEVELS
                pe.wait_ge(s_qk.sem, s_qk.at(l, n + 1))
                pe.wait_ge(s_st.sem, s_st.at(l, 4 * n))
                for hh in range(2):
                    for i in range(4):
                        f, r0, r1 = head_rows(hh * 4 + i)
                        last = mm(banks[:, 4 + i, hh * P:(hh + 1) * P], k_lvl[n % 2][r0:r1, f, 0:P],
                                  q_lvl[n % 2][r0:r1, f, P:2 * P], start=True, stop=True, tile_position=(r0, 0))
                        if hh == 1:
                            s_sc.by(last)

            def weighted_values(bank, i, h, v0, scores):
                r0 = (h % 2) * HEAD
                v = v_tok[:, :, v0 + h * HEAD:v0 + (h + 1) * HEAD]
                mm(banks[r0:r0 + HEAD, bank, i * SEQ:(i + 1) * SEQ], v[:, 0], scores[:, 0:SEQ],
                   start=True, stop=False, tile_position=(0, r0), skip_group_check=True)
                return mm(banks[r0:r0 + HEAD, bank, i * SEQ + P:(i + 1) * SEQ], v[:, 1], scores[:, SEQ:3 * P],
                          start=False, stop=True, tile_position=(0, r0), skip_group_check=True)

            def square_sums(l, g, bank):
                pe.wait_ge(s_sq.sem, s_sq.at(l, g + 1))
                s_ss.by(mm(banks[:, bank, :], head_ones, sq[:, (g % 2) * 512:(g % 2 + 1) * 512], start=True, stop=True))

            def swap_halves(l, g, bank):
                src = (mq, mk)[g // 2][:, (g % 2) * 2:(g % 2) * 2 + 2, :].rearrange("p a b -> p (a b)")
                pe.wait_ge(s_nrm.sem, s_nrm.at(l, g + 1))
                s_rot.by(mm(banks[:, bank, :], swap, src, start=True, stop=True))

            def moba_scores(l, hp):
                if hp >= 2:
                    pe.wait_ge(s_me.sem, s_me.at(l, hp - 1))
                for i in range(2):
                    r0 = i * HEAD
                    q_, k_ = mq[r0:r0 + HEAD, hp, :], mk[r0:r0 + HEAD, hp, :]
                    bank = 2 * (hp % 2) + i
                    mm(banks[:, bank, 0:P], q_[:, 0:P], k_[:, 0:P], start=True, stop=True, tile_position=(r0, 0))
                    s_ms.by(mm(banks[:, bank, P:3 * P], q_[:, P:SEQ], k_[:, 0:SEQ], start=True, stop=True,
                               tile_position=(r0, 0)))

            def moba_transpose(l, hp):
                pe.wait_ge(s_mp.sem, s_mp.at(l, hp + 1))
                if hp >= 1:
                    pe.wait_ge(s_mtc.sem, s_mtc.at(l, hp))
                for i in range(2):
                    for k in range(3):
                        dst = (0, 1, 2)[k]
                        last = nc.tensor.transpose(banks[:, 6 + i, dst * P:(dst + 1) * P], prob[hp % 2][:, i, k * P:(k + 1) * P], ident)
                s_mt.by(last)

            def moba_values(l, hp):
                pe.wait_ge(s_mtc.sem, s_mtc.at(l, hp + 1))
                if hp >= 2:
                    pe.wait_ge(s_moc.sem, s_moc.at(l, hp - 1))
                for i in range(2):
                    last = weighted_values(4 + hp % 2, 0, 2 * hp + i, 512, prob_t[hp % 2][:, i, :])
                s_mo.by(last)

            pe.wait_ge(s_cst, 16)
            base = 0
            for l in range(DEPTH):
                transpose_tokens(l, 0)
                pe.wait_ge(s_ht.sem, s_ht.at(l, 4))
                units = [
                    (0, lambda u: project_t(u, 0, 0, 2)),
                    (0, lambda u: project_t(u, 0, 256, 2)),
                    (1, lambda u: project_t(u, 1, 0, 2)),
                    (1, lambda u: project_t(u, 1, 256, 1, LOWRANK)),
                    (2, lambda u: project_t(u, 2, 0, 2)),
                    (2, lambda u: project_tok(u, (0, 1), 2, 256, 256)),
                    (None, lambda u: mm(banks[:, u % 4, 0:SEQ], par[0:LOWRANK, P_W2:P_W2 + P], lr_t[0:LOWRANK, :], start=True, stop=True)),
                    (3, lambda u: project_tok(u, (0, 1), 3, 0, 256)),
                    (4, lambda u: project_t(u, 4, 0, 2)),
                    (5, lambda u: project_t(u, 5, 0, 2)),
                    (5, lambda u: project_t(u, 5, 256, 2)),
                    (6, lambda u: project_t(u, 6, 0, 2)),
                    (6, lambda u: project_t(u, 6, 256, 2)),
                    (7, lambda u: project_tok(u, (0,), 7, 0, 512)),
                    (7, lambda u: project_tok(u, (1,), 7, 0, 512)),
                ]

                def project(u):
                    j, work_of = units[u]
                    if j is not None and (u == 0 or units[u - 1][0] != j):
                        chunk_in(l, j, base)
                    if u >= 4:
                        pe.wait_ge(s_ev.sem, s_ev.at(l, u - 3))
                    if u == 5:
                        pe.wait_ge(s_flow.sem, s_flow.at(l, 1))
                    if u == 6:
                        pe.wait_ge(s_ev.sem, s_ev.at(l, 4))
                    last = work_of(u)
                    s_pj.by(last)

                for u in range(9):
                    project(u)
                for n in range(LEVELS - 2):
                    level(l, n)
                    project(9 + n)
                for g in range(2):
                    square_sums(l, g, g)
                level(l, LEVELS - 2)
                for g in range(2, 4):
                    square_sums(l, g, g)
                level(l, LEVELS - 1)
                for g in range(4):
                    swap_halves(l, g, g)
                cross(l)
                for g in range(2):
                    pe.wait_ge(s_stx.sem, s_stx.at(l, 4))
                    pe.wait_ge(s_st.sem, s_st.at(l, 4 * LEVELS))
                    for i in range(2):
                        for hh in range(2):
                            h = 4 * g + 2 * i + hh
                            last = weighted_values(4 + g, i, h, 0, st[:, h, :])
                    s_lo.by(last)
                for g in range(4):
                    pe.wait_ge(s_mqk.sem, s_mqk.at(l, g + 1))
                moba_scores(l, 0)
                moba_scores(l, 1)
                for g in range(4, 6):
                    square_sums(l, g, g + 2)
                pe.wait_ge(s_lmix.sem, s_lmix.at(l, 2))
                for hp in range(4):
                    moba_transpose(l, hp)
                    if hp + 2 < 4:
                        moba_scores(l, hp + 2)
                    moba_values(l, hp)
                pe.wait_ge(s_moc.sem, s_moc.at(l, 4))
                for j in range(OUT_CHUNKS):
                    chunk_in(l, len(IN_CHUNKS) + j, base)
                    w = ring_slot(len(IN_CHUNKS) + j, OUT_COLS)
                    for t in range(NT):
                        for c in range(KC):
                            last = mm(banks[:, j, t * OUT_COLS:(t + 1) * OUT_COLS], mix_t[:, c, t * P:(t + 1) * P],
                                      w[:, c, :], start=c == 0, stop=c == KC - 1)
                    s_wo.by(last)

                transpose_tokens(l, 1)
                pe.wait_ge(s_ht.sem, s_ht.at(l, 8))
                wr = par[:, P_WR:P_WR + KC * NR].rearrange("p (c n) -> p c n", n=NR)
                for t in range(NT):
                    for c in range(KC):
                        last = mm(banks[:, 4, t * NR:(t + 1) * NR], h_t[:, c, t * P:(t + 1) * P], wr[:, c, :],
                                  start=c == 0, stop=c == KC - 1)
                s_lg.by(last)
                pe.wait_ge(s_sel1.sem, s_sel1.at(l, 1))
                chosen = rt[:, 0:NT * EXPERTS].rearrange("p (t e) -> p t e", t=NT)
                mm(banks[:, 5, 0:16], before, chosen[:, 0], start=True, stop=True)
                mm(banks[:, 5, 16:32], all_ones, chosen[:, 0], start=True, stop=False)
                mm(banks[:, 5, 16:32], before, chosen[:, 1], start=False, stop=True)
                mm(banks[:, 5, 32:48], all_ones, chosen[:, 0], start=True, stop=False)
                s_pos.by(mm(banks[:, 5, 32:48], all_ones, chosen[:, 1], start=False, stop=True))

                def gather(half):
                    for c in range(4 * half, 4 * half + 4):
                        for t in range(NT):
                            last = mm(banks[:, half, (c % 4) * P:(c % 4 + 1) * P], xn[:, t, c, :], sel[:, t, :],
                                      start=t == 0, stop=t == NT - 1)
                    m_g.by(last)

                def turn_selection():
                    for t in range(NT):
                        last = nc.tensor.transpose(banks[:, 4, t * P:(t + 1) * P], selw[:, t, :], ident)
                    m_swt.by(last)

                pe.wait_ge(s_np.sem, s_np.at(l, 1))
                n_pairs = pe.value_load(npairs_i[0:1, l:l + 1], min_val=PAIRS, max_val=PAIRS * ROUNDS)
                pe.wait_ge(m_sel.sem, m_sel.at(base, l + 1))
                gather(0)
                gather(1)
                turn_selection()
                with pe.Fori(0, n_pairs) as p:
                    it = base + p
                    pe.wait_ge(m_xg.sem, m_xg.at(it + l, 2))
                    for kind, bank in ((0, 3), (1, 4)):
                        if kind == 1:
                            pe.wait_ge(m_swc.sem, m_swc.at(it + l, 1))
                        for half in range(2):
                            j = 2 * kind + half
                            pe.wait_ge(s_slot[j], 16 * (2 * (l + 1) + 1 + it))
                            w = ring[:, j * RING_ELEMS:(j + 1) * RING_ELEMS].rearrange("p (e c n) -> p e c n", e=2, n=FF)
                            for c in range(4):
                                for e in range(2):
                                    r0 = e * SLOTS
                                    k = half * 4 + c
                                    last = mm(banks[r0:r0 + SLOTS, bank, :], xg[:, k, r0:r0 + SLOTS], w[:, e, c, :],
                                              start=k == 0, stop=k == KC - 1, tile_position=(0, r0), skip_group_check=True)
                            m_free.by(last)
                    pe.wait_ge(m_sel.sem, m_sel.at(it + l, 2))
                    gather(0)
                    pe.wait_ge(m_h.sem, m_h.at(it, 1))
                    for c in range(FC):
                        last = nc.tensor.transpose(banks[:, 3, c * P:(c + 1) * P], hid[:, c, :], ident)
                    m_ht.by(last)
                    turn_selection()
                    pe.wait_ge(m_htc.sem, m_htc.at(it, 1))
                    for half in range(2):
                        j = 4 + half
                        pe.wait_ge(s_slot[j], 16 * (2 * (l + 1) + 1 + it))
                        w = ring[:, j * RING_ELEMS:(j + 1) * RING_ELEMS].rearrange("p (e c n) -> p e c n", e=2, n=D_MODEL)
                        for c in range(2):
                            for nh in range(2):
                                for e in range(2):
                                    r0 = e * SLOTS
                                    k = half * 2 + c
                                    last = mm(banks[r0:r0 + SLOTS, 5 + nh, :], hid_t[:, k, r0:r0 + SLOTS],
                                              w[:, e, c, nh * 512:(nh + 1) * 512], start=k == 0, stop=k == FC - 1,
                                              tile_position=(0, r0), skip_group_check=True)
                        m_free.by(last)
                    gather(1)
                    for i in range(4):
                        t, nh = i // 2, i % 2
                        bank = (7, 2)[i % 2]
                        pe.wait_ge(m_yc.sem, m_yc.at(it, 2))
                        pe.wait_ge(m_xadd.sem, m_xadd.at(it, i - 1))
                        m_z.by(mm(banks[:, bank, :], selw_t[:, t * P:(t + 1) * P], y_e[:, nh * 512:(nh + 1) * 512],
                                  start=True, stop=True))
                base = base + n_pairs

        @block.scalar
        def _(act):
            fn = nc.scalar.activation
            steps = [0]

            def link(ins):
                steps[0] += 1
                ins.then_inc(s_act, 1)
                act.wait_ge(s_act, steps[0])

            def token_norm(l, use, ready):
                act.wait_ge(*ready)
                for t in range(NT):
                    s_ssq.by(fn(n_buf[:, t * D_MODEL:(t + 1) * D_MODEL], x_tok[:, t, :], ACT.Square, accum_out=ssq[:, t:t + 1]))
                act.wait_ge(s_ssq.sem, s_ssq.at(l, NT * (use + 1)))
                s_std.by(fn(std, ssq, ACT.Sqrt, bias=eps, scale=1.0 / D_MODEL))

            def bank2(b):
                return banks[:, b, :].rearrange("p (a b) -> p a b", a=2)

            act.wait_ge(s_cst, 16)
            act.wait_ge(s_lb, 1)
            fn(lbt[:, 0:2 * DEPTH], lbt[:, 0:2 * DEPTH], ACT.Exp).then_inc(s_lbe, 1)
            base = 0
            for l in range(DEPTH):
                token_norm(l, 0, (s_x, 16) if l == 0 else (m_xadd.sem, m_xadd.at(base, 0)))

                def copy_unit(u):
                    b = u % 4
                    act.wait_ge(s_pj.sem, s_pj.at(l, u + 1))
                    if u == 0:
                        last = fn(qf[:, 1:3, :], bank2(b), ACT.Silu)
                    elif u == 1:
                        fn(sig_p, bank2(b), ACT.Sigmoid)
                        last = fn(sig_n, bank2(b), ACT.Sigmoid, scale=-1.0)
                    elif u == 2:
                        last = fn(gates[:, 0:2, :], bank2(b), ACT.Silu)
                    elif u == 3:
                        last = fn(lr_t[0:LOWRANK, :], banks[0:LOWRANK, b, 0:SEQ], ACT.Copy)
                    elif u == 4:
                        fn(qf[:, 0, :], banks[:, b, 0:SEQ], ACT.Copy, scale=float(GLA_DK) ** -0.5)
                        last = fn(kf[:, 0, :], banks[:, b, SEQ:2 * SEQ], ACT.Copy)
                    elif u == 5:
                        last = fn(v_tok[:, :, 0:256], bank2(b), ACT.Copy)
                    elif u == 6:
                        last = fn(gk_z, banks[:, b, 0:SEQ], ACT.Identity, bias=par[:, P_GKB:P_GKB + 1])
                    elif u == 7:
                        last = fn(v_tok[:, :, 256:512], bank2(b), ACT.Copy)
                    elif u == 8:
                        last = fn(gates[:, 2:4, :], bank2(b), ACT.Silu)
                    elif u < 13:
                        dst, i = ((mq, 0), (mq, 2), (mk, 0), (mk, 2))[u - 9]
                        last = fn(dst[:, i:i + 2, :], bank2(b), ACT.Copy)
                    else:
                        last = fn(v_tok[:, u - 13, 512:1024], banks[:, b, :], ACT.Copy)
                    s_ev.by(last)

                def level_decay(n):
                    act.wait_ge(s_dist.sem, s_dist.at(l, n))
                    link(fn(dist[n % 2], dist[n % 2], ACT.Abs))
                    s_fall.by(fn(fall[n % 2], dist[n % 2], ACT.Exp, scale=-1.0))

                act.wait_ge(s_par_l.sem, s_par_l.at(l, 1))
                for u in range(7):
                    copy_unit(u)
                act.wait_ge(s_ev.sem, s_ev.at(l, 7))
                link(fn(gk_e, gk_z, ACT.Abs))
                link(fn(gk_e, gk_e, ACT.Exp, scale=-1.0))
                s_gke.by(fn(gk_e, gk_e, ACT.Ln, bias=one))
                act.wait_ge(s_fcl.sem, s_fcl.at(l, 1))
                s_lnf.by(fn(ln_f, sig_p, ACT.Ln))
                copy_unit(7)
                copy_unit(8)
                level_decay(1)
                level_decay(2)
                for u in range(9, 15):
                    copy_unit(u)
                    level_decay(u - 6)

                def head_std(g, bank):
                    act.wait_ge(s_ss.sem, s_ss.at(l, g + 1))
                    s_hs.by(fn(rs[:, (g % 2) * 512:(g % 2 + 1) * 512], banks[:, bank, :], ACT.Sqrt, bias=eps, scale=1.0 / HEAD))

                for g in range(4):
                    if g >= 2:
                        act.wait_ge(s_ss.sem, s_ss.at(l, g - 1))
                    src = (mq, mk)[g // 2][:, (g % 2) * 2:(g % 2) * 2 + 2, :].rearrange("p a b -> p (a b)")
                    s_sq.by(fn(sq[:, (g % 2) * 512:(g % 2 + 1) * 512], src, ACT.Square))
                    if g % 2:
                        for gg in (g - 1, g):
                            if gg >= 2:
                                act.wait_ge(s_nrm.sem, s_nrm.at(l, gg - 1))
                            head_std(gg, gg)
                for i in range(4):
                    act.wait_ge(s_sc.sem, s_sc.at(l, 4 * LEVELS + i + 1))
                    src = banks[:, 4 + i, 0:2 * P].rearrange("p (h i) -> p h i", h=2)
                    s_stx.by(fn(st_pair[:, :, i, P:2 * P], src, ACT.Copy))
                for g in range(4, 6):
                    act.wait_ge(s_lo.sem, s_lo.at(l, g - 3))
                    act.wait_ge(s_ss.sem, s_ss.at(l, g - 1))
                    s_sq.by(fn(sq[:, (g % 2) * 512:(g % 2 + 1) * 512], banks[:, g, :], ACT.Square))
                for g in range(4, 6):
                    act.wait_ge(s_nrm.sem, s_nrm.at(l, g - 1))
                    head_std(g, g + 2)

                def moba_exp(hp):
                    act.wait_ge(s_mm.sem, s_mm.at(l, hp + 1))
                    k = hp % 2
                    for i in range(2):
                        for qt in range(2):
                            c = 2 * i + qt
                            o = prob[k][:, i, 0:P] if qt == 0 else prob[k][:, i, P:3 * P]
                            src = banks[:, 2 * k + i, 0:P] if qt == 0 else banks[:, 2 * k + i, P:3 * P]
                            last = fn(o, src, ACT.Exp, bias=nb4[k][:, c:c + 1], scale=HEAD ** -0.5, accum_out=sum4[k][:, c:c + 1])
                    s_me.by(last)

                moba_exp(0)
                moba_exp(1)
                for hp in range(4):
                    act.wait_ge(s_mt.sem, s_mt.at(l, hp + 1))
                    if hp >= 2:
                        act.wait_ge(s_mo.sem, s_mo.at(l, hp - 1))
                    src = banks[:, 6:8, 0:3 * P]
                    s_mtc.by(fn(prob_t[hp % 2], src, ACT.Copy))
                    if hp + 2 < 4:
                        moba_exp(hp + 2)
                    act.wait_ge(s_mo.sem, s_mo.at(l, hp + 1))
                    s_moc.by(fn(mix_t[:, 2 + hp, :], banks[:, 4 + hp % 2, 0:SEQ], ACT.Copy))

                token_norm(l, 1, (s_xa.sem, s_xa.at(l, 2 * OUT_CHUNKS)))
                act.wait_ge(s_ra.sem, s_ra.at(l, 1))
                s_re.by(fn(rt[:, R_EXP:R_EXP + 10], rt[:, R_EXP:R_EXP + 10], ACT.Exp))

                act.wait_ge(s_np.sem, s_np.at(l, 1))
                n_pairs = act.value_load(npairs_i[0:1, l:l + 1], min_val=PAIRS, max_val=PAIRS * ROUNDS)

                def copy_selection(i):
                    act.wait_ge(m_swt.sem, i)
                    m_swc.by(fn(selw_t, banks[:, 4, 0:SEQ], ACT.Copy))

                copy_selection(m_swt.at(base + l, 1))
                with act.Fori(0, n_pairs) as p:
                    it = base + p
                    act.wait_ge(m_free.sem, m_free.at(it, 2))
                    m_silu.by(fn(silu_g, banks[:, 3, :].rearrange("s (p c) -> s c p", c=FC), ACT.Silu))
                    act.wait_ge(m_ht.sem, m_ht.at(it, 1))
                    m_htc.by(fn(hid_t, banks[:, 3, :].rearrange("p (c s) -> p c s", c=FC), ACT.Copy))
                    act.wait_ge(m_free.sem, m_free.at(it, RING))
                    for nh in range(2):
                        m_yc.by(fn(y_e[:, nh * 512:(nh + 1) * 512], banks[:, 5 + nh, :], ACT.Copy))
                    act.wait_ge(m_z.sem, m_z.at(it, 4))
                    copy_selection(m_swt.at(it + l, 2))
                base = base + n_pairs

        @block.vector
        def _(dve):
            v = nc.vector
            steps = [0]

            def link(ins):
                steps[0] += 1
                ins.then_inc(s_vec, 1)
                dve.wait_ge(s_vec, steps[0])

            def pc(c, n=1):
                return par[:, c:c + n]

            def halves(g):
                return slice((g % 2) * 512, (g % 2 + 1) * 512)

            v.memset(par_all[:, :], 0.0).then_inc(s_zero, 1)
            v.memset(small[:, 0:320], 0.0).then_inc(m_xadd.sem, m_xadd.ahead)
            v.memset(small[:, 320:640], 0.0).then_inc(m_free.sem, m_free.ahead)
            dve.wait_ge(m_xadd.sem, m_xadd.ahead)
            dve.wait_ge(m_free.sem, m_free.ahead)
            dve.wait_ge(s_cst, 16)
            dve.wait_ge(s_par, 16 * 16 * DEPTH)
            lb_cols = [par_all[:, l * NPAR + P_LB:l * NPAR + P_LB + 2] for l in range(DEPTH)]
            top, tot, part = lbt[:, 16:18], lbt[:, 18:20], lbt[:, 20:22]
            link(v.tensor_copy(top, lb_cols[0]))
            for l in range(1, DEPTH):
                link(v.tensor_tensor(top, top, lb_cols[l], ALU.max))
            for l in range(DEPTH):
                last = v.tensor_tensor(lbt[:, 2 * l:2 * l + 2], lb_cols[l], top, ALU.subtract)
            last.then_inc(s_lb, 1)
            dve.wait_ge(s_lbe, 1)
            link(v.tensor_copy(tot, lbt[:, 0:2]))
            for l in range(1, DEPTH):
                link(v.tensor_tensor(tot, tot, lbt[:, 2 * l:2 * l + 2], ALU.add))
            link(v.reciprocal(tot, tot))
            for l in range(DEPTH):
                link(v.tensor_tensor(lbt[:, 2 * l:2 * l + 2], lbt[:, 2 * l:2 * l + 2], tot, ALU.mult))
            link(v.tensor_copy(part, lbt[:, 0:2]))
            for l in range(DEPTH):
                if l > 0:
                    link(v.tensor_tensor(part, part, lbt[:, 2 * l:2 * l + 2], ALU.add))
                link(v.tensor_tensor(lb_cols[l], part, lbt[:, 0:2], ALU.subtract))

            base = 0
            for l in range(DEPTH):
                link(v.tensor_copy(par[:, :], par_all[:, l * NPAR:(l + 1) * NPAR]))
                lb = pc(P_LB, 2)
                link(v.tensor_scalar(lb_one, lb, -1.0, 1.0, ALU.mult, ALU.add))
                s_par_l.by(v.tensor_scalar(lb_ind, lb, F_MIN, None, ALU.is_lt))

                def norm_tokens(use, gain):
                    dve.wait_ge(s_std.sem, s_std.at(l, use + 1))
                    link(v.reciprocal(rstd, std))
                    for t in range(NT):
                        s_xn.by(v.tensor_scalar(xn[:, t], x_tok[:, t].rearrange("p (q c) -> p c q", c=KC), rstd[:, t:t + 1],
                                                None, ALU.mult))
                    for t in range(NT):
                        for half in range(2):
                            b = 2 * t + half
                            dve.wait_ge(s_tr.sem, s_tr.at(l, 4 * use + b + 1))
                            g = pc(gain + 4 * half, 4).unsqueeze(2)
                            s_ht.by(v.tensor_tensor(h_t[:, half * 4:half * 4 + 4, t * P:(t + 1) * P],
                                                    banks[:, b, :].rearrange("p (c t) -> p c t", c=4), bc(g, 4, P), ALU.mult))

                norm_tokens(0, PG_ATT)
                dve.wait_ge(s_par_l.sem, s_par_l.at(l, 1))
                dve.wait_ge(s_ev.sem, s_ev.at(l, 2))
                bank1 = banks[:, 1, :].rearrange("p (a b) -> p a b", a=2)
                s_flow.by(v.tensor_scalar(f_low, bank1, -LN_F_MIN, 0.0, ALU.add, ALU.min))
                for f in range(2):
                    link(v.tensor_scalar(sig_p[:, f, :], sig_p[:, f, :], lb_one[:, f:f + 1], lb[:, f:f + 1], ALU.mult, ALU.add))
                s_fcl.by(v.tensor_scalar(sig_p, sig_p, F_MIN, None, ALU.max))
                for f in range(2):
                    last = v.tensor_scalar(kf[:, 1 + f, :], sig_n[:, f, :], lb_one[:, f:f + 1], None, ALU.mult)
                s_qk.by(last)
                dve.wait_ge(s_gke.sem, s_gke.at(l, 1))
                link(v.scalar_tensor_tensor(log_d[:, 0, :], gk_z, 0.0, gk_e, ALU.min, ALU.subtract))
                link(v.tensor_scalar(log_d[:, 0, :], log_d[:, 0, :], 1.0 / GLA_TAU, None, ALU.mult))
                dve.wait_ge(s_lnf.sem, s_lnf.at(l, 1))
                dve.wait_ge(s_flow.sem, s_flow.at(l, 1))
                for f in range(2):
                    link(v.scalar_tensor_tensor(log_d[:, 1 + f, :], f_low[:, f, :], lb_ind[:, f:f + 1], ln_f[:, f, :],
                                                ALU.mult, ALU.add))
                for f in range(3):
                    link(v.tensor_tensor_scan(b_chunk[:, f, :], const("chunk_keep"), log_d[:, f, :], 0.0, ALU.mult, ALU.add))
                    link(v.tensor_tensor_scan(b_full[:, f, :], const("ones_row"), log_d[:, f, :], 0.0, ALU.mult, ALU.add))

                def level_distance(n):
                    s = 1 << (n - 1)
                    b = (b_chunk if 2 * s <= LIN_CHUNK else b_full).rearrange("p f (k w) -> p (f k) w", w=2 * s)
                    o = dist[n % 2].rearrange("p (k w) -> p k w", w=2 * s)
                    s_dist.by(v.tensor_tensor(o, b, bc(b[:, :, s - 1:s], 3 * SEQ // (2 * s), 2 * s), ALU.subtract))

                def level_scale(n):
                    dve.wait_ge(s_fall.sem, s_fall.at(l, n))
                    f = fall[n % 2].rearrange("p (f t) -> p f t", f=3)
                    v.tensor_tensor(q_lvl[n % 2], qf, f, ALU.mult)
                    s_qk.by(v.tensor_tensor(k_lvl[n % 2], kf, f, ALU.mult))

                def take_scores(n):
                    mask = masks[:, n:n + 1, :].unsqueeze(1)
                    for i in range(4):
                        dve.wait_ge(s_sc.sem, s_sc.at(l, 4 * n + i + 1))
                        src = banks[:, 4 + i, :].rearrange("p (h t i) -> p h t i", h=2, t=NT)
                        dst = st_pair[:, :, i, :].rearrange("p h (k c) -> p h k c", k=3)[:, :, 0:3:2, :]
                        if n == 0:
                            s_st.by(v.tensor_tensor(dst, src, bc(mask, 2, NT, P), ALU.mult))
                        else:
                            dve.wait_ge(s_st.sem, s_st.at(l, 4 * (n - 1) + i + 1))
                            s_st.by(v.copy_predicated(dst, bc(mask.bitcast(U32), 2, NT, P), src))

                level_distance(1)
                level_distance(2)
                level_scale(1)
                take_scores(0)
                for n in range(3, LEVELS + 1):
                    level_distance(n)
                    level_scale(n - 1)
                    take_scores(n - 2)
                level_scale(LEVELS)
                def moba_norm(g):
                    dve.wait_ge(s_hs.sem, s_hs.at(l, g + 1))
                    link(v.reciprocal(rs[:, halves(g)], rs[:, halves(g)]))
                    m = (mq, mk)[g // 2][:, (g % 2) * 2:(g % 2) * 2 + 2, :].rearrange("p a b -> p (a b)")
                    s_nrm.by(v.scalar_tensor_tensor(m, m, pc(P_QN + g // 2), rs[:, halves(g)], ALU.mult, ALU.mult))

                moba_norm(0)
                moba_norm(1)
                moba_norm(2)
                moba_norm(3)
                take_scores(LEVELS - 1)
                tmp = work[:, 4 * w3 + 0:4 * w3 + 512]
                for g in range(4):
                    m = (mq, mk)[g // 2][:, (g % 2) * 2:(g % 2) * 2 + 2, :]
                    dve.wait_ge(s_rot.sem, s_rot.at(l, g + 1))
                    tmp3 = tmp.rearrange("p (a b) -> p a b", a=2)
                    v.tensor_tensor(tmp3, banks[:, g, :].rearrange("p (a b) -> p a b", a=2), bc(sin.unsqueeze(1), 2, SEQ), ALU.mult)
                    link(v.tensor_tensor(m, m, bc(cos.unsqueeze(1), 2, SEQ), ALU.mult))
                    s_mqk.by(v.tensor_tensor(m, m, tmp3, ALU.add))
                    dve.wait_ge(s_mqk.sem, s_mqk.at(l, g + 1))

                def moba_max(hp):
                    k = hp % 2
                    dve.wait_ge(s_ms.sem, s_ms.at(l, 2 * hp + 2))
                    first = banks[:, 2 * k:2 * k + 2, 0:P]
                    second = banks[:, 2 * k:2 * k + 2, P:3 * P]
                    mask = bc(causal.unsqueeze(1), 2, P)
                    v.tensor_tensor(first, first, mask, ALU.add)
                    link(v.tensor_tensor(second[:, :, P:SEQ], second[:, :, P:SEQ], mask, ALU.add))
                    m = mx4[k].rearrange("p (i q) -> p i q", i=2)
                    v.tensor_reduce(m[:, :, 0:1], first, AX.X, ALU.max)
                    link(v.tensor_reduce(m[:, :, 1:2], second, AX.X, ALU.max))
                    s_mm.by(v.tensor_scalar(nb4[k], mx4[k], -(HEAD ** -0.5), None, ALU.mult))

                def moba_normalise(hp):
                    k = hp % 2
                    dve.wait_ge(s_me.sem, s_me.at(l, hp + 1))
                    link(v.reciprocal(rsum4[k], sum4[k]))
                    r = rsum4[k].rearrange("p (i q) -> p i q", i=2)
                    v.tensor_tensor(prob[k][:, :, 0:P], prob[k][:, :, 0:P], bc(r[:, :, 0:1], 2, P), ALU.mult)
                    s_mp.by(v.tensor_tensor(prob[k][:, :, P:3 * P], prob[k][:, :, P:3 * P], bc(r[:, :, 1:2], 2, 2 * P), ALU.mult))

                moba_max(0)
                moba_max(1)
                for g in range(2):
                    dve.wait_ge(s_hs.sem, s_hs.at(l, 5 + g))
                    link(v.reciprocal(rs[:, halves(g)], rs[:, halves(g)]))
                    link(v.scalar_tensor_tensor(tmp, banks[:, 4 + g, :], pc((P_GLA, P_HGRN)[g]), rs[:, halves(g)], ALU.mult, ALU.mult))
                    dst = mix_t[:, 6 * g:6 * g + 2, :]
                    s_lmix.by(v.tensor_tensor(dst, tmp.rearrange("p (a b) -> p a b", a=2), gates[:, 2 * g:2 * g + 2, :], ALU.mult))
                    dve.wait_ge(s_lmix.sem, s_lmix.at(l, g + 1))
                moba_normalise(0)
                moba_max(2)
                moba_normalise(1)
                moba_max(3)
                moba_normalise(2)
                moba_normalise(3)
                for j in range(OUT_CHUNKS):
                    dve.wait_ge(s_wo.sem, s_wo.at(l, j + 1))
                    for t in range(NT):
                        xs = x_tok[:, t, j * OUT_COLS:(j + 1) * OUT_COLS]
                        s_xa.by(v.tensor_tensor(xs, xs, banks[:, j, t * OUT_COLS:(t + 1) * OUT_COLS], ALU.add))

                norm_tokens(1, PG_FFN)
                NE = EXPERTS
                chosen = view(rt, 0, NT, NE)
                logits = view(rt, 32, NT, NR)
                lg, le = logits[:, :, 0:GROUPS], logits[:, :, GROUPS:NR]
                eg, goh = view(rt, 80, NT, GROUPS), view(rt, 96, NT, GROUPS)
                ee, oh1, oh2, lem = (view(rt, 128 + 32 * i, NT, NE) for i in range(4))
                lem2, comb, slots_ = (view(rt, 256 + 32 * i, NT, NE) for i in range(3))
                one2 = [view(rt, 384 + 2 * i, NT, 1) for i in range(8)]
                gmax, vm, m1, m2, gg, w1, w2, den = one2
                ex_g = view(rt, R_EXP, NT, GROUPS)
                ex_e = view(rt, R_EXP + NT * GROUPS, NT, 1)
                rank = const("rank").unsqueeze(1)

                def first_max(vals, top, hot, scratch, n):
                    link(v.tensor_reduce(top, vals, AX.X, ALU.max))
                    link(v.tensor_tensor(scratch, vals, bc(top, NT, n), ALU.is_equal))
                    link(v.tensor_tensor(scratch, scratch, bc(rank[:, :, 0:n], NT, n), ALU.mult))
                    link(v.tensor_reduce(vm, scratch, AX.X, ALU.max))
                    link(v.tensor_tensor(hot, scratch, bc(vm, NT, n), ALU.is_equal))

                dve.wait_ge(s_lg.sem, s_lg.at(l, 1))
                link(v.tensor_copy(logits, banks[:, 4, 0:NT * NR].rearrange("p (t n) -> p t n", t=NT)))
                first_max(lg, gmax, goh, eg, GROUPS)
                link(v.tensor_tensor(ex_g, lg, bc(gmax, NT, GROUPS), ALU.subtract))
                link(v.tensor_scalar(goh, goh, -1.0, -NEG, ALU.add, ALU.mult))
                for t in range(NT):
                    link(v.tensor_tensor(lem[:, t].rearrange("p (g e) -> p g e", g=GROUPS),
                                         le[:, t].rearrange("p (g e) -> p g e", g=GROUPS),
                                         bc(goh[:, t].unsqueeze(2), GROUPS, NE // GROUPS), ALU.add))
                first_max(lem, m1, oh1, ee, NE)
                link(v.scalar_tensor_tensor(lem2, oh1, 2 * NEG, lem, ALU.mult, ALU.add))
                first_max(lem2, m2, oh2, ee, NE)
                s_ra.by(v.tensor_tensor(ex_e, m2, m1, ALU.subtract))
                s_sel1.by(v.tensor_tensor(chosen, oh1, oh2, ALU.add))
                dve.wait_ge(s_sel1.sem, s_sel1.at(l, 1))
                dve.wait_ge(s_re.sem, s_re.at(l, 1))
                link(v.tensor_reduce(gg, ex_g, AX.X, ALU.add))
                link(v.reciprocal(gg, gg))
                link(v.tensor_scalar(den, ex_e, 1.0, None, ALU.add))
                link(v.reciprocal(den, den))
                link(v.tensor_tensor(w1, den, gg, ALU.mult))
                link(v.tensor_tensor(w2, w1, ex_e, ALU.mult))
                link(v.tensor_tensor(oh1, oh1, bc(w1, NT, NE), ALU.mult))
                link(v.tensor_tensor(oh2, oh2, bc(w2, NT, NE), ALU.mult))
                link(v.tensor_tensor(comb, oh1, oh2, ALU.add))
                link(v.memset(pos_r, -1.0))
                link(v.memset(comb_r, 0.0))
                dve.wait_ge(s_pos.sem, s_pos.at(l, 1))
                link(v.scalar_tensor_tensor(slots_, banks[:, 5, 0:2 * NE].rearrange("p (t e) -> p t e", t=NT), 1.0, chosen,
                                            ALU.add, ALU.mult))
                for r in range(ROUNDS):
                    link(v.tensor_scalar(pos_r[:, :, r * NE:(r + 1) * NE], slots_, -1.0 - r * SLOTS, None, ALU.add))
                    link(v.tensor_copy(comb_r[:, :, r * NE:(r + 1) * NE], comb))
                fullest, over = rt[:, 420:421], rt[:, 424:424 + ROUNDS - 1]
                link(v.tensor_reduce(fullest, banks[:, 5, 32:48], AX.X, ALU.max))
                link(v.tensor_scalar(over, const("edges"), fullest, None, ALU.is_lt))
                link(v.tensor_reduce(fullest, over, AX.X, ALU.add))
                s_np.by(v.tensor_scalar(npairs_i[:, l:l + 1], fullest, float(PAIRS), float(PAIRS), ALU.mult, ALU.add))

                dve.wait_ge(s_np.sem, s_np.at(l, 1))
                n_pairs = dve.value_load(npairs_i[0:1, l:l + 1], min_val=PAIRS, max_val=PAIRS * ROUNDS)

                def select(c):
                    for t in range(NT):
                        for e in range(2):
                            pos = pos_r[:, t, bass.ds(c + e, 1)]
                            wgt = comb_r[:, t, bass.ds(c + e, 1)]
                            o = slice(e * SLOTS, (e + 1) * SLOTS)
                            v.tensor_scalar(sel[:, t, o], const("slot"), pos, None, ALU.is_equal)
                            last = v.tensor_scalar(selw[:, t, o], const("slot"), pos, wgt, ALU.is_equal, ALU.mult)
                    m_sel.by(last)

                def copy_gathered(half, value):
                    dve.wait_ge(m_g.sem, value)
                    g = pc(PG_FFN + 4 * half, 4).unsqueeze(2)
                    m_xg.by(v.tensor_tensor(xg[:, 4 * half:4 * half + 4, :], banks[:, half, :].rearrange("p (c s) -> p c s", c=4),
                                            bc(g, 4, P), ALU.mult))

                select(0)
                for half in range(2):
                    copy_gathered(half, m_g.at(base + l, half + 1))
                with dve.Fori(0, n_pairs) as p:
                    it = base + p
                    dve.wait_ge(m_free.sem, m_free.at(it, 1))
                    select(2 * p + 2)
                    dve.wait_ge(m_silu.sem, m_silu.at(it, 1))
                    dve.wait_ge(m_free.sem, m_free.at(it, 4))
                    m_h.by(v.tensor_tensor(hid, silu_g, banks[:, 4, :].rearrange("s (p c) -> s c p", c=FC), ALU.mult))
                    for half in range(2):
                        copy_gathered(half, m_g.at(it + l, 2 + half + 1))
                    for i in range(4):
                        t, nh = i // 2, i % 2
                        dve.wait_ge(m_z.sem, m_z.at(it, i + 1))
                        dve.wait_ge(m_xadd.sem, m_xadd.at(it, i - 3))
                        xs = x_tok[:, t, nh * 512:(nh + 1) * 512]
                        m_xadd.by(v.tensor_tensor(xs, xs, banks[:, (7, 2)[i % 2], :], ALU.add))
                base = base + n_pairs


def kernel(**inputs):
    import numpy as _np
    import concourse.bacc as _bacc
    from concourse import mybir as _mybir
    from concourse.bass_utils import run_bass_kernel_spmd as _run

    consts = host_constants()
    nc = _bacc.Bacc("TRN2", target_bir_lowering=False, num_devices=1)
    arrays, args = {}, {}
    for name, value in {**inputs, "consts": consts}.items():
        a = _np.ascontiguousarray(value)
        arrays[f"in_{name}_dram"] = a
        args[name] = nc.dram_tensor(f"in_{name}_dram", a.shape, _mybir.dt.from_np(a.dtype), kind="ExternalInput").ap()
    shape = inputs["x"].shape
    out = nc.dram_tensor("out_dram", shape, _mybir.dt.float32, kind="ExternalOutput").ap()
    build(nc, args, out)
    return _run(nc, [arrays], core_ids=[0]).results[0]["out_dram"]
```

```python
from contextlib import ExitStack

import numpy as np

import concourse.bass as bass
from concourse import mybir

F32 = mybir.dt.float32
U32 = mybir.dt.uint32
I32 = mybir.dt.int32
ALU = mybir.AluOpType
ACT = mybir.ActivationFunctionType
AX = mybir.AxisListType

P = 128
D_MODEL = 1024
SEQ = 256
DEPTH = 2
NT = SEQ // P
KC = D_MODEL // P
LIN_HEADS = 8
GLA_HEADS = 4
GLA_DK = 32
LOWRANK = 16
HEAD = 64
LIN_CHUNK = 16
MOBA_HEADS = 8
EXPERTS = 16
GROUPS = 4
FF = 512
FC = FF // P
EPS = 1e-6
GLA_TAU = 16.0
SLOTS = 64
ROUNDS = SEQ // SLOTS
PAIRS = EXPERTS // 2
LEVELS = 8
NEG = -1.0e30
F_MIN = 2.0 ** -60
LN_F_MIN = float(np.log(F_MIN))

A_Q, A_K, A_V, A_G, A_LR, B_Q, B_K, B_V, C_Q, C_F, C_I, C_G = (
    0, 128, 256, 512, 768, 784, 1296, 1808, 2320, 2576, 2832, 3088)
IN_CHUNKS = [(C_Q, 512), (A_G, 272), (A_Q, 256), (B_Q, 512), (B_K, 512), (A_V, 256), (C_I, 512), (B_V, 512)]
LAST_UNIT = [1, 3, 4, 7, 9, 10, 12, 14]
OUT_COLS = 256
OUT_CHUNKS = D_MODEL // OUT_COLS
RING = 6
RING_ELEMS = 4096
ATT_CHUNKS = len(IN_CHUNKS) + OUT_CHUNKS
assert ATT_CHUNKS % RING == 0

PG_ATT, PG_FFN, PG_ROUTER, P_GLA, P_QN, P_KN, P_HGRN, P_LB, P_GKB, P_W2 = 0, 8, 16, 24, 25, 26, 27, 28, 30, 31
NR = GROUPS + EXPERTS
P_WR = P_W2 + P
NPAR = P_WR + KC * NR
R_EXP = 400

CONSTS = {}
EARLY = P + 2


def host_constants():
    i = np.arange(P)
    cols = []

    def add(name, a):
        a = np.asarray(a, np.float32).reshape(P, -1)
        CONSTS[name] = (sum(c.shape[1] for c in cols), a.shape[1])
        cols.append(a)

    add("ident", np.eye(P))
    add("eps", np.full((P, 1), EPS))
    add("one", np.ones((P, 1)))
    add("head_ones", (i[:, None] // HEAD) == (i[None, :] // HEAD))
    add("all_ones", np.ones((P, P)))
    add("before", i[:, None] < i[None, :])
    d = i % HEAD
    swap = np.zeros((P, P))
    for m in range(P):
        if d[m] < 8:
            swap[m + 8, m] = -1.0
        elif d[m] < 16:
            swap[m - 8, m] = 1.0
    add("swap", swap)
    inv = np.float32(500000.0) ** (-(np.arange(0, 16, 2, dtype=np.float32) / np.float32(16)))
    ang = np.arange(SEQ, dtype=np.float32)[:, None] * inv[None, :].astype(np.float32)
    cos, sin = np.ones((P, SEQ)), np.zeros((P, SEQ))
    for m in range(P):
        if d[m] < 16:
            cos[m] = np.cos(ang[:, d[m] % 8])
            sin[m] = np.sin(ang[:, d[m] % 8])
    add("cos", cos)
    add("sin", sin)
    add("causal", np.where(i[None, :] <= i[:, None], 0.0, NEG))
    masks = np.zeros((P, LEVELS, P))
    masks[i, 0, i] = 1.0
    for n in range(1, LEVELS):
        s = 1 << (n - 1)
        same = (i[:, None] // (2 * s)) == (i[None, :] // (2 * s))
        masks[:, n] = same & ((i[:, None] // s) % 2 == 0) & ((i[None, :] // s) % 2 == 1)
    add("masks", masks)
    add("chunk_keep", np.tile((np.arange(SEQ) % LIN_CHUNK != 0)[None, :], (P, 1)))
    add("ones_row", np.ones((P, SEQ)))
    add("edges", np.tile(np.arange(1, ROUNDS) * SLOTS, (P, 1)))
    add("slot", np.tile(np.arange(SLOTS), (P, 1)))
    add("rank", np.tile(EXPERTS - np.arange(EXPERTS), (P, 1)))
    return np.concatenate(cols, axis=1)


def packed_params(a):
    out = np.zeros((P, DEPTH, NPAR), np.float32)

    def put(l, c, value):
        out[:value.shape[0], l, c:c + value.shape[1]] = value

    for l in range(DEPTH):
        put(l, PG_ATT, a["attn_norm_g"][l].reshape(P, KC))
        put(l, PG_FFN, a["ffn_norm_g"][l].reshape(P, KC))
        put(l, PG_ROUTER, a["ffn_norm_g"][l].reshape(KC, P).T)
        for c, name in ((P_GLA, "gla_norm_g"), (P_QN, "moba_qnorm_g"), (P_KN, "moba_knorm_g"), (P_HGRN, "hgrn_norm_g")):
            put(l, c, np.tile(a[name][l], P // HEAD)[:, None])
        put(l, P_LB, a["hgrn_lb_param"][l].reshape(2, P).T)
        put(l, P_GKB, a["gla_gk_b"][l][:, None])
        put(l, P_W2, a["gla_gk_w2"][l])
        router = np.concatenate([a["w_router_group"][l], a["w_router_expert"][l]], axis=1)
        put(l, P_WR, router.reshape(KC, P, NR).transpose(1, 0, 2).reshape(P, KC * NR))
    return out.reshape(P, DEPTH * NPAR)


class Signal:

    def __init__(self, sem, per, ahead=0):
        self.sem, self.per, self.ahead = sem, per, ahead

    def by(self, ins, k=1):
        ins.then_inc(self.sem, k)
        return ins

    def at(self, base, n):
        return base * self.per + (n + self.ahead)


def build(nc, a, out):
    with ExitStack() as ctx:
        def sb(name, cols, dt=F32):
            return ctx.enter_context(nc.sbuf_tensor(name, [P, cols], dt))

        def view(t, off, *dims):
            n = int(np.prod(dims))
            v = t[:, off:off + n]
            if len(dims) == 2:
                v = v.rearrange("p (a b) -> p a b", a=dims[0])
            elif len(dims) == 3:
                v = v.rearrange("p (a b c) -> p a b c", a=dims[0], b=dims[1])
            return v

        ncst = sum(n for _, n in CONSTS.values())
        cst = sb("cst", ncst)
        par_all = sb("par_all", DEPTH * NPAR)
        ring = sb("ring", RING * RING_ELEMS)
        x_buf = sb("x_buf", NT * D_MODEL)
        n_buf = sb("n_buf", NT * D_MODEL)
        t_buf = sb("t_buf", KC * SEQ)
        lin_buf = sb("lin_buf", 4 * 3 * SEQ)
        gate_buf = sb("gate_buf", 4 * SEQ)
        v_buf = sb("v_buf", NT * D_MODEL)
        mqk_buf = sb("mqk_buf", 2 * 4 * SEQ)
        work = sb("work", 8 * 3 * SEQ)
        st_buf = sb("st_buf", LIN_HEADS * 3 * P)
        small = sb("small", 640)
        npairs_i = sb("npairs_i", 2, I32)
        banks = ctx.enter_context(nc.psum_tensor("banks", [P, 8, 512], F32))

        def const(name, *dims):
            off, n = CONSTS[name]
            return view(cst, off, *(dims or (n,)))

        ident, head_ones, all_ones, before, swap = (const(n) for n in ("ident", "head_ones", "all_ones", "before", "swap"))
        cos, sin, causal = const("cos"), const("sin"), const("causal")
        masks = const("masks", LEVELS, P)
        eps, one = const("eps"), const("one")

        x_tok = view(x_buf, 0, NT, D_MODEL)
        xn = view(n_buf, 0, NT, KC, P)
        mix_t = view(n_buf, 0, KC, SEQ)
        h_t = view(t_buf, 0, KC, SEQ)
        qf, kf, b_chunk, b_full = (view(lin_buf, i * 3 * SEQ, 3, SEQ) for i in range(4))
        gates = view(gate_buf, 0, 4, SEQ)
        v_tok = view(v_buf, 0, NT, D_MODEL)
        mq, mk = view(mqk_buf, 0, 4, SEQ), view(mqk_buf, 4 * SEQ, 4, SEQ)
        w3 = 3 * SEQ
        dist = [view(work, (4 * i + 0) * w3, w3) for i in range(2)]
        fall = [view(work, (4 * i + 1) * w3, w3) for i in range(2)]
        q_lvl = [view(work, (4 * i + 2) * w3, 3, SEQ) for i in range(2)]
        k_lvl = [view(work, (4 * i + 3) * w3, 3, SEQ) for i in range(2)]
        log_d = view(work, 0, 3, SEQ)
        st = view(st_buf, 0, LIN_HEADS, 3 * P)
        st_pair = st_buf[:, :].rearrange("p (h i c) -> p h i c", h=2, i=4)
        sq_qk = view(n_buf, 0, 2, 2 * SEQ)
        rs_qk = view(n_buf, 4 * SEQ, 2, 2 * SEQ)
        sq_lin = view(t_buf, 0, 2, 2 * SEQ)
        rs_lin = view(t_buf, 4 * SEQ, 2, 2 * SEQ)
        sig_p, sig_n, f_low = (view(st_buf, i * 2 * SEQ, 2, SEQ) for i in range(3))
        gk_z, lr_t, gk_e = (view(st_buf, (6 + i) * SEQ, SEQ) for i in range(3))
        ln_f = view(st_buf, 9 * SEQ, 2, SEQ)
        prob = [view(lin_buf, i * 2 * 3 * P, 2, 3 * P) for i in range(MOBA_HEADS // 2)]
        prob_t = [view(work, (2 + i) * 2 * 3 * P, 2, 3 * P) for i in range(2)]
        xg = view(work, 0, KC, P)
        sel = view(work, 1024, NT, P)
        selw = view(work, 1280, NT, P)
        selw_t = view(work, 1536, SEQ)
        silu_g = view(work, 1792, FC, P)
        hid = view(work, 2304, FC, P)
        hid_t = view(work, 2816, FC, P)
        y_e = view(work, 3328, D_MODEL)
        rt = view(work, 4352, 1024)

        ssq, std, rstd = small[:, 0:2], small[:, 2:4], small[:, 4:6]
        ssq_part = view(small, 8, NT, OUT_CHUNKS)
        mx4, nb4, sum4, rsum4 = ([small[:, 16 + 16 * k + 4 * i:20 + 16 * k + 4 * i] for i in range(4)] for k in range(4))
        lb_one_all, lb_ind_all = view(small, 80, DEPTH, 2), view(small, 84, DEPTH, 2)
        lbt = small[:, 88:110]
        NCOL = 2 * PAIRS * ROUNDS + 4
        pos_r = view(small, 112, NT, NCOL)
        comb_r = view(small, 112 + NT * NCOL, NT, NCOL)

        def sem(name):
            return ctx.enter_context(nc.semaphore(name))

        def signal(name, per, ahead=0):
            return Signal(sem(name), per, ahead)

        s_ident, s_cst, s_par = sem("identity_in"), sem("constants_in"), sem("params_in")
        s_x = [sem(f"x_tile{t}_in") for t in range(NT)]
        s_prep = sem("params_prepared")
        s_lb, s_lbe = sem("lower_bounds"), sem("lower_bound_exp")
        s_out = sem("out_stored")
        s_slot = [sem(f"slot{i}_in") for i in range(RING)]
        s_ssq = signal("square_sums", NT)
        s_std = signal("std", NT)
        s_xn = signal("tokens_normed", NT)
        s_tr = signal("tokens_transposed", 2 * NT)
        s_ht = signal("h_t_ready", 2 * NT)
        s_pj = signal("projected", 15)
        s_ev = signal("projection_copied", 15)
        s_sig = signal("sigmoids", 1)
        s_flow = signal("f_low_read", 1)
        s_fcl = signal("f_clamped", 1)
        s_lnf = signal("log_f", 1)
        s_gke = signal("gla_log_part", 1)
        s_dist = signal("level_distance", LEVELS)
        s_fall = signal("level_decay", LEVELS)
        s_qk = signal("level_qk", LEVELS + 1)
        s_sc = signal("level_scores", 4 * LEVELS + 4)
        s_st = signal("level_scores_taken", 4 * LEVELS)
        s_stx = signal("cross_scores_taken", 4)
        s_sq = signal("head_squares", 6)
        s_ss = signal("head_square_sums", 6)
        s_hs = signal("head_std", 6)
        s_nrm = signal("moba_normed", 4)
        s_rot = signal("moba_swapped", 4)
        s_mqk = signal("moba_qk_ready", 4)
        s_lo = signal("linear_out", 2)
        s_lmix = signal("linear_mixed", 2)
        s_ms = signal("moba_scores", 8)
        s_mm = signal("moba_max", 4)
        s_me = signal("moba_exp", 4)
        s_mp = signal("moba_probs", 4)
        s_mt = signal("moba_probs_transposed", 4)
        s_mtc = signal("moba_probs_t_copied", 4)
        s_mo = signal("moba_out", 4)
        s_moc = signal("moba_out_copied", 4)
        s_wo = signal("out_projected", OUT_CHUNKS)
        s_xa = signal("x_attended", 2 * OUT_CHUNKS)
        s_pssq = signal("part_square_sums", NT * OUT_CHUNKS)
        s_rssq = signal("router_square_sums", 1)
        s_rstd = signal("router_std", 1)
        s_rinv = signal("router_rstd", 1)
        s_xe = signal("expert_tokens_normed", 1)
        s_xt = signal("x_transposed", OUT_CHUNKS)
        s_xtc = signal("x_t_copied", OUT_CHUNKS)
        s_lg = signal("router_logits", 1)
        s_ra = signal("router_exp_in", 1)
        s_re = signal("router_exp", 1)
        s_sel1 = signal("experts_chosen", 1)
        s_pos = signal("slots_counted", 1)
        s_np = signal("pair_count", 1)
        s_vec = sem("vector_step")
        s_act = sem("scalar_step")
        m_sel = signal("selection", 1)
        m_g = signal("gathered", 2)
        m_xg = signal("gathered_copied", 2)
        m_swt = signal("selection_transposed", 1)
        m_swc = signal("selection_t_copied", 1)
        m_silu = signal("silu", 1)
        m_h = signal("hidden", 1)
        m_ht = signal("hidden_transposed", 1)
        m_htc = signal("hidden_t_copied", 1)
        m_yc = signal("down_copied", 2)
        m_z = signal("scattered", 4)
        m_xadd = signal("x_added", 4, ahead=4)
        m_free = signal("expert_chunks_used", RING, ahead=RING)

        def pcol(l, c, n=1, rows=P):
            return par_all[0:rows, l * NPAR + c:l * NPAR + c + n]

        pair_banks = {"A": slice(0, 2), "B": slice(2, 4), "C": slice(6, 8)}
        score_banks = [pair_banks[k] for k in "ABCB"]
        turn_banks = [pair_banks[k] for k in "AACA"]
        wo_bank = (2, 3, 0, 1)
        unit_bank = (0, 1, 2, 3, 0, 1, 2, 3, 0, 1, 2, 1, 0, 3, 2)
        ss_bank, rot_bank = (3, 0, 2, 3, 6, 7), (1, 2, 0, 1)
        xt_bank, lg_bank = (4, 6, 4, 6), (7, 5)

        def bc(ap, *shape):
            return ap.to_broadcast([P, *shape])

        block = ctx.enter_context(nc.Block())

        @block.sync
        def _(sp):
            for t in range(NT):
                sp.dma_start(x_tok[:, t], a["x"][0, t * P:(t + 1) * P]).then_inc(s_x[t], 16)

            def chunk_used(l, j):
                if j < len(IN_CHUNKS):
                    sp.wait_ge(s_pj.sem, s_pj.at(l, LAST_UNIT[j] + 1))
                else:
                    sp.wait_ge(s_wo.sem, s_wo.at(l, j - len(IN_CHUNKS) + 1))

            base = 0
            for l in range(DEPTH):
                for j in range(ATT_CHUNKS):
                    if j >= RING:
                        chunk_used(l, j - RING)
                    elif l > 0:
                        sp.wait_ge(m_free.sem, m_free.at(base, j + 1 - RING))
                    slot = ring[:, (j % RING) * RING_ELEMS:(j % RING + 1) * RING_ELEMS]
                    if j < len(IN_CHUNKS):
                        c0, n = IN_CHUNKS[j]
                        dst = slot[:, 0:KC * n].rearrange("p (c n) -> p c n", c=KC)
                        src = a["w_in"][l].rearrange("(p c) n -> p c n", c=KC)[:, :, c0:c0 + n]
                    else:
                        c0, n = (j - len(IN_CHUNKS)) * OUT_COLS, OUT_COLS
                        dst = slot[:, 0:KC * n].rearrange("p (c n) -> p c n", c=KC)
                        src = a["w_out"][l].rearrange("(c p) n -> p c n", c=KC)[:, :, c0:c0 + n]
                    sp.dma_start(dst, src).then_inc(s_slot[j % RING], 16)

                def load_pair(before, first=False):
                    for j in range(RING):
                        kind, half = j // 2, j % 2
                        if first:
                            chunk_used(l, ATT_CHUNKS - RING + j)
                        else:
                            sp.wait_ge(m_free.sem, m_free.at(base + before, j + 1))
                        e0 = ((before + 1) % PAIRS) * 2
                        name = ("w_exp_gate", "w_exp_up", "w_exp_down")[kind]
                        w = a[name][l][bass.ds(e0, 2)]
                        rows = KC if kind < 2 else FC
                        run = rows * (FF if kind < 2 else D_MODEL) // 2
                        src = w.rearrange("e (p c) n -> p e (c n)", p=P)[:, :, half * run:(half + 1) * run]
                        dst = ring[:, j * RING_ELEMS:(j + 1) * RING_ELEMS].rearrange("p (e r) -> p e r", e=2)
                        sp.dma_start(dst, src).then_inc(s_slot[j], 16)

                load_pair(-1, first=True)
                with sp.Fori(0, PAIRS - 1) as p:
                    load_pair(p)
                sp.wait_ge(s_np.sem, s_np.at(l, 1))
                n = sp.value_load(npairs_i[0:1, l:l + 1], min_val=PAIRS, max_val=PAIRS * ROUNDS)
                with sp.If(n > PAIRS):
                    with sp.Fori(PAIRS - 1, n - 1) as p:
                        load_pair(p)
                base = base + n
            for t in range(NT):
                sp.wait_ge(m_xadd.sem, m_xadd.at(base, 2 * t - 2))
                sp.dma_start(out[0, t * P:(t + 1) * P], x_tok[:, t]).then_inc(s_out, 16)
            sp.wait_ge(s_out, 16 * NT)

        @block.tensor
        def _(pe):
            mm = nc.tensor.matmul

            def chunk_in(l, j, base):
                pe.wait_ge(s_slot[j % RING], 16 * (2 * l + base + j // RING + 1))

            def ring_slot(j, n):
                s = j % RING
                return ring[:, s * RING_ELEMS:s * RING_ELEMS + KC * n].rearrange("p (c n) -> p c n", c=KC)

            def transpose_tokens(l):
                for t in range(NT):
                    pe.wait_ge(s_xn.sem, s_xn.at(l, t + 1))
                    for half in range(2):
                        b = t * 2 + half
                        for c in range(4):
                            last = nc.tensor.transpose(banks[:, b, c * P:(c + 1) * P], xn[:, t, half * 4 + c, :], ident)
                        s_tr.by(last)

            def project_t(u, j, f0, tiles, width=P):
                w = ring_slot(j, IN_CHUNKS[j][1])
                for i in range(tiles):
                    for c in range(KC):
                        last = mm(banks[0:width, unit_bank[u], i * SEQ:(i + 1) * SEQ], w[:, c, f0 + i * P:f0 + i * P + width],
                                  h_t[:, c, :], start=c == 0, stop=c == KC - 1)
                return last

            def project_tok(u, t_list, j, f0, n):
                w = ring_slot(j, IN_CHUNKS[j][1])
                for i, t in enumerate(t_list):
                    for c in range(KC):
                        last = mm(banks[:, unit_bank[u], i * n:(i + 1) * n], h_t[:, c, t * P:(t + 1) * P],
                                  w[:, c, f0:f0 + n], start=c == 0, stop=c == KC - 1)
                return last

            def head_rows(h):
                if h < GLA_HEADS:
                    return 0, h * GLA_DK, (h + 1) * GLA_DK
                return 1 + (h - GLA_HEADS) // 2, (h % 2) * HEAD, (h % 2 + 1) * HEAD

            def level(l, n):
                q_, k_ = (qf, kf) if n == 0 else (q_lvl[n % 2], k_lvl[n % 2])
                pe.wait_ge(s_qk.sem, s_qk.at(l, n + 1))
                if n == 0:
                    pe.wait_ge(s_ev.sem, s_ev.at(l, 5))
                if n > 0:
                    pe.wait_ge(s_st.sem, s_st.at(l, 4 * n))
                for hh in range(2):
                    for t in range(NT):
                        for i in range(4):
                            f, r0, r1 = head_rows(hh * 4 + i)
                            col = (2 * hh + t) * P
                            last = mm(banks[:, 4 + i, col:col + P], k_[r0:r1, f, t * P:(t + 1) * P],
                                      q_[r0:r1, f, t * P:(t + 1) * P], start=True, stop=True, tile_position=(r0, 0))
                            if hh == 1 and t == NT - 1:
                                s_sc.by(last)

            def cross(l):
                n = LEVELS
                pe.wait_ge(s_qk.sem, s_qk.at(l, n + 1))
                pe.wait_ge(s_st.sem, s_st.at(l, 4 * n))
                for hh in range(2):
                    for i in range(4):
                        f, r0, r1 = head_rows(hh * 4 + i)
                        last = mm(banks[:, 4 + i, hh * P:(hh + 1) * P], k_lvl[n % 2][r0:r1, f, 0:P],
                                  q_lvl[n % 2][r0:r1, f, P:2 * P], start=True, stop=True, tile_position=(r0, 0))
                        if hh == 1:
                            s_sc.by(last)

            def weighted_values(bank, i, h, v0, scores):
                r0 = (h % 2) * HEAD
                v = v_tok[:, :, v0 + h * HEAD:v0 + (h + 1) * HEAD]
                mm(banks[r0:r0 + HEAD, bank, i * SEQ:(i + 1) * SEQ], v[:, 0], scores[:, 0:SEQ],
                   start=True, stop=False, tile_position=(0, r0), skip_group_check=True)
                return mm(banks[r0:r0 + HEAD, bank, i * SEQ + P:(i + 1) * SEQ], v[:, 1], scores[:, SEQ:3 * P],
                          start=False, stop=True, tile_position=(0, r0), skip_group_check=True)

            def square_sums(l, g):
                pe.wait_ge(s_sq.sem, s_sq.at(l, g + 1))
                if g == 0:
                    pe.wait_ge(s_ev.sem, s_ev.at(l, 8))
                elif g == 1:
                    pe.wait_ge(s_ev.sem, s_ev.at(l, 9))
                elif g == 2:
                    pe.wait_ge(s_ev.sem, s_ev.at(l, 11))
                elif g == 3:
                    pe.wait_ge(s_hs.sem, s_hs.at(l, 1))
                else:
                    pe.wait_ge(s_me.sem, s_me.at(l, 3))
                src = (sq_qk if g < 4 else sq_lin)[:, g % 2]
                s_ss.by(mm(banks[:, ss_bank[g], :], head_ones, src, start=True, stop=True))

            def swap_halves(l, g):
                src = (mq, mk)[g // 2][:, (g % 2) * 2:(g % 2) * 2 + 2, :].rearrange("p a b -> p (a b)")
                pe.wait_ge(s_nrm.sem, s_nrm.at(l, g + 1))
                if g == 0:
                    pe.wait_ge(s_ev.sem, s_ev.at(l, 12))
                elif g == 1:
                    pe.wait_ge(s_hs.sem, s_hs.at(l, 3))
                elif g == 2:
                    pe.wait_ge(s_ev.sem, s_ev.at(l, 13))
                else:
                    pe.wait_ge(s_mqk.sem, s_mqk.at(l, 1))
                s_rot.by(mm(banks[:, rot_bank[g], :], swap, src, start=True, stop=True))

            def moba_scores(l, hp):
                if hp == 0:
                    pe.wait_ge(s_mqk.sem, s_mqk.at(l, 4))
                elif hp == 1:
                    pe.wait_ge(s_ev.sem, s_ev.at(l, 15))
                elif hp == 2:
                    pe.wait_ge(s_stx.sem, s_stx.at(l, 4))
                else:
                    pe.wait_ge(s_me.sem, s_me.at(l, 2))
                for i in range(2):
                    r0 = i * HEAD
                    q_, k_ = mq[r0:r0 + HEAD, hp, :], mk[r0:r0 + HEAD, hp, :]
                    bank = score_banks[hp].start + i
                    mm(banks[:, bank, 0:P], q_[:, 0:P], k_[:, 0:P], start=True, stop=True, tile_position=(r0, 0))
                    s_ms.by(mm(banks[:, bank, P:3 * P], q_[:, P:SEQ], k_[:, 0:SEQ], start=True, stop=True,
                               tile_position=(r0, 0)))

            def moba_transpose(l, hp):
                pe.wait_ge(s_mp.sem, s_mp.at(l, hp + 1))
                if hp == 1:
                    pe.wait_ge(s_mtc.sem, s_mtc.at(l, 1))
                elif hp == 2:
                    pe.wait_ge(s_hs.sem, s_hs.at(l, 6))
                elif hp == 3:
                    pe.wait_ge(s_mtc.sem, s_mtc.at(l, 2))
                for i in range(2):
                    for k in range(3):
                        last = nc.tensor.transpose(banks[:, turn_banks[hp].start + i, k * P:(k + 1) * P],
                                                   prob[hp][:, i, k * P:(k + 1) * P], ident)
                s_mt.by(last)

            def moba_values(l, hp):
                pe.wait_ge(s_mtc.sem, s_mtc.at(l, hp + 1))
                if hp < 2:
                    pe.wait_ge(s_lmix.sem, s_lmix.at(l, hp + 1))
                else:
                    pe.wait_ge(s_moc.sem, s_moc.at(l, hp - 1))
                for i in range(2):
                    last = weighted_values(4 + hp % 2, 0, 2 * hp + i, 512, prob_t[hp % 2][:, i, :])
                s_mo.by(last)

            def project_out(j, t, chunks):
                w = ring_slot(len(IN_CHUNKS) + j, OUT_COLS)
                for c in chunks:
                    last = mm(banks[:, wo_bank[j], t * OUT_COLS:(t + 1) * OUT_COLS], mix_t[:, c, t * P:(t + 1) * P],
                              w[:, c, :], start=c == lin_c[0], stop=c == moba_c[-1])
                return last

            def turn_x(l, j):
                pe.wait_ge(s_xa.sem, s_xa.at(l, NT * (j + 1)))
                if j >= 2:
                    pe.wait_ge(s_xtc.sem, s_xtc.at(l, j - 1))
                for i in range(2):
                    for t in range(NT):
                        c0 = (2 * j + i) * P
                        last = nc.tensor.transpose(banks[:, xt_bank[j], (i * NT + t) * P:(i * NT + t + 1) * P],
                                                   x_tok[:, t, c0:c0 + P], ident)
                s_xt.by(last)

            def router_logits(l, j):
                pe.wait_ge(s_xtc.sem, s_xtc.at(l, j + 1))
                wr = pcol(l, P_WR, KC * NR).rearrange("p (c n) -> p c n", n=NR)
                for c in (2 * j, 2 * j + 1):
                    for t in range(NT):
                        last = mm(banks[:, lg_bank[t], 0:NR], h_t[:, c, t * P:(t + 1) * P], wr[:, c, :],
                                  start=c == 0, stop=c == KC - 1)
                return last

            lin_c, moba_c = (0, 1, 6, 7), (2, 3, 4, 5)
            pe.wait_ge(s_ident, 16)
            base = 0
            for l in range(DEPTH):
                transpose_tokens(l)
                pe.wait_ge(s_ht.sem, s_ht.at(l, 4))
                units = [
                    (0, lambda u: project_t(u, 0, 0, 2)),
                    (0, lambda u: project_t(u, 0, 256, 2)),
                    (1, lambda u: project_t(u, 1, 256, 1, LOWRANK)),
                    (1, lambda u: project_t(u, 1, 0, 2)),
                    (2, lambda u: project_t(u, 2, 0, 2)),
                    (None, lambda u: mm(banks[:, unit_bank[u], 0:SEQ], pcol(l, P_W2, P, LOWRANK), lr_t[0:LOWRANK, :],
                                        start=True, stop=True)),
                    (3, lambda u: project_t(u, 3, 0, 2)),
                    (3, lambda u: project_t(u, 3, 256, 2)),
                    (4, lambda u: project_t(u, 4, 0, 2)),
                    (4, lambda u: project_t(u, 4, 256, 2)),
                    (5, lambda u: project_tok(u, (0, 1), 5, 0, 256)),
                    (6, lambda u: project_tok(u, (0, 1), 6, 0, 256)),
                    (6, lambda u: project_t(u, 6, 256, 2)),
                    (7, lambda u: project_tok(u, (0,), 7, 0, 512)),
                    (7, lambda u: project_tok(u, (1,), 7, 0, 512)),
                ]

                def project(u):
                    j, work_of = units[u]
                    if j is not None and (u == 0 or units[u - 1][0] != j):
                        chunk_in(l, j, base)
                    if 4 <= u < 11:
                        pe.wait_ge(s_ev.sem, s_ev.at(l, u - 3))
                    if u == 5:
                        pe.wait_ge(s_flow.sem, s_flow.at(l, 1))
                        pe.wait_ge(s_ev.sem, s_ev.at(l, 3))
                        pe.wait_ge(s_par, 16)
                    if u == 11:
                        pe.wait_ge(s_ev.sem, s_ev.at(l, 10))
                    if u == 12:
                        pe.wait_ge(s_hs.sem, s_hs.at(l, 2))
                    if u == 13:
                        pe.wait_ge(s_hs.sem, s_hs.at(l, 4))
                    if u == 14:
                        pe.wait_ge(s_mqk.sem, s_mqk.at(l, 2))
                    last = work_of(u)
                    s_pj.by(last)

                for u in range(6):
                    project(u)
                level(l, 0)
                project(6)
                project(7)
                level(l, 1)
                project(8)
                level(l, 2)
                project(9)
                level(l, 3)
                project(10)
                if l == 0:
                    pe.wait_ge(s_cst, 16)
                square_sums(l, 0)
                level(l, 4)
                square_sums(l, 1)
                project(11)
                square_sums(l, 2)
                level(l, 5)
                square_sums(l, 3)
                project(12)
                swap_halves(l, 0)
                level(l, 6)
                swap_halves(l, 1)
                project(13)
                swap_halves(l, 2)
                level(l, 7)
                swap_halves(l, 3)
                cross(l)
                project(14)
                for hp in range(3):
                    moba_scores(l, hp)
                pe.wait_ge(s_stx.sem, s_stx.at(l, 4))
                pe.wait_ge(s_st.sem, s_st.at(l, 4 * LEVELS))
                for g in range(2):
                    for i in range(2):
                        for hh in range(2):
                            h = 4 * g + 2 * i + hh
                            last = weighted_values(4 + g, i, h, 0, st[:, h, :])
                    s_lo.by(last)
                moba_transpose(l, 0)
                moba_scores(l, 3)
                square_sums(l, 4)
                square_sums(l, 5)
                moba_transpose(l, 1)
                moba_values(l, 0)
                moba_transpose(l, 2)
                moba_values(l, 1)
                moba_transpose(l, 3)
                chunk_in(l, len(IN_CHUNKS), base)
                pe.wait_ge(s_me.sem, s_me.at(l, 4))
                project_out(0, 0, lin_c)
                moba_values(l, 2)
                chunk_in(l, len(IN_CHUNKS) + 1, base)
                project_out(1, 0, lin_c)
                moba_values(l, 3)
                pe.wait_ge(s_moc.sem, s_moc.at(l, 4))
                for j in range(OUT_CHUNKS):
                    if j >= 2:
                        chunk_in(l, len(IN_CHUNKS) + j, base)
                    for t in range(NT):
                        last = project_out(j, t, moba_c if j < 2 and t == 0 else lin_c + moba_c)
                    s_wo.by(last)
                    if j >= 1:
                        turn_x(l, j - 1)
                if l == 0:
                    pe.wait_ge(s_prep, 1)
                for j in range(OUT_CHUNKS - 1):
                    router_logits(l, j)
                turn_x(l, OUT_CHUNKS - 1)
                s_lg.by(router_logits(l, OUT_CHUNKS - 1))
                pe.wait_ge(s_sel1.sem, s_sel1.at(l, 1))
                chosen = rt[:, 0:NT * EXPERTS].rearrange("p (t e) -> p t e", t=NT)
                mm(banks[:, 5, 0:16], before, chosen[:, 0], start=True, stop=True)
                mm(banks[:, 5, 16:32], all_ones, chosen[:, 0], start=True, stop=False)
                mm(banks[:, 5, 16:32], before, chosen[:, 1], start=False, stop=True)
                mm(banks[:, 5, 32:48], all_ones, chosen[:, 0], start=True, stop=False)
                s_pos.by(mm(banks[:, 5, 32:48], all_ones, chosen[:, 1], start=False, stop=True))

                def gather(half):
                    for c in range(4 * half, 4 * half + 4):
                        for t in range(NT):
                            last = mm(banks[:, half, (c % 4) * P:(c % 4 + 1) * P], xn[:, t, c, :], sel[:, t, :],
                                      start=t == 0, stop=t == NT - 1)
                    m_g.by(last)

                def turn_selection():
                    for t in range(NT):
                        last = nc.tensor.transpose(banks[:, 4, t * P:(t + 1) * P], selw[:, t, :], ident)
                    m_swt.by(last)

                pe.wait_ge(s_np.sem, s_np.at(l, 1))
                n_pairs = pe.value_load(npairs_i[0:1, l:l + 1], min_val=PAIRS, max_val=PAIRS * ROUNDS)
                pe.wait_ge(m_sel.sem, m_sel.at(base, l + 1))
                pe.wait_ge(s_xe.sem, s_xe.at(l, 1))
                gather(0)
                gather(1)
                turn_selection()
                with pe.Fori(0, n_pairs) as p:
                    it = base + p
                    pe.wait_ge(m_xg.sem, m_xg.at(it + l, 2))
                    for kind, bank in ((0, 3), (1, 4)):
                        if kind == 1:
                            pe.wait_ge(m_swc.sem, m_swc.at(it + l, 1))
                        for half in range(2):
                            j = 2 * kind + half
                            pe.wait_ge(s_slot[j], 16 * (2 * (l + 1) + 1 + it))
                            w = ring[:, j * RING_ELEMS:(j + 1) * RING_ELEMS].rearrange("p (e c n) -> p e c n", e=2, n=FF)
                            for c in range(4):
                                for e in range(2):
                                    r0 = e * SLOTS
                                    k = half * 4 + c
                                    last = mm(banks[r0:r0 + SLOTS, bank, :], xg[:, k, r0:r0 + SLOTS], w[:, e, c, :],
                                              start=k == 0, stop=k == KC - 1, tile_position=(0, r0), skip_group_check=True)
                            m_free.by(last)
                    pe.wait_ge(m_sel.sem, m_sel.at(it + l, 2))
                    gather(0)
                    pe.wait_ge(m_h.sem, m_h.at(it, 1))
                    for c in range(FC):
                        last = nc.tensor.transpose(banks[:, 3, c * P:(c + 1) * P], hid[:, c, :], ident)
                    m_ht.by(last)
                    turn_selection()
                    pe.wait_ge(m_htc.sem, m_htc.at(it, 1))
                    for half in range(2):
                        j = 4 + half
                        pe.wait_ge(s_slot[j], 16 * (2 * (l + 1) + 1 + it))
                        w = ring[:, j * RING_ELEMS:(j + 1) * RING_ELEMS].rearrange("p (e c n) -> p e c n", e=2, n=D_MODEL)
                        for c in range(2):
                            for nh in range(2):
                                for e in range(2):
                                    r0 = e * SLOTS
                                    k = half * 2 + c
                                    last = mm(banks[r0:r0 + SLOTS, 5 + nh, :], hid_t[:, k, r0:r0 + SLOTS],
                                              w[:, e, c, nh * 512:(nh + 1) * 512], start=k == 0, stop=k == FC - 1,
                                              tile_position=(0, r0), skip_group_check=True)
                        m_free.by(last)
                    gather(1)
                    for i in range(4):
                        t, nh = i // 2, i % 2
                        bank = (7, 2)[i % 2]
                        pe.wait_ge(m_yc.sem, m_yc.at(it, 2))
                        pe.wait_ge(m_xadd.sem, m_xadd.at(it, i - 1))
                        m_z.by(mm(banks[:, bank, :], selw_t[:, t * P:(t + 1) * P], y_e[:, nh * 512:(nh + 1) * 512],
                                  start=True, stop=True))
                base = base + n_pairs

        @block.scalar
        def _(act):
            fn = nc.scalar.activation
            steps = [0]

            def link(ins):
                steps[0] += 1
                ins.then_inc(s_act, 1)
                act.wait_ge(s_act, steps[0])

            def token_std(l, base):
                for t in range(NT):
                    if l == 0:
                        act.wait_ge(s_x[t], 16)
                    act.wait_ge(m_xadd.sem, m_xadd.at(base, 2 * t - 2))
                    s_ssq.by(fn(n_buf[:, t * D_MODEL:(t + 1) * D_MODEL], x_tok[:, t, :], ACT.Square, accum_out=ssq[:, t:t + 1]))
                    act.wait_ge(s_ssq.sem, s_ssq.at(l, t + 1))
                    if l == 0 and t == 0:
                        act.wait_ge(s_par, 16)
                    s_std.by(fn(std[:, t:t + 1], ssq[:, t:t + 1], ACT.Sqrt, bias=eps, scale=1.0 / D_MODEL))

            def bank2(b):
                return banks[:, b, :].rearrange("p (a b) -> p a b", a=2)

            act.dma_start(cst[:, 0:EARLY], a["consts"][:, 0:EARLY]).then_inc(s_ident, 16)
            act.dma_start(par_all[:, :], a["params"]).then_inc(s_par, 16)
            act.dma_start(cst[:, EARLY:], a["consts"][:, EARLY:]).then_inc(s_cst, 16)
            act.wait_ge(s_ident, 16)
            base = 0
            for l in range(DEPTH):
                token_std(l, base)
                if l == 0:
                    act.wait_ge(s_lb, 1)
                    fn(lbt[:, 0:2 * DEPTH], lbt[:, 0:2 * DEPTH], ACT.Exp).then_inc(s_lbe, 1)

                def copy_unit(u):
                    b = unit_bank[u]
                    act.wait_ge(s_pj.sem, s_pj.at(l, u + 1))
                    if u == 0:
                        last = fn(qf[:, 1:3, :], bank2(b), ACT.Silu)
                    elif u == 1:
                        fn(sig_p, bank2(b), ACT.Sigmoid)
                        last = fn(sig_n, bank2(b), ACT.Sigmoid, scale=-1.0)
                    elif u == 2:
                        last = fn(lr_t[0:LOWRANK, :], banks[0:LOWRANK, b, 0:SEQ], ACT.Copy)
                    elif u == 3:
                        last = fn(gates[:, 0:2, :], bank2(b), ACT.Silu)
                    elif u == 4:
                        fn(qf[:, 0, :], banks[:, b, 0:SEQ], ACT.Copy, scale=float(GLA_DK) ** -0.5)
                        last = fn(kf[:, 0, :], banks[:, b, SEQ:2 * SEQ], ACT.Copy)
                    elif u == 5:
                        last = fn(gk_z, banks[:, b, 0:SEQ], ACT.Identity, bias=pcol(l, P_GKB))
                    elif u < 10:
                        dst, i = ((mq, 0), (mq, 2), (mk, 0), (mk, 2))[u - 6]
                        last = fn(dst[:, i:i + 2, :], bank2(b), ACT.Copy)
                    elif u == 10:
                        last = fn(v_tok[:, :, 0:256], bank2(b), ACT.Copy)
                    elif u == 11:
                        last = fn(v_tok[:, :, 256:512], bank2(b), ACT.Copy)
                    elif u == 12:
                        last = fn(gates[:, 2:4, :], bank2(b), ACT.Silu)
                    else:
                        last = fn(v_tok[:, u - 13, 512:1024], banks[:, b, :], ACT.Copy)
                    s_ev.by(last)

                def level_decay(n):
                    act.wait_ge(s_dist.sem, s_dist.at(l, n))
                    link(fn(dist[n % 2], dist[n % 2], ACT.Abs))
                    s_fall.by(fn(fall[n % 2], dist[n % 2], ACT.Exp, scale=-1.0))

                def square_qk(g):
                    if g >= 2:
                        act.wait_ge(s_ss.sem, s_ss.at(l, g - 1))
                    act.wait_ge(s_ev.sem, s_ev.at(l, 7 + g))
                    src = (mq, mk)[g // 2][:, (g % 2) * 2:(g % 2) * 2 + 2, :].rearrange("p a b -> p (a b)")
                    s_sq.by(fn(sq_qk[:, g % 2], src, ACT.Square))

                def head_std(g):
                    act.wait_ge(s_ss.sem, s_ss.at(l, g + 1))
                    if g in (2, 3):
                        act.wait_ge(s_nrm.sem, s_nrm.at(l, g - 1))
                    dst = (rs_qk if g < 4 else rs_lin)[:, g % 2]
                    s_hs.by(fn(dst, banks[:, ss_bank[g], :], ACT.Sqrt, bias=eps, scale=1.0 / HEAD))

                for u in range(6):
                    copy_unit(u)
                act.wait_ge(s_ev.sem, s_ev.at(l, 6))
                link(fn(gk_e, gk_z, ACT.Abs))
                link(fn(gk_e, gk_e, ACT.Exp, scale=-1.0))
                s_gke.by(fn(gk_e, gk_e, ACT.Ln, bias=one))
                act.wait_ge(s_fcl.sem, s_fcl.at(l, 1))
                s_lnf.by(fn(ln_f, sig_p, ACT.Ln))
                for u in range(6, 10):
                    copy_unit(u)
                    if u < 9:
                        level_decay(u - 5)
                square_qk(0)
                square_qk(1)
                level_decay(4)
                copy_unit(10)
                head_std(0)
                level_decay(5)
                square_qk(2)
                head_std(1)
                square_qk(3)
                copy_unit(11)
                head_std(2)
                level_decay(6)
                head_std(3)
                copy_unit(12)
                level_decay(7)
                copy_unit(13)
                level_decay(8)
                for i in range(4):
                    act.wait_ge(s_sc.sem, s_sc.at(l, 4 * LEVELS + i + 1))
                    src = banks[:, 4 + i, 0:2 * P].rearrange("p (h i) -> p h i", h=2)
                    s_stx.by(fn(st_pair[:, :, i, P:2 * P], src, ACT.Copy))
                copy_unit(14)

                def moba_exp(hp):
                    act.wait_ge(s_mm.sem, s_mm.at(l, hp + 1))
                    for i in range(2):
                        bank = score_banks[hp].start + i
                        for qt in range(2):
                            c = 2 * i + qt
                            cols = slice(0, P) if qt == 0 else slice(P, 3 * P)
                            last = fn(prob[hp][:, i, cols], banks[:, bank, cols], ACT.Exp, bias=nb4[hp][:, c:c + 1],
                                      scale=HEAD ** -0.5, accum_out=sum4[hp][:, c:c + 1])
                    s_me.by(last)

                def copy_turned(hp):
                    act.wait_ge(s_mt.sem, s_mt.at(l, hp + 1))
                    if hp >= 2:
                        act.wait_ge(s_mo.sem, s_mo.at(l, hp - 1))
                    s_mtc.by(fn(prob_t[hp % 2], banks[:, turn_banks[hp], 0:3 * P], ACT.Copy))

                def copy_mixed(hp):
                    act.wait_ge(s_mo.sem, s_mo.at(l, hp + 1))
                    s_moc.by(fn(mix_t[:, 2 + hp, :], banks[:, 4 + hp % 2, 0:SEQ], ACT.Copy))

                for hp in range(3):
                    moba_exp(hp)
                for g in range(2):
                    act.wait_ge(s_lo.sem, s_lo.at(l, g + 1))
                    s_sq.by(fn(sq_lin[:, g], banks[:, 4 + g, :], ACT.Square))
                copy_turned(0)
                moba_exp(3)
                head_std(4)
                head_std(5)
                copy_turned(1)
                for hp in range(2, 4):
                    copy_mixed(hp - 2)
                    copy_turned(hp)
                copy_mixed(2)
                copy_mixed(3)

                for j in range(OUT_CHUNKS):
                    for t in range(NT):
                        act.wait_ge(s_xa.sem, s_xa.at(l, NT * j + t + 1))
                        junk = work[:, (NT * j + t) * OUT_COLS:(NT * j + t + 1) * OUT_COLS]
                        s_pssq.by(fn(junk, x_tok[:, t, j * OUT_COLS:(j + 1) * OUT_COLS], ACT.Square,
                                     accum_out=ssq_part[:, t, j:j + 1]))
                    act.wait_ge(s_xt.sem, s_xt.at(l, j + 1))
                    s_xtc.by(fn(h_t[:, 2 * j:2 * j + 2, :], banks[:, xt_bank[j], :].rearrange("p (c t) -> p c t", c=2), ACT.Copy))
                act.wait_ge(s_rssq.sem, s_rssq.at(l, 1))
                s_rstd.by(fn(std, ssq, ACT.Sqrt, bias=eps, scale=1.0 / D_MODEL))
                act.wait_ge(s_rinv.sem, s_rinv.at(l, 1))
                for t in range(NT):
                    last = fn(xn[:, t], x_tok[:, t].rearrange("p (q c) -> p c q", c=KC), ACT.Copy, scale=rstd[:, t:t + 1])
                s_xe.by(last)
                act.wait_ge(s_ra.sem, s_ra.at(l, 1))
                s_re.by(fn(rt[:, R_EXP:R_EXP + 10], rt[:, R_EXP:R_EXP + 10], ACT.Exp))

                act.wait_ge(s_np.sem, s_np.at(l, 1))
                n_pairs = act.value_load(npairs_i[0:1, l:l + 1], min_val=PAIRS, max_val=PAIRS * ROUNDS)

                def copy_selection(i):
                    act.wait_ge(m_swt.sem, i)
                    m_swc.by(fn(selw_t, banks[:, 4, 0:SEQ], ACT.Copy))

                copy_selection(m_swt.at(base + l, 1))
                with act.Fori(0, n_pairs) as p:
                    it = base + p
                    act.wait_ge(m_free.sem, m_free.at(it, 2))
                    m_silu.by(fn(silu_g, banks[:, 3, :].rearrange("s (p c) -> s c p", c=FC), ACT.Silu))
                    act.wait_ge(m_ht.sem, m_ht.at(it, 1))
                    m_htc.by(fn(hid_t, banks[:, 3, :].rearrange("p (c s) -> p c s", c=FC), ACT.Copy))
                    act.wait_ge(m_free.sem, m_free.at(it, RING))
                    for nh in range(2):
                        m_yc.by(fn(y_e[:, nh * 512:(nh + 1) * 512], banks[:, 5 + nh, :], ACT.Copy))
                    act.wait_ge(m_z.sem, m_z.at(it, 4))
                    copy_selection(m_swt.at(it + l, 2))
                base = base + n_pairs

        @block.vector
        def _(dve):
            v = nc.vector
            steps = [0]

            def link(ins):
                steps[0] += 1
                ins.then_inc(s_vec, 1)
                dve.wait_ge(s_vec, steps[0])

            def pc(c, n=1):
                return pcol(l, c, n)

            v.memset(small[:, 0:320], 0.0).then_inc(m_xadd.sem, m_xadd.ahead)
            v.memset(small[:, 320:640], 0.0).then_inc(m_free.sem, m_free.ahead)
            dve.wait_ge(m_xadd.sem, m_xadd.ahead)
            dve.wait_ge(m_free.sem, m_free.ahead)
            def prepare_params():
                lb_cols = [pcol(k, P_LB, 2) for k in range(DEPTH)]
                top, tot, part = lbt[:, 16:18], lbt[:, 18:20], lbt[:, 20:22]
                link(v.tensor_copy(top, lb_cols[0]))
                for k in range(1, DEPTH):
                    link(v.tensor_tensor(top, top, lb_cols[k], ALU.max))
                for k in range(DEPTH):
                    last = v.tensor_tensor(lbt[:, 2 * k:2 * k + 2], lb_cols[k], top, ALU.subtract)
                last.then_inc(s_lb, 1)
                dve.wait_ge(s_lbe, 1)
                link(v.tensor_copy(tot, lbt[:, 0:2]))
                for k in range(1, DEPTH):
                    link(v.tensor_tensor(tot, tot, lbt[:, 2 * k:2 * k + 2], ALU.add))
                link(v.reciprocal(tot, tot))
                for k in range(DEPTH):
                    link(v.tensor_tensor(lbt[:, 2 * k:2 * k + 2], lbt[:, 2 * k:2 * k + 2], tot, ALU.mult))
                link(v.tensor_copy(part, lbt[:, 0:2]))
                for k in range(DEPTH):
                    if k > 0:
                        link(v.tensor_tensor(part, part, lbt[:, 2 * k:2 * k + 2], ALU.add))
                    link(v.tensor_tensor(lb_cols[k], part, lbt[:, 0:2], ALU.subtract))
                    v.tensor_scalar(lb_one_all[:, k], lb_cols[k], -1.0, 1.0, ALU.mult, ALU.add)
                    v.tensor_scalar(lb_ind_all[:, k], lb_cols[k], F_MIN, None, ALU.is_lt)
                    wr = pcol(k, P_WR, KC * NR).rearrange("p (c n) -> p c n", n=NR)
                    last = v.tensor_tensor(wr, wr, bc(pcol(k, PG_ROUTER, KC).unsqueeze(2), KC, NR), ALU.mult)
                last.then_inc(s_prep, 1)
                dve.wait_ge(s_prep, 1)

            base = 0
            for l in range(DEPTH):
                lb, lb_one, lb_ind = pc(P_LB, 2), lb_one_all[:, l], lb_ind_all[:, l]

                for t in range(NT):
                    r = rstd[:, t:t + 1]
                    dve.wait_ge(s_std.sem, s_std.at(l, t + 1))
                    link(v.reciprocal(r, std[:, t:t + 1]))
                    s_xn.by(v.tensor_scalar(xn[:, t], x_tok[:, t].rearrange("p (q c) -> p c q", c=KC), r, None, ALU.mult))
                if l == 0:
                    dve.wait_ge(s_par, 16)
                for t in range(NT):
                    for half in range(2):
                        b = 2 * t + half
                        dve.wait_ge(s_tr.sem, s_tr.at(l, b + 1))
                        g = pc(PG_ATT + 4 * half, 4).unsqueeze(2)
                        s_ht.by(v.tensor_tensor(h_t[:, half * 4:half * 4 + 4, t * P:(t + 1) * P],
                                                banks[:, b, :].rearrange("p (c t) -> p c t", c=4), bc(g, 4, P), ALU.mult))
                if l == 0:
                    prepare_params()
                    dve.wait_ge(s_cst, 16)
                dve.wait_ge(s_ev.sem, s_ev.at(l, 2))
                bank1 = banks[:, 1, :].rearrange("p (a b) -> p a b", a=2)
                s_flow.by(v.tensor_scalar(f_low, bank1, -LN_F_MIN, 0.0, ALU.add, ALU.min))
                for f in range(2):
                    link(v.tensor_scalar(sig_p[:, f, :], sig_p[:, f, :], lb_one[:, f:f + 1], lb[:, f:f + 1], ALU.mult, ALU.add))
                s_fcl.by(v.tensor_scalar(sig_p, sig_p, F_MIN, None, ALU.max))
                for f in range(2):
                    last = v.tensor_scalar(kf[:, 1 + f, :], sig_n[:, f, :], lb_one[:, f:f + 1], None, ALU.mult)
                s_qk.by(last)
                dve.wait_ge(s_gke.sem, s_gke.at(l, 1))
                link(v.scalar_tensor_tensor(log_d[:, 0, :], gk_z, 0.0, gk_e, ALU.min, ALU.subtract))
                link(v.tensor_scalar(log_d[:, 0, :], log_d[:, 0, :], 1.0 / GLA_TAU, None, ALU.mult))
                dve.wait_ge(s_lnf.sem, s_lnf.at(l, 1))
                dve.wait_ge(s_flow.sem, s_flow.at(l, 1))
                for f in range(2):
                    link(v.scalar_tensor_tensor(log_d[:, 1 + f, :], f_low[:, f, :], lb_ind[:, f:f + 1], ln_f[:, f, :],
                                                ALU.mult, ALU.add))
                for f in range(3):
                    link(v.tensor_tensor_scan(b_chunk[:, f, :], const("chunk_keep"), log_d[:, f, :], 0.0, ALU.mult, ALU.add))
                    link(v.tensor_tensor_scan(b_full[:, f, :], const("ones_row"), log_d[:, f, :], 0.0, ALU.mult, ALU.add))

                def level_distance(n):
                    s = 1 << (n - 1)
                    b = (b_chunk if 2 * s <= LIN_CHUNK else b_full).rearrange("p f (k w) -> p (f k) w", w=2 * s)
                    o = dist[n % 2].rearrange("p (k w) -> p k w", w=2 * s)
                    s_dist.by(v.tensor_tensor(o, b, bc(b[:, :, s - 1:s], 3 * SEQ // (2 * s), 2 * s), ALU.subtract))

                def level_scale(n):
                    dve.wait_ge(s_fall.sem, s_fall.at(l, n))
                    f = fall[n % 2].rearrange("p (f t) -> p f t", f=3)
                    v.tensor_tensor(q_lvl[n % 2], qf, f, ALU.mult)
                    s_qk.by(v.tensor_tensor(k_lvl[n % 2], kf, f, ALU.mult))

                def take_scores(n):
                    mask = masks[:, n:n + 1, :].unsqueeze(1)
                    for i in range(4):
                        dve.wait_ge(s_sc.sem, s_sc.at(l, 4 * n + i + 1))
                        src = banks[:, 4 + i, :].rearrange("p (h t i) -> p h t i", h=2, t=NT)
                        dst = st_pair[:, :, i, :].rearrange("p h (k c) -> p h k c", k=3)[:, :, 0:3:2, :]
                        if n == 0:
                            s_st.by(v.tensor_tensor(dst, src, bc(mask, 2, NT, P), ALU.mult))
                        else:
                            dve.wait_ge(s_st.sem, s_st.at(l, 4 * (n - 1) + i + 1))
                            s_st.by(v.copy_predicated(dst, bc(mask.bitcast(U32), 2, NT, P), src))

                def moba_norm(g):
                    dve.wait_ge(s_hs.sem, s_hs.at(l, g + 1))
                    link(v.reciprocal(rs_qk[:, g % 2], rs_qk[:, g % 2]))
                    m = (mq, mk)[g // 2][:, (g % 2) * 2:(g % 2) * 2 + 2, :].rearrange("p a b -> p (a b)")
                    s_nrm.by(v.scalar_tensor_tensor(m, m, pc(P_QN + g // 2), rs_qk[:, g % 2], ALU.mult, ALU.mult))

                def moba_rotate(g):
                    m = (mq, mk)[g // 2][:, (g % 2) * 2:(g % 2) * 2 + 2, :]
                    turned = sq_qk[:, g % 2].rearrange("p (a b) -> p a b", a=2)
                    dve.wait_ge(s_rot.sem, s_rot.at(l, g + 1))
                    v.tensor_tensor(turned, banks[:, rot_bank[g], :].rearrange("p (a b) -> p a b", a=2),
                                    bc(sin.unsqueeze(1), 2, SEQ), ALU.mult)
                    link(v.tensor_tensor(m, m, bc(cos.unsqueeze(1), 2, SEQ), ALU.mult))
                    s_mqk.by(v.tensor_tensor(m, m, turned, ALU.add))
                    dve.wait_ge(s_mqk.sem, s_mqk.at(l, g + 1))

                def level_step(n):
                    level_distance(n)
                    level_scale(n - 1)
                    take_scores(n - 2)

                level_distance(1)
                level_distance(2)
                level_scale(1)
                take_scores(0)
                for n in range(3, 6):
                    level_step(n)
                moba_norm(0)
                level_step(6)
                moba_norm(1)
                moba_norm(2)
                level_step(7)
                moba_norm(3)
                moba_rotate(0)
                level_step(8)
                moba_rotate(1)
                moba_rotate(2)
                level_scale(LEVELS)
                take_scores(LEVELS - 1)
                moba_rotate(3)

                def moba_max(hp):
                    dve.wait_ge(s_ms.sem, s_ms.at(l, 2 * hp + 2))
                    first = banks[:, score_banks[hp], 0:P]
                    second = banks[:, score_banks[hp], P:3 * P]
                    mask = bc(causal.unsqueeze(1), 2, P)
                    v.tensor_tensor(first, first, mask, ALU.add)
                    link(v.tensor_tensor(second[:, :, P:SEQ], second[:, :, P:SEQ], mask, ALU.add))
                    m = mx4[hp].rearrange("p (i q) -> p i q", i=2)
                    v.tensor_reduce(m[:, :, 0:1], first, AX.X, ALU.max)
                    link(v.tensor_reduce(m[:, :, 1:2], second, AX.X, ALU.max))
                    s_mm.by(v.tensor_scalar(nb4[hp], mx4[hp], -(HEAD ** -0.5), None, ALU.mult))

                def moba_normalise(hp):
                    dve.wait_ge(s_me.sem, s_me.at(l, hp + 1))
                    link(v.reciprocal(rsum4[hp], sum4[hp]))
                    r = rsum4[hp].rearrange("p (i q) -> p i q", i=2)
                    v.tensor_tensor(prob[hp][:, :, 0:P], prob[hp][:, :, 0:P], bc(r[:, :, 0:1], 2, P), ALU.mult)
                    s_mp.by(v.tensor_tensor(prob[hp][:, :, P:3 * P], prob[hp][:, :, P:3 * P], bc(r[:, :, 1:2], 2, 2 * P), ALU.mult))

                def linear_mix(g):
                    tmp = dist[1][:, 0:2 * SEQ]
                    dve.wait_ge(s_hs.sem, s_hs.at(l, 5 + g))
                    link(v.reciprocal(rs_lin[:, g], rs_lin[:, g]))
                    link(v.scalar_tensor_tensor(tmp, banks[:, 4 + g, :], pc((P_GLA, P_HGRN)[g]), rs_lin[:, g], ALU.mult, ALU.mult))
                    dst = mix_t[:, 6 * g:6 * g + 2, :]
                    s_lmix.by(v.tensor_tensor(dst, tmp.rearrange("p (a b) -> p a b", a=2), gates[:, 2 * g:2 * g + 2, :], ALU.mult))
                    dve.wait_ge(s_lmix.sem, s_lmix.at(l, g + 1))

                moba_max(0)
                moba_max(1)
                moba_normalise(0)
                moba_max(2)
                moba_normalise(1)
                moba_max(3)
                linear_mix(0)
                moba_normalise(2)
                linear_mix(1)
                moba_normalise(3)
                for j in range(OUT_CHUNKS):
                    dve.wait_ge(s_wo.sem, s_wo.at(l, j + 1))
                    for t in range(NT):
                        xs = x_tok[:, t, j * OUT_COLS:(j + 1) * OUT_COLS]
                        s_xa.by(v.tensor_tensor(xs, xs, banks[:, wo_bank[j], t * OUT_COLS:(t + 1) * OUT_COLS], ALU.add))

                dve.wait_ge(s_pssq.sem, s_pssq.at(l, NT * OUT_CHUNKS))
                s_rssq.by(v.tensor_reduce(ssq.unsqueeze(2), ssq_part, AX.X, ALU.add))
                dve.wait_ge(s_rstd.sem, s_rstd.at(l, 1))
                s_rinv.by(v.reciprocal(rstd, std))
                dve.wait_ge(s_rinv.sem, s_rinv.at(l, 1))
                NE = EXPERTS
                chosen = view(rt, 0, NT, NE)
                logits = view(rt, 32, NT, NR)
                lg, le = logits[:, :, 0:GROUPS], logits[:, :, GROUPS:NR]
                eg, goh = view(rt, 80, NT, GROUPS), view(rt, 96, NT, GROUPS)
                ee, oh1, oh2, lem = (view(rt, 128 + 32 * i, NT, NE) for i in range(4))
                lem2, comb, slots_ = (view(rt, 256 + 32 * i, NT, NE) for i in range(3))
                one2 = [view(rt, 384 + 2 * i, NT, 1) for i in range(8)]
                gmax, vm, m1, m2, gg, w1, w2, den = one2
                ex_g = view(rt, R_EXP, NT, GROUPS)
                ex_e = view(rt, R_EXP + NT * GROUPS, NT, 1)
                rank = const("rank").unsqueeze(1)

                def first_max(vals, top, hot, scratch, n):
                    link(v.tensor_reduce(top, vals, AX.X, ALU.max))
                    link(v.tensor_tensor(scratch, vals, bc(top, NT, n), ALU.is_equal))
                    link(v.tensor_tensor(scratch, scratch, bc(rank[:, :, 0:n], NT, n), ALU.mult))
                    link(v.tensor_reduce(vm, scratch, AX.X, ALU.max))
                    link(v.tensor_tensor(hot, scratch, bc(vm, NT, n), ALU.is_equal))

                dve.wait_ge(s_lg.sem, s_lg.at(l, 1))
                for t in range(NT):
                    link(v.tensor_scalar(logits[:, t], banks[:, lg_bank[t], 0:NR], rstd[:, t:t + 1], None, ALU.mult))
                first_max(lg, gmax, goh, eg, GROUPS)
                link(v.tensor_tensor(ex_g, lg, bc(gmax, NT, GROUPS), ALU.subtract))
                link(v.tensor_scalar(goh, goh, -1.0, -NEG, ALU.add, ALU.mult))
                for t in range(NT):
                    link(v.tensor_tensor(lem[:, t].rearrange("p (g e) -> p g e", g=GROUPS),
                                         le[:, t].rearrange("p (g e) -> p g e", g=GROUPS),
                                         bc(goh[:, t].unsqueeze(2), GROUPS, NE // GROUPS), ALU.add))
                first_max(lem, m1, oh1, ee, NE)
                link(v.scalar_tensor_tensor(lem2, oh1, 2 * NEG, lem, ALU.mult, ALU.add))
                first_max(lem2, m2, oh2, ee, NE)
                s_ra.by(v.tensor_tensor(ex_e, m2, m1, ALU.subtract))
                s_sel1.by(v.tensor_tensor(chosen, oh1, oh2, ALU.add))
                dve.wait_ge(s_sel1.sem, s_sel1.at(l, 1))
                dve.wait_ge(s_re.sem, s_re.at(l, 1))
                link(v.tensor_reduce(gg, ex_g, AX.X, ALU.add))
                link(v.reciprocal(gg, gg))
                link(v.tensor_scalar(den, ex_e, 1.0, None, ALU.add))
                link(v.reciprocal(den, den))
                link(v.tensor_tensor(w1, den, gg, ALU.mult))
                link(v.tensor_tensor(w2, w1, ex_e, ALU.mult))
                link(v.tensor_tensor(oh1, oh1, bc(w1, NT, NE), ALU.mult))
                link(v.tensor_tensor(oh2, oh2, bc(w2, NT, NE), ALU.mult))
                link(v.tensor_tensor(comb, oh1, oh2, ALU.add))
                link(v.memset(pos_r, -1.0))
                link(v.memset(comb_r, 0.0))
                dve.wait_ge(s_pos.sem, s_pos.at(l, 1))
                link(v.scalar_tensor_tensor(slots_, banks[:, 5, 0:2 * NE].rearrange("p (t e) -> p t e", t=NT), 1.0, chosen,
                                            ALU.add, ALU.mult))
                for r in range(ROUNDS):
                    link(v.tensor_scalar(pos_r[:, :, r * NE:(r + 1) * NE], slots_, -1.0 - r * SLOTS, None, ALU.add))
                    link(v.tensor_copy(comb_r[:, :, r * NE:(r + 1) * NE], comb))
                fullest, over = rt[:, 420:421], rt[:, 424:424 + ROUNDS - 1]
                link(v.tensor_reduce(fullest, banks[:, 5, 32:48], AX.X, ALU.max))
                link(v.tensor_scalar(over, const("edges"), fullest, None, ALU.is_lt))
                link(v.tensor_reduce(fullest, over, AX.X, ALU.add))
                s_np.by(v.tensor_scalar(npairs_i[:, l:l + 1], fullest, float(PAIRS), float(PAIRS), ALU.mult, ALU.add))

                dve.wait_ge(s_np.sem, s_np.at(l, 1))
                n_pairs = dve.value_load(npairs_i[0:1, l:l + 1], min_val=PAIRS, max_val=PAIRS * ROUNDS)

                def select(c):
                    for t in range(NT):
                        for e in range(2):
                            pos = pos_r[:, t, bass.ds(c + e, 1)]
                            wgt = comb_r[:, t, bass.ds(c + e, 1)]
                            o = slice(e * SLOTS, (e + 1) * SLOTS)
                            v.tensor_scalar(sel[:, t, o], const("slot"), pos, None, ALU.is_equal)
                            last = v.tensor_scalar(selw[:, t, o], const("slot"), pos, wgt, ALU.is_equal, ALU.mult)
                    m_sel.by(last)

                def copy_gathered(half, value):
                    dve.wait_ge(m_g.sem, value)
                    g = pc(PG_FFN + 4 * half, 4).unsqueeze(2)
                    m_xg.by(v.tensor_tensor(xg[:, 4 * half:4 * half + 4, :], banks[:, half, :].rearrange("p (c s) -> p c s", c=4),
                                            bc(g, 4, P), ALU.mult))

                select(0)
                for half in range(2):
                    copy_gathered(half, m_g.at(base + l, half + 1))
                with dve.Fori(0, n_pairs) as p:
                    it = base + p
                    dve.wait_ge(m_free.sem, m_free.at(it, 1))
                    select(2 * p + 2)
                    dve.wait_ge(m_silu.sem, m_silu.at(it, 1))
                    dve.wait_ge(m_free.sem, m_free.at(it, 4))
                    m_h.by(v.tensor_tensor(hid, silu_g, banks[:, 4, :].rearrange("s (p c) -> s c p", c=FC), ALU.mult))
                    for half in range(2):
                        copy_gathered(half, m_g.at(it + l, 2 + half + 1))
                    for i in range(4):
                        t, nh = i // 2, i % 2
                        dve.wait_ge(m_z.sem, m_z.at(it, i + 1))
                        dve.wait_ge(m_xadd.sem, m_xadd.at(it, i - 3))
                        xs = x_tok[:, t, nh * 512:(nh + 1) * 512]
                        m_xadd.by(v.tensor_tensor(xs, xs, banks[:, (7, 2)[i % 2], :], ALU.add))
                base = base + n_pairs


def kernel(**inputs):
    import numpy as _np
    import concourse.bacc as _bacc
    from concourse import mybir as _mybir
    from concourse.bass_utils import run_bass_kernel_spmd as _run

    consts = host_constants()
    nc = _bacc.Bacc("TRN2", target_bir_lowering=False, num_devices=1)
    arrays, args = {}, {}
    packed = ("attn_norm_g", "ffn_norm_g", "gla_norm_g", "moba_qnorm_g", "moba_knorm_g", "hgrn_norm_g", "hgrn_lb_param",
              "gla_gk_b", "gla_gk_w2", "w_router_group", "w_router_expert")
    params = packed_params({name: _np.asarray(inputs[name]) for name in packed})
    given = {name: value for name, value in inputs.items() if name not in packed}
    for name, value in {**given, "consts": consts, "params": params}.items():
        a = _np.ascontiguousarray(value)
        arrays[f"in_{name}_dram"] = a
        args[name] = nc.dram_tensor(f"in_{name}_dram", a.shape, _mybir.dt.from_np(a.dtype), kind="ExternalInput").ap()
    shape = inputs["x"].shape
    out = nc.dram_tensor("out_dram", shape, _mybir.dt.float32, kind="ExternalOutput").ap()
    build(nc, args, out)
    return _run(nc, [arrays], core_ids=[0]).results[0]["out_dram"]
```

```python
from contextlib import ExitStack

import numpy as np

import concourse.bass as bass
from concourse import mybir

F32 = mybir.dt.float32
U32 = mybir.dt.uint32
I32 = mybir.dt.int32
ALU = mybir.AluOpType
ACT = mybir.ActivationFunctionType
AX = mybir.AxisListType

P = 128
D_MODEL = 1024
SEQ = 256
DEPTH = 2
NT = SEQ // P
KC = D_MODEL // P
LIN_HEADS = 8
GLA_HEADS = 4
GLA_DK = 32
LOWRANK = 16
HEAD = 64
LIN_CHUNK = 16
MOBA_HEADS = 8
EXPERTS = 16
GROUPS = 4
FF = 512
FC = FF // P
EPS = 1e-6
GLA_TAU = 16.0
SLOTS = 64
ROUNDS = SEQ // SLOTS
PAIRS = EXPERTS // 2
LEVELS = 8
DIAG = 32
DIAG_LEVELS = 6
NEG = -1.0e30
F_MIN = 2.0 ** -60
LN_F_MIN = float(np.log(F_MIN))

A_Q, A_K, A_V, A_G, A_LR, B_Q, B_K, B_V, C_Q, C_F, C_I, C_G = (
    0, 128, 256, 512, 768, 784, 1296, 1808, 2320, 2576, 2832, 3088)
IN_CHUNKS = [(C_Q, 512), (A_G, 272), (A_Q, 256), (B_Q, 512), (B_K, 512), (A_V, 256), (C_I, 512), (B_V, 512)]
LAST_UNIT = [1, 3, 4, 7, 9, 10, 14, 15]
OUT_COLS = 256
OUT_CHUNKS = D_MODEL // OUT_COLS
RING = 6
EXPERT_CHUNKS = [("w_exp_gate", 0), ("w_exp_gate", 1), ("w_exp_up", 0), ("w_exp_up", 1), ("w_exp_down", 0), ("w_exp_down", 1)]
EXTRA = 4
RING_ELEMS = 4096
ATT_CHUNKS = len(IN_CHUNKS) + OUT_CHUNKS
CHUNK_ELEMS = [KC * n for _, n in IN_CHUNKS] + [KC * OUT_COLS] * OUT_CHUNKS
assert ATT_CHUNKS % RING == 0

PG_ATT, PG_FFN, PG_ROUTER, P_GLA, P_QN, P_KN, P_HGRN, P_LB, P_GKB, P_W2 = 0, 8, 16, 24, 25, 26, 27, 28, 30, 31
NR = GROUPS + EXPERTS
P_WR = P_W2 + P
NPAR = P_WR + KC * NR
AHEAD_TURNS = 2
RT_END = 4784
R_EXP = 400

CONSTS = {}
EARLY = P + 2


def host_constants():
    i = np.arange(P)
    cols = []

    def add(name, a):
        a = np.asarray(a, np.float32).reshape(P, -1)
        CONSTS[name] = (sum(c.shape[1] for c in cols), a.shape[1])
        cols.append(a)

    add("ident", np.eye(P))
    add("eps", np.full((P, 1), EPS))
    add("one", np.ones((P, 1)))
    add("head_ones", (i[:, None] // HEAD) == (i[None, :] // HEAD))
    add("all_ones", np.ones((P, P)))
    add("before", i[:, None] < i[None, :])
    d = i % HEAD
    swap = np.zeros((P, P))
    for m in range(P):
        if d[m] < 8:
            swap[m + 8, m] = -1.0
        elif d[m] < 16:
            swap[m - 8, m] = 1.0
    add("swap", swap)
    inv = np.float32(500000.0) ** (-(np.arange(0, 16, 2, dtype=np.float32) / np.float32(16)))
    ang = np.arange(SEQ, dtype=np.float32)[:, None] * inv[None, :].astype(np.float32)
    cos, sin = np.ones((P, SEQ)), np.zeros((P, SEQ))
    for m in range(P):
        if d[m] < 16:
            cos[m] = np.cos(ang[:, d[m] % 8])
            sin[m] = np.sin(ang[:, d[m] % 8])
    add("cos", cos)
    add("sin", sin)
    add("causal", np.where(i[None, :] <= i[:, None], 0.0, NEG))
    j, q = i[:, None] % DIAG, np.arange(DIAG)[None, :]
    masks = [j == q]
    for n in range(1, DIAG_LEVELS):
        s = 1 << (n - 1)
        masks.append((j // (2 * s) == q // (2 * s)) & (j // s % 2 == 0) & (q // s % 2 == 1))
    add("masks", np.stack([np.tile(m, (1, NT)) for m in masks], axis=1))
    add("chunk_keep", np.tile((np.arange(SEQ) % LIN_CHUNK != 0)[None, :], (P, 1)))
    add("ones_row", np.ones((P, SEQ)))
    add("edges", np.tile(np.arange(1, ROUNDS) * SLOTS, (P, 1)))
    add("slot", np.tile(np.arange(SLOTS), (P, 1)))
    add("rank", np.tile(EXPERTS - np.arange(EXPERTS), (P, 1)))
    return np.concatenate(cols, axis=1)


def packed_params(a):
    out = np.zeros((P, DEPTH, NPAR), np.float32)

    def put(l, c, value):
        out[:value.shape[0], l, c:c + value.shape[1]] = value

    for l in range(DEPTH):
        put(l, PG_ATT, a["attn_norm_g"][l].reshape(P, KC))
        put(l, PG_FFN, a["ffn_norm_g"][l].reshape(P, KC))
        put(l, PG_ROUTER, a["ffn_norm_g"][l].reshape(KC, P).T)
        for c, name in ((P_GLA, "gla_norm_g"), (P_QN, "moba_qnorm_g"), (P_KN, "moba_knorm_g"), (P_HGRN, "hgrn_norm_g")):
            put(l, c, np.tile(a[name][l], P // HEAD)[:, None])
        put(l, P_LB, a["hgrn_lb_param"][l].reshape(2, P).T)
        put(l, P_GKB, a["gla_gk_b"][l][:, None])
        put(l, P_W2, a["gla_gk_w2"][l])
        router = np.concatenate([a["w_router_group"][l], a["w_router_expert"][l]], axis=1)
        put(l, P_WR, router.reshape(KC, P, NR).transpose(1, 0, 2).reshape(P, KC * NR))
    return out.reshape(P, DEPTH * NPAR)


def chunked_weights(w_in, w_out):
    w_in = w_in.reshape(DEPTH, P, KC, -1)
    w_out = w_out.reshape(DEPTH, KC, P, D_MODEL).transpose(0, 2, 1, 3)
    cuts = [w_in[..., c:c + n] for c, n in IN_CHUNKS]
    cuts += [w_out[..., j * OUT_COLS:(j + 1) * OUT_COLS] for j in range(OUT_CHUNKS)]
    return np.concatenate([c.reshape(DEPTH, P, -1) for c in cuts], axis=2)


class Signal:

    def __init__(self, sem, per, ahead=0):
        self.sem, self.per, self.ahead = sem, per, ahead

    def by(self, ins, k=1):
        ins.then_inc(self.sem, k)
        return ins

    def at(self, base, n):
        return base * self.per + (n + self.ahead)


def build(nc, a, out):
    with ExitStack() as ctx:
        def sb(name, cols, dt=F32):
            return ctx.enter_context(nc.sbuf_tensor(name, [P, cols], dt))

        def view(t, off, *dims):
            n = int(np.prod(dims))
            v = t[:, off:off + n]
            if len(dims) == 2:
                v = v.rearrange("p (a b) -> p a b", a=dims[0])
            elif len(dims) == 3:
                v = v.rearrange("p (a b c) -> p a b c", a=dims[0], b=dims[1])
            return v

        ncst = sum(n for _, n in CONSTS.values())
        cst = sb("cst", ncst)
        par_all = sb("par_all", DEPTH * NPAR)
        ring = sb("ring", RING * RING_ELEMS)
        x_buf = sb("x_buf", NT * D_MODEL)
        n_buf = sb("n_buf", NT * D_MODEL)
        att_buf = sb("att_buf", (EXTRA - 1) * RING_ELEMS)
        lin_buf, gate_buf = view(att_buf, 0, 12 * SEQ), view(att_buf, 12 * SEQ, 4 * SEQ)
        st_buf, dist_buf = view(att_buf, 16 * SEQ, LIN_HEADS * 3 * P), view(att_buf, 28 * SEQ, 4 * SEQ)
        v_buf, mqk_buf = view(att_buf, 32 * SEQ, NT * D_MODEL), view(att_buf, 40 * SEQ, 8 * SEQ)
        work = sb("work", RT_END + RING_ELEMS)
        t_buf = view(work, RT_END + RING_ELEMS - KC * SEQ, KC * SEQ)
        diag_buf = view(work, 7 * 3 * SEQ, LIN_HEADS * NT * DIAG)
        assert 7 * 3 * SEQ + LIN_HEADS * NT * DIAG <= RT_END + RING_ELEMS - KC * SEQ
        small = sb("small", 384)
        inner_i = sb("inner_i", DEPTH, I32)
        banks = ctx.enter_context(nc.psum_tensor("banks", [P, 8, 512], F32))

        def const(name, *dims):
            off, n = CONSTS[name]
            return view(cst, off, *(dims or (n,)))

        ident, head_ones, all_ones, before, swap = (const(n) for n in ("ident", "head_ones", "all_ones", "before", "swap"))
        cos, sin, causal = const("cos"), const("sin"), const("causal")
        masks = const("masks", DIAG_LEVELS, NT * DIAG)
        eps, one = const("eps"), const("one")

        x_tok = view(x_buf, 0, NT, D_MODEL)
        xn = view(n_buf, 0, NT, KC, P)
        mix_t = view(n_buf, 0, KC, SEQ)
        h_t = view(t_buf, 0, KC, SEQ)
        qf, kf, b_chunk, b_full = (view(lin_buf, i * 3 * SEQ, 3, SEQ) for i in range(4))
        gates = view(gate_buf, 0, 4, SEQ)
        v_tok = view(v_buf, 0, NT, D_MODEL)
        mq, mk = view(mqk_buf, 0, 4, SEQ), view(mqk_buf, 4 * SEQ, 4, SEQ)
        w3 = 3 * SEQ
        dist = [view(work, 0, w3), view(dist_buf, 0, w3)]
        fall = [view(work, (1 + 3 * i) * w3, w3) for i in range(2)]
        q_lvl = [view(work, (2 + 3 * i) * w3, 3, SEQ) for i in range(2)]
        k_lvl = [view(work, (3 + 3 * i) * w3, 3, SEQ) for i in range(2)]
        log_d = view(work, 0, 3, SEQ)
        sq_qk = view(n_buf, 0, 2, 2 * SEQ)
        rs_qk = view(n_buf, 4 * SEQ, 2, 2 * SEQ)
        sq_lin = view(work, 0, 2, 2 * SEQ)
        rs_lin = view(work, 4 * w3, 2, 2 * SEQ)
        st = view(st_buf, 0, LIN_HEADS, 3 * P)
        diag = view(diag_buf, 0, LIN_HEADS, NT * DIAG)
        st_pair = st_buf[:, :].rearrange("p (h i c) -> p h i c", h=2, i=4)
        sig_p, sig_n, f_low = (view(st_buf, i * 2 * SEQ, 2, SEQ) for i in range(3))
        gk_z, lr_t, gk_e = (view(st_buf, (6 + i) * SEQ, SEQ) for i in range(3))
        ln_f = view(st_buf, 9 * SEQ, 2, SEQ)
        prob = [view(lin_buf, i * 2 * 3 * P, 2, 3 * P) for i in range(MOBA_HEADS // 2)]
        prob_t = [view(work, (2 + i) * 2 * 3 * P, 2, 3 * P) for i in range(2)]
        xg = view(work, 0, KC, P)
        sel = view(work, 1024, NT, P)
        selw = view(work, 1280, NT, P)
        selw_t = view(work, 1536, SEQ)
        silu_g = view(work, 1792, FC, P)
        hid = view(work, 2304, FC, P)
        hid_t = view(work, 2816, FC, P)
        y_e = view(work, 3328, D_MODEL)
        rt = view(work, RT_END - 432, 432)

        ssq, rstd = small[:, 0:2], small[:, 4:6]
        ssq_part = view(small, 8, NT, OUT_CHUNKS)
        mx4, nb4, sum4, rsum4 = ([small[:, 16 + 16 * k + 4 * i:20 + 16 * k + 4 * i] for i in range(4)] for k in range(4))
        lb_one_all, lb_ind_all = view(small, 80, DEPTH, 2), view(small, 84, DEPTH, 2)
        lbt = small[:, 88:110]
        table_junk = small[:, 110:111]
        NCOL = 2 * PAIRS * ROUNDS + 4
        pos_r = view(small, 112, NT, NCOL)
        comb_r = view(small, 112 + NT * NCOL, NT, NCOL)

        def sem(name):
            return ctx.enter_context(nc.semaphore(name))

        def signal(name, per, ahead=0):
            return Signal(sem(name), per, ahead)

        s_ident, s_cst, s_par = sem("identity_in"), sem("constants_in"), sem("params_in")
        s_x = [sem(f"x_tile{t}_in") for t in range(NT)]
        s_prep = sem("params_prepared")
        s_lb, s_lbe = sem("lower_bounds"), sem("lower_bound_exp")
        s_out = sem("out_stored")
        s_slot = [sem(f"slot{i}_in") for i in range(RING)]
        s_extra = [sem(f"extra{i}_in") for i in range(EXTRA)]
        s_ssq = signal("square_sums", NT)
        s_std = signal("token_std", NT)
        s_xn = signal("tokens_normed", NT)
        s_tr = signal("tokens_transposed", 2 * NT)
        s_ht = signal("h_t_ready", 2 * NT)
        s_pj = signal("projected", 16)
        s_ev = signal("projection_copied", 16)
        s_flow = signal("f_low_read", 1)
        s_fcl = signal("f_clamped", 1)
        s_lnf = signal("log_f", 1)
        s_gke = signal("gla_log_part", 1)
        s_dist = signal("level_distance", LEVELS)
        s_fall = signal("level_decay", LEVELS)
        s_qk = signal("level_qk", LEVELS + 1)
        s_sc = signal("level_scores", LEVELS + 1)
        s_st = signal("level_scores_taken", LEVELS)
        s_dg = signal("diagonal_blocks_placed", 1)
        s_stx = signal("cross_scores_taken", 4)
        s_sq = signal("head_squares", 6)
        s_ss = signal("head_square_sums", 6)
        s_hs = signal("head_rstd", 6)
        s_nrm = signal("moba_normed", 4)
        s_rot = signal("moba_swapped", 4)
        s_mqk = signal("moba_qk_ready", 4)
        s_lo = signal("linear_out", 2)
        s_lmix = signal("linear_mixed", 2)
        s_ms = signal("moba_scores", 8)
        s_mm = signal("moba_max", 4)
        s_me = signal("moba_exp", 4)
        s_mp = signal("moba_probs", 4)
        s_mt = signal("moba_probs_transposed", 4)
        s_mtc = signal("moba_probs_t_copied", 4)
        s_mo = signal("moba_out", 4)
        s_moc = signal("moba_out_copied", 4)
        s_wo = signal("out_projected", OUT_CHUNKS)
        s_xa = signal("x_attended", 2 * OUT_CHUNKS)
        s_pssq = signal("part_square_sums", NT * OUT_CHUNKS)
        s_rssq = signal("router_square_sums", 1)
        s_rstd = signal("router_std", 1)
        s_rinv = signal("router_rstd", 1)
        s_xe = signal("expert_tokens_normed", 1)
        s_xt = signal("x_transposed", OUT_CHUNKS)
        s_xtc = signal("x_t_copied", OUT_CHUNKS)
        s_lg = signal("router_logits", 1)
        s_ra = signal("router_exp_in", 1)
        s_re = signal("router_exp", 1)
        s_sel1 = signal("experts_chosen", 1)
        s_pos = signal("slots_counted", 1)
        s_tot = signal("expert_totals", 1)
        s_np = signal("pair_count", 1)
        s_vec = sem("vector_step")
        s_act = sem("scalar_step")
        m_sel = signal("selection", 1)
        m_selw = signal("weighted_selection", 1)
        m_g = signal("gathered", 2)
        m_xg = signal("gathered_copied", 2)
        m_swt = signal("selection_transposed", 1)
        m_swc = signal("selection_t_copied", 1)
        m_silu = signal("silu", 1)
        m_h = signal("hidden", 1)
        m_ht = signal("hidden_transposed", 1)
        m_htc = signal("hidden_t_copied", 1)
        m_yc = signal("down_copied", 2)
        m_z = signal("scattered", 4, ahead=4)
        m_xadd = signal("x_added", 4, ahead=4)
        m_free = signal("expert_chunks_used", RING, ahead=2 * RING)

        def pcol(l, c, n=1, rows=P):
            return par_all[0:rows, l * NPAR + c:l * NPAR + c + n]

        pair_banks = {"A": slice(0, 2), "B": slice(2, 4), "C": slice(6, 8)}
        score_banks = [pair_banks[k] for k in "ABBB"]
        turn_banks = [pair_banks[k] for k in "ACAA"]
        def slot_in(engine, l, j, loads, half, base):
            engine.wait_ge(s_slot[j], 16 * ((half if j < EXTRA else base) + 2 * l + loads))

        def expert_chunk(k, j, n):
            buf, start = ring, j * RING_ELEMS
            if k == 1 and j < EXTRA:
                buf, start = (att_buf, start) if j < EXTRA - 1 else (work, RT_END)
            return buf[:, start:start + RING_ELEMS].rearrange("p (e c n) -> p e c n", e=2, n=n)

        wo_bank = (6, 7, 2, 3)
        unit_bank = (0, 1, 2, 3, 0, 1, 2, 3, 0, 1, 2, 1, 0, 3, 2, 0)
        ss_bank, rot_bank = (3, 0, 2, 3, 6, 7), (1, 2, 0, 1)
        xt_bank, lg_bank = (4, 0, 4, 0), (1, 5)

        def bc(ap, *shape):
            return ap.to_broadcast([P, *shape])

        block = ctx.enter_context(nc.Block())

        @block.sync
        def _(sp):
            for t in range(NT):
                sp.dma_start(x_tok[:, t], a["x"][0, t * P:(t + 1) * P]).then_inc(s_x[t], 16)

            def chunk_used(l, j):
                if j < len(IN_CHUNKS):
                    sp.wait_ge(s_pj.sem, s_pj.at(l, LAST_UNIT[j] + 1))
                else:
                    sp.wait_ge(s_wo.sem, s_wo.at(l, j - len(IN_CHUNKS) + 1))

            base, half = 0, 0
            for l in range(DEPTH):
                def load_attention(j):
                    if j >= RING:
                        chunk_used(l, j - RING)
                    elif l > 0:
                        sp.wait_ge(m_free.sem, m_free.at(base, j + 1 - (2 * RING if j < EXTRA else RING)))
                    start, n = sum(CHUNK_ELEMS[:j]), CHUNK_ELEMS[j]
                    s = (j % RING) * RING_ELEMS
                    sp.dma_start(ring[:, s:s + n], a["mixer_weights"][l, :, start:start + n]).then_inc(s_slot[j % RING], 16)

                def load_expert(pair, k, j):
                    name, hf = EXPERT_CHUNKS[j]
                    w = a[name][l][bass.ds((pair % PAIRS) * 2, 2)]
                    run = RING_ELEMS // 2
                    src = w.rearrange("e (p c) n -> p e (c n)", p=P)[:, :, hf * run:(hf + 1) * run]
                    dst = expert_chunk(k, j, run)[:, :, 0]
                    done = s_extra[j] if k == 1 and j < EXTRA else s_slot[j]
                    sp.dma_start(dst, src).then_inc(done, 16)

                for j in range(ATT_CHUNKS):
                    load_attention(j)
                for j in range(2):
                    chunk_used(l, ATT_CHUNKS - RING + j)
                    load_expert(0, 0, j)
                sp.wait_ge(s_lo.sem, s_lo.at(l, 2))
                sp.wait_ge(s_lmix.sem, s_lmix.at(l, 2))
                load_expert(1, 1, 1)
                sp.wait_ge(s_mt.sem, s_mt.at(l, 4))
                load_expert(1, 1, 0)
                sp.wait_ge(s_mo.sem, s_mo.at(l, 4))
                load_expert(1, 1, 2)
                for j in range(2, RING):
                    chunk_used(l, ATT_CHUNKS - RING + j)
                    load_expert(0, 0, j)
                sp.wait_ge(s_lg.sem, s_lg.at(l, 1))
                load_expert(1, 1, 3)

                def load_next(pair, k, chunks):
                    for j in chunks:
                        sp.wait_ge(m_free.sem, m_free.at(base + pair, j + 1))
                        if j < EXTRA:
                            load_expert(pair + 2, k, j)
                        else:
                            load_expert(pair + 1, 1 - k, j)

                def load_turn(q):
                    for k in range(2):
                        load_next(2 * q + k, k, range(EXTRA, RING))
                        load_next(2 * q + k, k, range(EXTRA))

                for pair in range(2 * AHEAD_TURNS):
                    load_next(pair, pair % 2, range(RING) if pair < 2 * AHEAD_TURNS - 1 else (0, 1, 4, 5, 2, 3))
                with sp.Fori(AHEAD_TURNS, PAIRS // 2 - 1) as q:
                    load_turn(q)
                sp.wait_ge(s_np.sem, s_np.at(l, 1))
                inner = sp.value_load(inner_i[0:1, l:l + 1], min_val=PAIRS // 2 - 1, max_val=PAIRS // 2 * ROUNDS - 1)
                with sp.If(inner > PAIRS // 2 - 1):
                    with sp.Fori(PAIRS // 2 - 1, inner) as q:
                        load_turn(q)
                half = half + inner + 1
                base = half * 2
                for j in range(EXTRA, RING):
                    sp.wait_ge(m_free.sem, m_free.at(base, j + 1 - 2 * RING))
                    load_expert(PAIRS - 1, 1, j)
            for t in range(NT):
                sp.wait_ge(m_xadd.sem, m_xadd.at(base, 2 * t - 2))
                sp.dma_start(out[0, t * P:(t + 1) * P], x_tok[:, t]).then_inc(s_out, 16)
            sp.wait_ge(s_out, 16 * NT)

        @block.tensor
        def _(pe):
            mm = nc.tensor.matmul

            def chunk_in(l, j):
                slot_in(pe, l, j % RING, j // RING + 1, half, base)

            def ring_slot(j, n):
                s = j % RING
                return ring[:, s * RING_ELEMS:s * RING_ELEMS + KC * n].rearrange("p (c n) -> p c n", c=KC)

            def transpose_tokens(l):
                for t in range(NT):
                    pe.wait_ge(s_xn.sem, s_xn.at(l, t + 1))
                    for half in range(2):
                        b = t * 2 + half
                        for c in range(4):
                            last = nc.tensor.transpose(banks[:, b, c * P:(c + 1) * P], xn[:, t, half * 4 + c, :], ident)
                        s_tr.by(last)

            def project_t(u, j, f0, tiles, width=P):
                w = ring_slot(j, IN_CHUNKS[j][1])
                for i in range(tiles):
                    for c in range(KC):
                        last = mm(banks[0:width, unit_bank[u], i * SEQ:(i + 1) * SEQ], w[:, c, f0 + i * P:f0 + i * P + width],
                                  h_t[:, c, :], start=c == 0, stop=c == KC - 1)
                return last

            def project_tok(u, t_list, j, f0, n):
                w = ring_slot(j, IN_CHUNKS[j][1])
                for i, t in enumerate(t_list):
                    for c in range(KC):
                        last = mm(banks[:, unit_bank[u], i * n:(i + 1) * n], h_t[:, c, t * P:(t + 1) * P],
                                  w[:, c, f0:f0 + n], start=c == 0, stop=c == KC - 1)
                return last

            def head_rows(h):
                if h < GLA_HEADS:
                    return 0, h * GLA_DK, (h + 1) * GLA_DK
                return 1 + (h - GLA_HEADS) // 2, (h % 2) * HEAD, (h % 2 + 1) * HEAD

            def level(l, n):
                q_, k_ = (qf, kf) if n == 0 else (q_lvl[n % 2], k_lvl[n % 2])
                pe.wait_ge(s_qk.sem, s_qk.at(l, n + 1))
                if n == 0:
                    pe.wait_ge(s_ev.sem, s_ev.at(l, 5))
                if n > 0:
                    pe.wait_ge(s_st.sem, s_st.at(l, n))
                half = (1 << n) // 2
                if n < DIAG_LEVELS:
                    width, blocks = DIAG, [(b, b) for b in range(0, P, DIAG)]
                else:
                    width, blocks = half, [(b, b + half) for b in range(0, P, 2 * half)]
                for hh in range(2):
                    for t in range(NT):
                        for kb, qb in blocks:
                            for i in range(4):
                                f, r0, r1 = head_rows(hh * 4 + i)
                                col = (NT * hh + t) * width
                                last = mm(banks[kb:kb + width, 4 + i, col:col + width],
                                          k_[r0:r1, f, t * P + kb:t * P + kb + width],
                                          q_[r0:r1, f, t * P + qb:t * P + qb + width],
                                          start=True, stop=True, tile_position=(r0, kb))
                s_sc.by(last)

            def cross(l):
                n = LEVELS
                pe.wait_ge(s_qk.sem, s_qk.at(l, n + 1))
                pe.wait_ge(s_st.sem, s_st.at(l, n))
                for hh in range(2):
                    for i in range(4):
                        f, r0, r1 = head_rows(hh * 4 + i)
                        last = mm(banks[:, 4 + i, hh * P:(hh + 1) * P], k_lvl[n % 2][r0:r1, f, 0:P],
                                  q_lvl[n % 2][r0:r1, f, P:2 * P], start=True, stop=True, tile_position=(r0, 0))
                s_sc.by(last)

            def weighted_values(bank, i, h, v0, scores):
                r0 = (h % 2) * HEAD
                v = v_tok[:, :, v0 + h * HEAD:v0 + (h + 1) * HEAD]
                mm(banks[r0:r0 + HEAD, bank, i * SEQ:(i + 1) * SEQ], v[:, 0], scores[:, 0:SEQ],
                   start=True, stop=False, tile_position=(0, r0), skip_group_check=True)
                return mm(banks[r0:r0 + HEAD, bank, i * SEQ + P:(i + 1) * SEQ], v[:, 1], scores[:, SEQ:3 * P],
                          start=False, stop=True, tile_position=(0, r0), skip_group_check=True)

            def square_sums(l, g):
                pe.wait_ge(s_sq.sem, s_sq.at(l, g + 1))
                if g == 0:
                    pe.wait_ge(s_ev.sem, s_ev.at(l, 8))
                elif g == 1:
                    pe.wait_ge(s_ev.sem, s_ev.at(l, 9))
                elif g == 2:
                    pe.wait_ge(s_ev.sem, s_ev.at(l, 11))
                elif g == 3:
                    pe.wait_ge(s_hs.sem, s_hs.at(l, 1))
                else:
                    pe.wait_ge(s_stx.sem, s_stx.at(l, 4))
                src = (sq_qk if g < 4 else sq_lin)[:, g % 2]
                s_ss.by(mm(banks[:, ss_bank[g], :], head_ones, src, start=True, stop=True))

            def swap_halves(l, g):
                src = (mq, mk)[g // 2][:, (g % 2) * 2:(g % 2) * 2 + 2, :].rearrange("p a b -> p (a b)")
                pe.wait_ge(s_nrm.sem, s_nrm.at(l, g + 1))
                if g == 0:
                    pe.wait_ge(s_ev.sem, s_ev.at(l, 12))
                elif g == 1:
                    pe.wait_ge(s_hs.sem, s_hs.at(l, 3))
                elif g == 2:
                    pe.wait_ge(s_ev.sem, s_ev.at(l, 13))
                else:
                    pe.wait_ge(s_mqk.sem, s_mqk.at(l, 1))
                s_rot.by(mm(banks[:, rot_bank[g], :], swap, src, start=True, stop=True))

            def moba_scores(l, hp):
                if hp == 0:
                    pe.wait_ge(s_ev.sem, s_ev.at(l, 13))
                    pe.wait_ge(s_mqk.sem, s_mqk.at(l, 4))
                elif hp == 1:
                    pe.wait_ge(s_ev.sem, s_ev.at(l, 15))
                else:
                    pe.wait_ge(s_me.sem, s_me.at(l, hp))
                for i in range(2):
                    r0 = i * HEAD
                    q_, k_ = mq[r0:r0 + HEAD, hp, :], mk[r0:r0 + HEAD, hp, :]
                    bank = score_banks[hp].start + i
                    mm(banks[:, bank, 0:P], q_[:, 0:P], k_[:, 0:P], start=True, stop=True, tile_position=(r0, 0))
                    s_ms.by(mm(banks[:, bank, P:3 * P], q_[:, P:SEQ], k_[:, 0:SEQ], start=True, stop=True,
                               tile_position=(r0, 0)))

            def moba_transpose(l, hp):
                pe.wait_ge(s_mp.sem, s_mp.at(l, hp + 1))
                if hp == 1:
                    pe.wait_ge(s_hs.sem, s_hs.at(l, 6))
                elif hp == 2:
                    pe.wait_ge(s_ev.sem, s_ev.at(l, 16))
                elif hp == 3:
                    pe.wait_ge(s_mtc.sem, s_mtc.at(l, 3))
                for i in range(2):
                    for k in range(3):
                        last = nc.tensor.transpose(banks[:, turn_banks[hp].start + i, k * P:(k + 1) * P],
                                                   prob[hp][:, i, k * P:(k + 1) * P], ident)
                s_mt.by(last)

            def moba_values(l, hp):
                pe.wait_ge(s_mtc.sem, s_mtc.at(l, hp + 1))
                if hp == 0:
                    pe.wait_ge(s_ev.sem, s_ev.at(l, 16))
                if hp < 2:
                    pe.wait_ge(s_lmix.sem, s_lmix.at(l, hp + 1))
                else:
                    pe.wait_ge(s_moc.sem, s_moc.at(l, hp - 1))
                for i in range(2):
                    last = weighted_values(4 + hp % 2, 0, 2 * hp + i, 512, prob_t[hp % 2][:, i, :])
                s_mo.by(last)

            def project_out(j, t, chunks):
                w = ring_slot(len(IN_CHUNKS) + j, OUT_COLS)
                for c in chunks:
                    last = mm(banks[:, wo_bank[j], t * OUT_COLS:(t + 1) * OUT_COLS], mix_t[:, c, t * P:(t + 1) * P],
                              w[:, c, :], start=c == lin_c[0], stop=c == moba_c[-1])
                return last

            def turn_x(l, j):
                pe.wait_ge(s_xa.sem, s_xa.at(l, NT * (j + 1)))
                if j >= 2:
                    pe.wait_ge(s_xtc.sem, s_xtc.at(l, j - 1))
                for i in range(2):
                    for t in range(NT):
                        c0 = (2 * j + i) * P
                        last = nc.tensor.transpose(banks[:, xt_bank[j], (i * NT + t) * P:(i * NT + t + 1) * P],
                                                   x_tok[:, t, c0:c0 + P], ident)
                s_xt.by(last)

            def router_logits(l, j):
                pe.wait_ge(s_xtc.sem, s_xtc.at(l, j + 1))
                wr = pcol(l, P_WR, KC * NR).rearrange("p (c n) -> p c n", n=NR)
                for c in (2 * j, 2 * j + 1):
                    for t in range(NT):
                        last = mm(banks[:, lg_bank[t], 0:NR], h_t[:, c, t * P:(t + 1) * P], wr[:, c, :],
                                  start=c == 0, stop=c == KC - 1)
                return last

            lin_c, moba_c = (0, 1, 6, 7), (2, 3, 4, 5)
            pe.wait_ge(s_ident, 16)
            base, half = 0, 0
            for l in range(DEPTH):
                transpose_tokens(l)
                pe.wait_ge(s_ht.sem, s_ht.at(l, 4))
                units = [
                    (0, lambda u: project_t(u, 0, 0, 2)),
                    (0, lambda u: project_t(u, 0, 256, 2)),
                    (1, lambda u: project_t(u, 1, 256, 1, LOWRANK)),
                    (1, lambda u: project_t(u, 1, 0, 2)),
                    (2, lambda u: project_t(u, 2, 0, 2)),
                    (None, lambda u: mm(banks[:, unit_bank[u], 0:SEQ], pcol(l, P_W2, P, LOWRANK), lr_t[0:LOWRANK, :],
                                        start=True, stop=True)),
                    (3, lambda u: project_t(u, 3, 0, 2)),
                    (3, lambda u: project_t(u, 3, 256, 2)),
                    (4, lambda u: project_t(u, 4, 0, 2)),
                    (4, lambda u: project_t(u, 4, 256, 2)),
                    (5, lambda u: project_tok(u, (0, 1), 5, 0, 256)),
                    (6, lambda u: project_tok(u, (0, 1), 6, 0, 256)),
                    (6, lambda u: project_t(u, 6, 256, 1)),
                    (7, lambda u: project_tok(u, (0,), 7, 0, 512)),
                    (6, lambda u: project_t(u, 6, 256 + P, 1)),
                    (7, lambda u: project_tok(u, (1,), 7, 0, 512)),
                ]

                def project(u):
                    j, work_of = units[u]
                    if j is not None and (u == 0 or max(k for k, _ in units[:u] if k is not None) < j):
                        chunk_in(l, j)
                    if 4 <= u < 11:
                        pe.wait_ge(s_ev.sem, s_ev.at(l, u - 3))
                    if u == 5:
                        pe.wait_ge(s_flow.sem, s_flow.at(l, 1))
                        pe.wait_ge(s_ev.sem, s_ev.at(l, 3))
                        pe.wait_ge(s_par, 16)
                    if u == 11:
                        pe.wait_ge(s_ev.sem, s_ev.at(l, 10))
                    if u == 12:
                        pe.wait_ge(s_hs.sem, s_hs.at(l, 2))
                    if u == 13:
                        pe.wait_ge(s_hs.sem, s_hs.at(l, 4))
                    if u == 14:
                        pe.wait_ge(s_mqk.sem, s_mqk.at(l, 2))
                    if u == 15:
                        pe.wait_ge(s_mtc.sem, s_mtc.at(l, 1))
                    last = work_of(u)
                    s_pj.by(last)

                for u in range(6):
                    project(u)
                level(l, 0)
                project(6)
                project(7)
                level(l, 1)
                project(8)
                level(l, 2)
                project(9)
                level(l, 3)
                project(10)
                if l == 0:
                    pe.wait_ge(s_cst, 16)
                square_sums(l, 0)
                level(l, 4)
                square_sums(l, 1)
                project(11)
                square_sums(l, 2)
                level(l, 5)
                square_sums(l, 3)
                project(12)
                swap_halves(l, 0)
                level(l, 6)
                swap_halves(l, 1)
                project(13)
                swap_halves(l, 2)
                level(l, 7)
                swap_halves(l, 3)
                project(14)
                cross(l)
                for hp in range(2):
                    moba_scores(l, hp)
                pe.wait_ge(s_stx.sem, s_stx.at(l, 4))
                pe.wait_ge(s_st.sem, s_st.at(l, LEVELS))
                pe.wait_ge(s_dg.sem, s_dg.at(l, 1))
                for g in range(2):
                    for i in range(2):
                        for hh in range(2):
                            h = 4 * g + 2 * i + hh
                            last = weighted_values(4 + g, i, h, 0, st[:, h, :])
                    s_lo.by(last)
                moba_transpose(l, 0)
                moba_scores(l, 2)
                square_sums(l, 4)
                square_sums(l, 5)
                project(15)
                moba_transpose(l, 1)
                moba_scores(l, 3)
                moba_values(l, 0)
                moba_transpose(l, 2)
                moba_values(l, 1)
                pe.wait_ge(s_mtc.sem, s_mtc.at(l, 2))
                for j in range(2):
                    chunk_in(l, len(IN_CHUNKS) + j)
                    project_out(j, 0, lin_c)
                moba_transpose(l, 3)
                pe.wait_ge(s_me.sem, s_me.at(l, 4))
                chunk_in(l, len(IN_CHUNKS) + 2)
                project_out(2, 0, lin_c)
                moba_values(l, 2)
                moba_values(l, 3)
                chunk_in(l, len(IN_CHUNKS) + 3)
                project_out(3, 0, lin_c)
                pe.wait_ge(s_moc.sem, s_moc.at(l, 4))
                for j in range(OUT_CHUNKS):
                    project_out(j, 0, moba_c)
                    last = project_out(j, 1, lin_c + moba_c)
                    s_wo.by(last)
                    if j >= 1:
                        turn_x(l, j - 1)
                if l == 0:
                    pe.wait_ge(s_prep, 1)
                for j in range(OUT_CHUNKS - 1):
                    router_logits(l, j)
                turn_x(l, OUT_CHUNKS - 1)
                s_lg.by(router_logits(l, OUT_CHUNKS - 1))
                pe.wait_ge(s_sel1.sem, s_sel1.at(l, 1))
                chosen = rt[:, 0:NT * EXPERTS].rearrange("p (t e) -> p t e", t=NT)
                mm(banks[:, 5, 0:16], before, chosen[:, 0], start=True, stop=True)
                mm(banks[:, 5, 16:32], all_ones, chosen[:, 0], start=True, stop=False)
                s_pos.by(mm(banks[:, 5, 16:32], before, chosen[:, 1], start=False, stop=True))
                mm(banks[:, 6, 0:EXPERTS], all_ones, chosen[:, 0], start=True, stop=False)
                s_tot.by(mm(banks[:, 6, 0:EXPERTS], all_ones, chosen[:, 1], start=False, stop=True))

                def gather(hf, chunks=range(4)):
                    for c in chunks:
                        for t in range(NT):
                            last = mm(banks[:, hf, c * P:(c + 1) * P], xn[:, t, 4 * hf + c, :], sel[:, t, :],
                                      start=t == 0, stop=t == NT - 1)
                    if chunks[-1] == 3:
                        m_g.by(last)

                def turn_selection(value):
                    pe.wait_ge(m_selw.sem, value)
                    for t in range(NT):
                        last = nc.tensor.transpose(banks[:, 4, t * P:(t + 1) * P], selw[:, t, :], ident)
                    m_swt.by(last)

                pe.wait_ge(m_sel.sem, m_sel.at(base, 1))
                pe.wait_ge(s_xe.sem, s_xe.at(l, 1))
                gather(0)
                gather(1)
                turn_selection(m_selw.at(base, 1))
                pe.wait_ge(s_np.sem, s_np.at(l, 1))
                inner = pe.value_load(inner_i[0:1, l:l + 1], min_val=PAIRS // 2 - 1, max_val=PAIRS // 2 * ROUNDS - 1)

                def expert_pair(q, k, last_pair=False):
                    it = base + 2 * q + k

                    def expert_chunk_in(j):
                        if j >= EXTRA:
                            slot_in(pe, l + 1, j, q * 2 + k + 1, half, base)
                        elif k == 0:
                            slot_in(pe, l + 1, j, q + 1, half, base)
                        else:
                            pe.wait_ge(s_extra[j], 16 * (half + q + 1))

                    for kind, bank in ((0, 3), (1, 4)):
                        if kind == 1:
                            pe.wait_ge(m_swc.sem, m_swc.at(it, 1))
                        for j in (2 * kind, 2 * kind + 1):
                            if kind == 0:
                                pe.wait_ge(m_xg.sem, m_xg.at(it, j + 1))
                            expert_chunk_in(j)
                            w = expert_chunk(k, j, FF)
                            for c in range(4):
                                for e in range(2):
                                    r0 = e * SLOTS
                                    row = EXPERT_CHUNKS[j][1] * 4 + c
                                    last = mm(banks[r0:r0 + SLOTS, bank, :], xg[:, row, r0:r0 + SLOTS], w[:, e, c, :],
                                              start=j % 2 == 0 and c == 0, stop=j % 2 == 1 and c == 3,
                                              tile_position=(0, r0), skip_group_check=True)
                            m_free.by(last)
                    if not last_pair:
                        pe.wait_ge(m_sel.sem, m_sel.at(it, 2))
                        gather(0)
                    pe.wait_ge(m_h.sem, m_h.at(it, 1))
                    for c in range(FC):
                        last = nc.tensor.transpose(banks[:, 3, c * P:(c + 1) * P], hid[:, c, :], ident)
                    m_ht.by(last)
                    if not last_pair:
                        turn_selection(m_selw.at(it, 2))
                        gather(1, range(2))
                    pe.wait_ge(m_htc.sem, m_htc.at(it, 1))
                    for j in (4, 5):
                        expert_chunk_in(j)
                        w = expert_chunk(k, j, D_MODEL)
                        for c in range(2):
                            for nh in range(2):
                                for e in range(2):
                                    r0 = e * SLOTS
                                    row = EXPERT_CHUNKS[j][1] * 2 + c
                                    last = mm(banks[r0:r0 + SLOTS, 5 + nh, :], hid_t[:, row, r0:r0 + SLOTS],
                                              w[:, e, c, nh * 512:(nh + 1) * 512], start=row == 0, stop=row == FC - 1,
                                              tile_position=(0, r0), skip_group_check=True)
                        m_free.by(last)
                    if not last_pair:
                        gather(1, range(2, 4))
                    for i in range(4):
                        t, nh = i // 2, i % 2
                        bank = (7, 2)[i % 2]
                        pe.wait_ge(m_yc.sem, m_yc.at(it, nh + 1))
                        pe.wait_ge(m_xadd.sem, m_xadd.at(it, i - 1))
                        m_z.by(mm(banks[:, bank, :], selw_t[:, t * P:(t + 1) * P], y_e[:, nh * 512:(nh + 1) * 512],
                                  start=True, stop=True))
                with pe.Fori(0, inner) as q:
                    for k in range(2):
                        expert_pair(q, k)
                expert_pair(inner, 0)
                expert_pair(inner, 1, last_pair=True)
                half = half + inner + 1
                base = half * 2

        @block.scalar
        def _(act):
            fn = nc.scalar.activation
            steps = [0]

            def link(ins):
                steps[0] += 1
                ins.then_inc(s_act, 1)
                act.wait_ge(s_act, steps[0])

            def load_table(function):
                fn(table_junk, one, function)

            def token_std(l, base):
                load_table(ACT.Sqrt)
                for t in range(NT):
                    if l == 0:
                        act.wait_ge(s_x[t], 16)
                    act.wait_ge(m_xadd.sem, m_xadd.at(base, 2 * t - 2))
                    s_ssq.by(fn(n_buf[:, t * D_MODEL:(t + 1) * D_MODEL], x_tok[:, t, :], ACT.Square, accum_out=ssq[:, t:t + 1]))
                    act.wait_ge(s_ssq.sem, s_ssq.at(l, t + 1))
                    s_std.by(fn(rstd[:, t:t + 1], ssq[:, t:t + 1], ACT.Sqrt, bias=eps, scale=1.0 / D_MODEL))

            def bank2(b):
                return banks[:, b, :].rearrange("p (a b) -> p a b", a=2)

            act.dma_start(cst[:, 0:EARLY], a["consts"][:, 0:EARLY]).then_inc(s_ident, 16)
            act.dma_start(par_all[:, :], a["params"]).then_inc(s_par, 16)
            act.dma_start(cst[:, EARLY:], a["consts"][:, EARLY:]).then_inc(s_cst, 16)
            act.wait_ge(s_ident, 16)
            act.wait_ge(m_free.sem, m_free.ahead)
            act.wait_ge(m_xadd.sem, m_xadd.ahead)
            act.wait_ge(m_z.sem, m_z.ahead)
            base = 0
            for l in range(DEPTH):
                token_std(l, base)
                if l == 0:
                    act.wait_ge(s_par, 16)
                for t in range(NT):
                    act.wait_ge(s_tr.sem, s_tr.at(l, 2 * t + 2))
                    for c in range(4, KC):
                        last = fn(h_t[:, c, t * P:(t + 1) * P], banks[:, 2 * t + 1, (c - 4) * P:(c - 3) * P], ACT.Copy,
                                  scale=pcol(l, PG_ATT + c))
                    s_ht.by(last)
                if l == 0:
                    act.wait_ge(s_lb, 1)
                    fn(lbt[:, 0:2 * DEPTH], lbt[:, 0:2 * DEPTH], ACT.Exp).then_inc(s_lbe, 1)

                def copy_unit(u):
                    b = unit_bank[u]
                    act.wait_ge(s_pj.sem, s_pj.at(l, u + 1))
                    if u == 0:
                        last = fn(qf[:, 1:3, :], bank2(b), ACT.Silu)
                    elif u == 1:
                        fn(sig_p, bank2(b), ACT.Sigmoid)
                        last = fn(sig_n, bank2(b), ACT.Sigmoid, scale=-1.0)
                    elif u == 2:
                        last = fn(lr_t[0:LOWRANK, :], banks[0:LOWRANK, b, 0:SEQ], ACT.Copy)
                    elif u == 3:
                        last = fn(gates[:, 0:2, :], bank2(b), ACT.Silu)
                    elif u == 4:
                        fn(qf[:, 0, :], banks[:, b, 0:SEQ], ACT.Copy, scale=float(GLA_DK) ** -0.5)
                        last = fn(kf[:, 0, :], banks[:, b, SEQ:2 * SEQ], ACT.Copy)
                    elif u == 5:
                        last = fn(gk_z, banks[:, b, 0:SEQ], ACT.Identity, bias=pcol(l, P_GKB))
                    elif u < 10:
                        dst, i = ((mq, 0), (mq, 2), (mk, 0), (mk, 2))[u - 6]
                        last = fn(dst[:, i:i + 2, :], bank2(b), ACT.Copy)
                    elif u == 10:
                        last = fn(v_tok[:, :, 0:256], bank2(b), ACT.Copy)
                    elif u == 11:
                        last = fn(v_tok[:, :, 256:512], bank2(b), ACT.Copy)
                    elif u == 12:
                        last = fn(gates[:, 2, :], banks[:, b, 0:SEQ], ACT.Silu)
                    elif u == 14:
                        last = fn(gates[:, 3, :], banks[:, b, 0:SEQ], ACT.Silu)
                    else:
                        last = fn(v_tok[:, (u - 13) // 2, 512:1024], banks[:, b, :], ACT.Copy)
                    s_ev.by(last)

                def level_decay(n):
                    act.wait_ge(s_dist.sem, s_dist.at(l, n))
                    link(fn(dist[n % 2], dist[n % 2], ACT.Abs))
                    s_fall.by(fn(fall[n % 2], dist[n % 2], ACT.Exp, scale=-1.0))

                def square_qk(g):
                    if g >= 2:
                        act.wait_ge(s_ss.sem, s_ss.at(l, g - 1))
                    act.wait_ge(s_ev.sem, s_ev.at(l, 7 + g))
                    src = (mq, mk)[g // 2][:, (g % 2) * 2:(g % 2) * 2 + 2, :].rearrange("p a b -> p (a b)")
                    s_sq.by(fn(sq_qk[:, g % 2], src, ACT.Square))

                def head_rstd(*groups):
                    for g in groups:
                        act.wait_ge(s_ss.sem, s_ss.at(l, g + 1))
                        if g in (2, 3):
                            act.wait_ge(s_nrm.sem, s_nrm.at(l, g - 1))
                        last = fn(rs_of(g), banks[:, ss_bank[g], :], ACT.Ln, bias=eps, scale=1.0 / HEAD)
                    link(last)
                    for g in groups:
                        s_hs.by(fn(rs_of(g), rs_of(g), ACT.Exp, scale=-0.5))

                def rs_of(g):
                    return (rs_qk if g < 4 else rs_lin)[:, g % 2]

                for u in range(6):
                    copy_unit(u)
                act.wait_ge(s_ev.sem, s_ev.at(l, 6))
                link(fn(gk_e, gk_z, ACT.Abs))
                link(fn(gk_e, gk_e, ACT.Exp, scale=-1.0))
                s_gke.by(fn(gk_e, gk_e, ACT.Ln, bias=one))
                act.wait_ge(s_fcl.sem, s_fcl.at(l, 1))
                s_lnf.by(fn(ln_f, sig_p, ACT.Ln))
                for u in range(6, 10):
                    copy_unit(u)
                    if u < 9:
                        level_decay(u - 5)
                square_qk(0)
                square_qk(1)
                level_decay(4)
                copy_unit(10)
                head_rstd(0)
                level_decay(5)
                square_qk(2)
                head_rstd(1)
                square_qk(3)
                copy_unit(11)
                head_rstd(2)
                level_decay(6)
                head_rstd(3)
                copy_unit(12)
                level_decay(7)
                copy_unit(13)
                level_decay(8)
                act.wait_ge(s_st.sem, s_st.at(l, DIAG_LEVELS))
                for b in range(0, P, DIAG):
                    dst = st[b:b + DIAG, :, :].rearrange("p h (k c) -> p h k c", k=3)[:, :, 0:3:2, b:b + DIAG]
                    last = fn(dst, diag[b:b + DIAG].rearrange("p h (t c) -> p h t c", t=NT), ACT.Copy)
                s_dg.by(last)
                copy_unit(14)
                for i in range(4):
                    act.wait_ge(s_sc.sem, s_sc.at(l, LEVELS + 1))
                    src = banks[:, 4 + i, 0:2 * P].rearrange("p (h i) -> p h i", h=2)
                    s_stx.by(fn(st_pair[:, :, i, P:2 * P], src, ACT.Copy))

                def moba_exp(hp):
                    act.wait_ge(s_mm.sem, s_mm.at(l, hp + 1))
                    for i in range(2):
                        bank = score_banks[hp].start + i
                        for qt in range(2):
                            c = 2 * i + qt
                            cols = slice(0, P) if qt == 0 else slice(P, 3 * P)
                            last = fn(prob[hp][:, i, cols], banks[:, bank, cols], ACT.Exp, bias=nb4[hp][:, c:c + 1],
                                      scale=HEAD ** -0.5, accum_out=sum4[hp][:, c:c + 1])
                    s_me.by(last)

                def copy_turned(hp):
                    act.wait_ge(s_mt.sem, s_mt.at(l, hp + 1))
                    if hp >= 2:
                        act.wait_ge(s_mo.sem, s_mo.at(l, hp - 1))
                    s_mtc.by(fn(prob_t[hp % 2], banks[:, turn_banks[hp], 0:3 * P], ACT.Copy))

                def copy_mixed(hp):
                    act.wait_ge(s_mo.sem, s_mo.at(l, hp + 1))
                    s_moc.by(fn(mix_t[:, 2 + hp, :], banks[:, 4 + hp % 2, 0:SEQ], ACT.Copy))

                moba_exp(0)
                moba_exp(1)
                for g in range(2):
                    act.wait_ge(s_lo.sem, s_lo.at(l, g + 1))
                    s_sq.by(fn(sq_lin[:, g], banks[:, 4 + g, :], ACT.Square))
                copy_turned(0)
                moba_exp(2)
                head_rstd(4, 5)
                copy_unit(15)
                copy_turned(1)
                moba_exp(3)
                for hp in range(2, 4):
                    copy_mixed(hp - 2)
                    copy_turned(hp)
                copy_mixed(2)
                copy_mixed(3)

                load_table(ACT.Sqrt)
                for j in range(OUT_CHUNKS):
                    for t in range(NT):
                        act.wait_ge(s_xa.sem, s_xa.at(l, NT * j + t + 1))
                        junk = work[:, (NT * j + t) * OUT_COLS:(NT * j + t + 1) * OUT_COLS]
                        s_pssq.by(fn(junk, x_tok[:, t, j * OUT_COLS:(j + 1) * OUT_COLS], ACT.Square,
                                     accum_out=ssq_part[:, t, j:j + 1]))
                    act.wait_ge(s_xt.sem, s_xt.at(l, j + 1))
                    s_xtc.by(fn(h_t[:, 2 * j:2 * j + 2, :], banks[:, xt_bank[j], :].rearrange("p (c t) -> p c t", c=2), ACT.Copy))
                act.wait_ge(s_rssq.sem, s_rssq.at(l, 1))
                s_rstd.by(fn(rstd, ssq, ACT.Sqrt, bias=eps, scale=1.0 / D_MODEL))
                act.wait_ge(s_rinv.sem, s_rinv.at(l, 1))
                for t in range(NT):
                    last = fn(xn[:, t], x_tok[:, t].rearrange("p (q c) -> p c q", c=KC), ACT.Copy, scale=rstd[:, t:t + 1])
                s_xe.by(last)
                load_table(ACT.Exp)
                act.wait_ge(s_ra.sem, s_ra.at(l, 1))
                s_re.by(fn(rt[:, R_EXP:R_EXP + 10], rt[:, R_EXP:R_EXP + 10], ACT.Exp))

                act.wait_ge(s_np.sem, s_np.at(l, 1))
                inner = act.value_load(inner_i[0:1, l:l + 1], min_val=PAIRS // 2 - 1, max_val=PAIRS // 2 * ROUNDS - 1)

                def expert_pair(it):
                    act.wait_ge(m_swt.sem, m_swt.at(it, 1))
                    act.wait_ge(m_z.sem, m_z.at(it, 0))
                    m_swc.by(fn(selw_t, banks[:, 4, 0:SEQ], ACT.Copy))
                    act.wait_ge(m_free.sem, m_free.at(it, 2))
                    m_silu.by(fn(silu_g, banks[:, 3, :].rearrange("s (p c) -> s c p", c=FC), ACT.Silu))
                    act.wait_ge(m_ht.sem, m_ht.at(it, 1))
                    m_htc.by(fn(hid_t, banks[:, 3, :].rearrange("p (c s) -> p c s", c=FC), ACT.Copy))
                    act.wait_ge(m_free.sem, m_free.at(it, RING))
                    for nh in range(2):
                        m_yc.by(fn(y_e[:, nh * 512:(nh + 1) * 512], banks[:, 5 + nh, :], ACT.Copy))

                with act.Fori(0, inner) as q:
                    for k in range(2):
                        expert_pair(base + 2 * q + k)
                for k in range(2):
                    expert_pair(base + 2 * inner + k)
                base = base + 2 * inner + 2

        @block.vector
        def _(dve):
            v = nc.vector
            steps = [0]

            def link(ins):
                steps[0] += 1
                ins.then_inc(s_vec, 1)
                dve.wait_ge(s_vec, steps[0])

            def pc(c, n=1):
                return pcol(l, c, n)

            v.memset(small[:, 0:128], 0.0).then_inc(m_xadd.sem, m_xadd.ahead)
            v.memset(small[:, 128:256], 0.0).then_inc(m_free.sem, m_free.ahead)
            v.memset(small[:, 256:384], 0.0).then_inc(m_z.sem, m_z.ahead)
            dve.wait_ge(m_xadd.sem, m_xadd.ahead)
            dve.wait_ge(m_free.sem, m_free.ahead)
            dve.wait_ge(m_z.sem, m_z.ahead)
            def prepare_params():
                lb_cols = [pcol(k, P_LB, 2) for k in range(DEPTH)]
                top, tot, part = lbt[:, 16:18], lbt[:, 18:20], lbt[:, 20:22]
                link(v.tensor_copy(top, lb_cols[0]))
                for k in range(1, DEPTH):
                    link(v.tensor_tensor(top, top, lb_cols[k], ALU.max))
                for k in range(DEPTH):
                    last = v.tensor_tensor(lbt[:, 2 * k:2 * k + 2], lb_cols[k], top, ALU.subtract)
                last.then_inc(s_lb, 1)
                dve.wait_ge(s_lbe, 1)
                link(v.tensor_copy(tot, lbt[:, 0:2]))
                for k in range(1, DEPTH):
                    link(v.tensor_tensor(tot, tot, lbt[:, 2 * k:2 * k + 2], ALU.add))
                link(v.reciprocal(tot, tot))
                for k in range(DEPTH):
                    link(v.tensor_tensor(lbt[:, 2 * k:2 * k + 2], lbt[:, 2 * k:2 * k + 2], tot, ALU.mult))
                link(v.tensor_copy(part, lbt[:, 0:2]))
                for k in range(DEPTH):
                    if k > 0:
                        link(v.tensor_tensor(part, part, lbt[:, 2 * k:2 * k + 2], ALU.add))
                    link(v.tensor_tensor(lb_cols[k], part, lbt[:, 0:2], ALU.subtract))
                    v.tensor_scalar(lb_one_all[:, k], lb_cols[k], -1.0, 1.0, ALU.mult, ALU.add)
                    v.tensor_scalar(lb_ind_all[:, k], lb_cols[k], F_MIN, None, ALU.is_lt)
                    wr = pcol(k, P_WR, KC * NR).rearrange("p (c n) -> p c n", n=NR)
                    last = v.tensor_tensor(wr, wr, bc(pcol(k, PG_ROUTER, KC).unsqueeze(2), KC, NR), ALU.mult)
                last.then_inc(s_prep, 1)
                dve.wait_ge(s_prep, 1)

            base = 0
            for l in range(DEPTH):
                lb, lb_one, lb_ind = pc(P_LB, 2), lb_one_all[:, l], lb_ind_all[:, l]

                for t in range(NT):
                    r = rstd[:, t:t + 1]
                    dve.wait_ge(s_std.sem, s_std.at(l, t + 1))
                    link(v.reciprocal(r, r))
                    s_xn.by(v.tensor_scalar(xn[:, t], x_tok[:, t].rearrange("p (q c) -> p c q", c=KC), r, None, ALU.mult))
                if l == 0:
                    dve.wait_ge(s_par, 16)
                for t in range(NT):
                    dve.wait_ge(s_tr.sem, s_tr.at(l, 2 * t + 1))
                    s_ht.by(v.tensor_tensor(h_t[:, 0:4, t * P:(t + 1) * P],
                                            banks[:, 2 * t, :].rearrange("p (c t) -> p c t", c=4),
                                            bc(pc(PG_ATT, 4).unsqueeze(2), 4, P), ALU.mult))
                if l == 0:
                    prepare_params()
                    dve.wait_ge(s_cst, 16)
                dve.wait_ge(s_ev.sem, s_ev.at(l, 2))
                bank1 = banks[:, 1, :].rearrange("p (a b) -> p a b", a=2)
                s_flow.by(v.tensor_scalar(f_low, bank1, -LN_F_MIN, 0.0, ALU.add, ALU.min))
                for f in range(2):
                    link(v.tensor_scalar(sig_p[:, f, :], sig_p[:, f, :], lb_one[:, f:f + 1], lb[:, f:f + 1], ALU.mult, ALU.add))
                s_fcl.by(v.tensor_scalar(sig_p, sig_p, F_MIN, None, ALU.max))
                for f in range(2):
                    last = v.tensor_scalar(kf[:, 1 + f, :], sig_n[:, f, :], lb_one[:, f:f + 1], None, ALU.mult)
                s_qk.by(last)
                dve.wait_ge(s_gke.sem, s_gke.at(l, 1))
                link(v.scalar_tensor_tensor(log_d[:, 0, :], gk_z, 0.0, gk_e, ALU.min, ALU.subtract))
                link(v.tensor_scalar(log_d[:, 0, :], log_d[:, 0, :], 1.0 / GLA_TAU, None, ALU.mult))
                dve.wait_ge(s_lnf.sem, s_lnf.at(l, 1))
                dve.wait_ge(s_flow.sem, s_flow.at(l, 1))
                for f in range(2):
                    link(v.scalar_tensor_tensor(log_d[:, 1 + f, :], f_low[:, f, :], lb_ind[:, f:f + 1], ln_f[:, f, :],
                                                ALU.mult, ALU.add))
                for f in range(3):
                    link(v.tensor_tensor_scan(b_chunk[:, f, :], const("chunk_keep"), log_d[:, f, :], 0.0, ALU.mult, ALU.add))
                    link(v.tensor_tensor_scan(b_full[:, f, :], const("ones_row"), log_d[:, f, :], 0.0, ALU.mult, ALU.add))

                def level_distance(n):
                    s = 1 << (n - 1)
                    b = (b_chunk if 2 * s <= LIN_CHUNK else b_full).rearrange("p f (k w) -> p (f k) w", w=2 * s)
                    o = dist[n % 2].rearrange("p (k w) -> p k w", w=2 * s)
                    s_dist.by(v.tensor_tensor(o, b, bc(b[:, :, s - 1:s], 3 * SEQ // (2 * s), 2 * s), ALU.subtract))

                def level_scale(n):
                    dve.wait_ge(s_fall.sem, s_fall.at(l, n))
                    f = fall[n % 2].rearrange("p (f t) -> p f t", f=3)
                    v.tensor_tensor(q_lvl[n % 2], qf, f, ALU.mult)
                    s_qk.by(v.tensor_tensor(k_lvl[n % 2], kf, f, ALU.mult))

                def take_scores(n):
                    dve.wait_ge(s_sc.sem, s_sc.at(l, n + 1))
                    if n < DIAG_LEVELS:
                        src = banks[:, 4:8, 0:2 * NT * DIAG].rearrange("p i (h c) -> p i h c", h=2)
                        dst = diag.rearrange("p (h i) c -> p i h c", h=2)
                        mask = masks[:, n:n + 1, :].unsqueeze(1)
                        if n == 0:
                            s_st.by(v.tensor_tensor(dst, src, bc(mask, 4, 2, NT * DIAG), ALU.mult))
                        else:
                            dve.wait_ge(s_st.sem, s_st.at(l, n))
                            s_st.by(v.copy_predicated(dst, bc(mask.bitcast(U32), 4, 2, NT * DIAG), src))
                    else:
                        half = (1 << n) // 2
                        for b in range(0, P, 2 * half):
                            for hh in range(2):
                                src = banks[b:b + half, 4:8, hh * NT * half:(hh + 1) * NT * half]
                                dst = st_pair[b:b + half, hh].rearrange("p i (k c) -> p i k c", k=3)
                                last = v.tensor_copy(dst[:, :, 0:3:2, b + half:b + 2 * half],
                                                     src.rearrange("p i (t c) -> p i t c", t=NT))
                        s_st.by(last)

                def moba_norm(g):
                    dve.wait_ge(s_hs.sem, s_hs.at(l, g + 1))
                    m = (mq, mk)[g // 2][:, (g % 2) * 2:(g % 2) * 2 + 2, :].rearrange("p a b -> p (a b)")
                    s_nrm.by(v.scalar_tensor_tensor(m, m, pc(P_QN + g // 2), rs_qk[:, g % 2], ALU.mult, ALU.mult))

                def moba_rotate(g):
                    m = (mq, mk)[g // 2][:, (g % 2) * 2:(g % 2) * 2 + 2, :]
                    turned = sq_qk[:, g % 2].rearrange("p (a b) -> p a b", a=2)
                    dve.wait_ge(s_rot.sem, s_rot.at(l, g + 1))
                    v.tensor_tensor(turned, banks[:, rot_bank[g], :].rearrange("p (a b) -> p a b", a=2),
                                    bc(sin.unsqueeze(1), 2, SEQ), ALU.mult)
                    link(v.tensor_tensor(m, m, bc(cos.unsqueeze(1), 2, SEQ), ALU.mult))
                    s_mqk.by(v.tensor_tensor(m, m, turned, ALU.add))
                    dve.wait_ge(s_mqk.sem, s_mqk.at(l, g + 1))

                def level_step(n):
                    level_distance(n)
                    level_scale(n - 1)
                    take_scores(n - 2)

                level_distance(1)
                level_distance(2)
                level_scale(1)
                take_scores(0)
                v.memset(st_buf, 0.0)
                for n in range(3, 6):
                    level_step(n)
                moba_norm(0)
                level_step(6)
                moba_norm(1)
                moba_norm(2)
                level_step(7)
                moba_norm(3)
                moba_rotate(0)
                level_step(8)
                moba_rotate(1)
                moba_rotate(2)
                level_scale(LEVELS)
                take_scores(LEVELS - 1)
                moba_rotate(3)

                def moba_max(hp):
                    dve.wait_ge(s_ms.sem, s_ms.at(l, 2 * hp + 2))
                    first = banks[:, score_banks[hp], 0:P]
                    second = banks[:, score_banks[hp], P:3 * P]
                    mask = bc(causal.unsqueeze(1), 2, P)
                    v.tensor_tensor(first, first, mask, ALU.add)
                    link(v.tensor_tensor(second[:, :, P:SEQ], second[:, :, P:SEQ], mask, ALU.add))
                    m = mx4[hp].rearrange("p (i q) -> p i q", i=2)
                    v.tensor_reduce(m[:, :, 0:1], first, AX.X, ALU.max)
                    link(v.tensor_reduce(m[:, :, 1:2], second, AX.X, ALU.max))
                    s_mm.by(v.tensor_scalar(nb4[hp], mx4[hp], -(HEAD ** -0.5), None, ALU.mult))

                def moba_normalise(hp):
                    dve.wait_ge(s_me.sem, s_me.at(l, hp + 1))
                    link(v.reciprocal(rsum4[hp], sum4[hp]))
                    r = rsum4[hp].rearrange("p (i q) -> p i q", i=2)
                    v.tensor_tensor(prob[hp][:, :, 0:P], prob[hp][:, :, 0:P], bc(r[:, :, 0:1], 2, P), ALU.mult)
                    s_mp.by(v.tensor_tensor(prob[hp][:, :, P:3 * P], prob[hp][:, :, P:3 * P], bc(r[:, :, 1:2], 2, 2 * P), ALU.mult))

                def linear_mix(g):
                    tmp = dist[1][:, 0:2 * SEQ]
                    dve.wait_ge(s_hs.sem, s_hs.at(l, 5 + g))
                    link(v.scalar_tensor_tensor(tmp, banks[:, 4 + g, :], pc((P_GLA, P_HGRN)[g]), rs_lin[:, g], ALU.mult, ALU.mult))
                    dst = mix_t[:, 6 * g:6 * g + 2, :]
                    s_lmix.by(v.tensor_tensor(dst, tmp.rearrange("p (a b) -> p a b", a=2), gates[:, 2 * g:2 * g + 2, :], ALU.mult))
                    dve.wait_ge(s_lmix.sem, s_lmix.at(l, g + 1))

                moba_max(0)
                moba_max(1)
                moba_normalise(0)
                moba_normalise(1)
                moba_max(2)
                moba_normalise(2)
                linear_mix(0)
                linear_mix(1)
                moba_max(3)
                moba_normalise(3)
                for j in range(OUT_CHUNKS):
                    dve.wait_ge(s_wo.sem, s_wo.at(l, j + 1))
                    for t in range(NT):
                        xs = x_tok[:, t, j * OUT_COLS:(j + 1) * OUT_COLS]
                        s_xa.by(v.tensor_tensor(xs, xs, banks[:, wo_bank[j], t * OUT_COLS:(t + 1) * OUT_COLS], ALU.add))

                NE = EXPERTS
                chosen = view(rt, 0, NT, NE)
                logits = view(rt, 32, NT, NR)
                lg, le = logits[:, :, 0:GROUPS], logits[:, :, GROUPS:NR]
                eg, other = view(rt, 80, NT, GROUPS), view(rt, 96, NT, GROUPS)
                ee, oh1, oh2, lem = (view(rt, 128 + 32 * i, NT, NE) for i in range(4))
                lem2, comb, slots_ = (view(rt, 256 + 32 * i, NT, NE) for i in range(3))
                one2 = [view(rt, 384 + 2 * i, NT, 1) for i in range(8)]
                gmax, vm, m1, m2, gg, w1, w2, den = one2
                ex_g = view(rt, R_EXP, NT, GROUPS)
                ex_e = view(rt, R_EXP + NT * GROUPS, NT, 1)
                rank = const("rank").unsqueeze(1)

                def first_max(vals, top, hot, scratch, n, op=ALU.is_equal):
                    link(v.tensor_reduce(top, vals, AX.X, ALU.max))
                    for t in range(NT):
                        last = v.scalar_tensor_tensor(scratch[:, t], vals[:, t], top[:, t], rank[:, 0, 0:n],
                                                      ALU.is_equal, ALU.mult)
                    link(last)
                    link(v.tensor_reduce(vm, scratch, AX.X, ALU.max))
                    link(v.tensor_tensor(hot, scratch, bc(vm, NT, n), op))

                def select(c):
                    for t in range(NT):
                        for e in range(2):
                            pos = pos_r[:, t, bass.ds(c + e, 1)]
                            last = v.tensor_scalar(sel[:, t, e * SLOTS:(e + 1) * SLOTS], const("slot"), pos, None, ALU.is_equal)
                    m_sel.by(last)

                def select_weighted(c):
                    for t in range(NT):
                        for e in range(2):
                            pos = pos_r[:, t, bass.ds(c + e, 1)]
                            wgt = comb_r[:, t, bass.ds(c + e, 1)]
                            last = v.tensor_scalar(selw[:, t, e * SLOTS:(e + 1) * SLOTS], const("slot"), pos, wgt,
                                                   ALU.is_equal, ALU.mult)
                    m_selw.by(last)

                v.memset(pos_r, -1.0)
                v.memset(comb_r, 0.0)
                dve.wait_ge(s_pssq.sem, s_pssq.at(l, NT * OUT_CHUNKS))
                s_rssq.by(v.tensor_reduce(ssq.unsqueeze(2), ssq_part, AX.X, ALU.add))
                dve.wait_ge(s_lg.sem, s_lg.at(l, 1))
                for t in range(NT):
                    last = v.tensor_copy(logits[:, t], banks[:, lg_bank[t], 0:NR])
                link(last)
                first_max(lg, gmax, other, eg, GROUPS, ALU.not_equal)
                for t in range(NT):
                    last = v.scalar_tensor_tensor(lem[:, t].rearrange("p (g e) -> p g e", g=GROUPS),
                                                  bc(other[:, t].unsqueeze(2), GROUPS, NE // GROUPS), NEG,
                                                  le[:, t].rearrange("p (g e) -> p g e", g=GROUPS), ALU.mult, ALU.add)
                link(last)
                first_max(lem, m1, oh1, ee, NE)
                dve.wait_ge(s_rstd.sem, s_rstd.at(l, 1))
                s_rinv.by(v.reciprocal(rstd, rstd))
                dve.wait_ge(s_rinv.sem, s_rinv.at(l, 1))
                rs = rstd.unsqueeze(2)
                link(v.scalar_tensor_tensor(lem2, oh1, 2 * NEG, lem, ALU.mult, ALU.add))
                first_max(lem2, m2, oh2, ee, NE)
                s_sel1.by(v.tensor_tensor(chosen, oh1, oh2, ALU.add))
                v.tensor_tensor(ex_g, lg, bc(gmax, NT, GROUPS), ALU.subtract)
                link(v.tensor_tensor(ex_e, m2, m1, ALU.subtract))
                v.tensor_tensor(ex_g, ex_g, bc(rs, NT, GROUPS), ALU.mult)
                s_ra.by(v.tensor_tensor(ex_e, ex_e, rs, ALU.mult))
                dve.wait_ge(s_sel1.sem, s_sel1.at(l, 1))
                dve.wait_ge(s_pos.sem, s_pos.at(l, 1))
                link(v.scalar_tensor_tensor(slots_, banks[:, 5, 0:2 * NE].rearrange("p (t e) -> p t e", t=NT), 1.0, chosen,
                                            ALU.add, ALU.mult))

                link(v.tensor_scalar(pos_r[:, :, 0:NE], slots_, -1.0, None, ALU.add))
                select(0)
                dve.wait_ge(s_re.sem, s_re.at(l, 1))
                v.tensor_reduce(gg, ex_g, AX.X, ALU.add)
                link(v.tensor_scalar(den, ex_e, 1.0, None, ALU.add))
                v.reciprocal(gg, gg)
                link(v.reciprocal(den, den))
                link(v.tensor_tensor(w1, den, gg, ALU.mult))
                link(v.tensor_tensor(w2, w1, ex_e, ALU.mult))
                v.tensor_tensor(oh1, oh1, bc(w1, NT, NE), ALU.mult)
                link(v.tensor_tensor(oh2, oh2, bc(w2, NT, NE), ALU.mult))
                link(v.tensor_tensor(comb, oh1, oh2, ALU.add))
                link(v.tensor_copy(comb_r[:, :, 0:NE], comb))

                def copy_gathered(half, value):
                    dve.wait_ge(m_g.sem, value)
                    g = pc(PG_FFN + 4 * half, 4).unsqueeze(2)
                    m_xg.by(v.tensor_tensor(xg[:, 4 * half:4 * half + 4, :], banks[:, half, :].rearrange("p (c s) -> p c s", c=4),
                                            bc(g, 4, P), ALU.mult))

                select_weighted(0)
                fullest, over = rt[:, 420:421], rt[:, 424:424 + ROUNDS - 1]
                dve.wait_ge(s_tot.sem, s_tot.at(l, 1))
                link(v.tensor_reduce(fullest, banks[:, 6, 0:EXPERTS], AX.X, ALU.max))
                link(v.tensor_scalar(over, const("edges"), fullest, None, ALU.is_lt))
                link(v.tensor_reduce(fullest, over, AX.X, ALU.add))
                s_np.by(v.tensor_scalar(inner_i[:, l:l + 1], fullest, float(PAIRS // 2), float(PAIRS // 2 - 1),
                                      ALU.mult, ALU.add))
                for r in range(1, ROUNDS):
                    v.tensor_scalar(pos_r[:, :, r * NE:(r + 1) * NE], slots_, -1.0 - r * SLOTS, None, ALU.add)
                    last = v.tensor_copy(comb_r[:, :, r * NE:(r + 1) * NE], comb)
                link(last)
                dve.wait_ge(s_np.sem, s_np.at(l, 1))
                inner = dve.value_load(inner_i[0:1, l:l + 1], min_val=PAIRS // 2 - 1, max_val=PAIRS // 2 * ROUNDS - 1)
                for half in range(2):
                    copy_gathered(half, m_g.at(base, half + 1))

                def expert_pair(q, k, last_pair=False):
                    it = base + 2 * q + k
                    if not last_pair:
                        dve.wait_ge(m_free.sem, m_free.at(it, 1))
                        select(4 * q + 2 * k + 2)
                        select_weighted(4 * q + 2 * k + 2)
                    dve.wait_ge(m_silu.sem, m_silu.at(it, 1))
                    dve.wait_ge(m_free.sem, m_free.at(it, 4))
                    m_h.by(v.tensor_tensor(hid, silu_g, banks[:, 4, :].rearrange("s (p c) -> s c p", c=FC), ALU.mult))
                    if not last_pair:
                        for half in range(2):
                            copy_gathered(half, m_g.at(it, 2 + half + 1))
                    for i in range(4):
                        t, nh = i // 2, i % 2
                        dve.wait_ge(m_z.sem, m_z.at(it, i + 1))
                        dve.wait_ge(m_xadd.sem, m_xadd.at(it, i - 3))
                        xs = x_tok[:, t, nh * 512:(nh + 1) * 512]
                        m_xadd.by(v.tensor_tensor(xs, xs, banks[:, (7, 2)[i % 2], :], ALU.add))
                with dve.Fori(0, inner) as q:
                    for k in range(2):
                        expert_pair(q, k)
                expert_pair(inner, 0)
                expert_pair(inner, 1, last_pair=True)
                base = base + 2 * inner + 2


def kernel(**inputs):
    import numpy as _np
    import concourse.bacc as _bacc
    from concourse import mybir as _mybir
    from concourse.bass_utils import run_bass_kernel_spmd as _run

    consts = host_constants()
    nc = _bacc.Bacc("TRN2", target_bir_lowering=False, num_devices=1)
    arrays, args = {}, {}
    packed = ("attn_norm_g", "ffn_norm_g", "gla_norm_g", "moba_qnorm_g", "moba_knorm_g", "hgrn_norm_g", "hgrn_lb_param",
              "gla_gk_b", "gla_gk_w2", "w_router_group", "w_router_expert")
    params = packed_params({name: _np.asarray(inputs[name]) for name in packed})
    laid_out = {name: inputs[name] for name in ("x", "w_exp_gate", "w_exp_up", "w_exp_down")}
    laid_out |= {"consts": consts, "params": params,
                 "mixer_weights": chunked_weights(_np.asarray(inputs["w_in"]), _np.asarray(inputs["w_out"]))}
    for name, value in laid_out.items():
        a = _np.ascontiguousarray(value)
        arrays[f"in_{name}_dram"] = a
        args[name] = nc.dram_tensor(f"in_{name}_dram", a.shape, _mybir.dt.from_np(a.dtype), kind="ExternalInput").ap()
    shape = inputs["x"].shape
    out = nc.dram_tensor("out_dram", shape, _mybir.dt.float32, kind="ExternalOutput").ap()
    build(nc, args, out)
    return _run(nc, [arrays], core_ids=[0]).results[0]["out_dram"]
```
